# Optimizing a Trainium2 kernel written in Bass

```python
import jax, jax.numpy as jnp
from jax import lax
import numpy as np

D_MODEL = 1024
BATCH = 1
SEQ = 1024
DEPTH = 2

CHUNK = 64
Q_BLOCK = 2 * CHUNK
N_MIXERS = 2
CONV_WIDTH = 3
MIX_WIDTH = D_MODEL
SB_HEADS = 16
SB_HEAD_DIM = MIX_WIDTH // SB_HEADS
N_MEM = 256
MEM_HEADS = 4
MEM_HEAD_DIM = 128
MEM_WIDTH = MEM_HEADS * MEM_HEAD_DIM
IN_WIDTH = 3 * MIX_WIDTH + MEM_WIDTH
OUT_WIDTH = MIX_WIDTH + MEM_WIDTH
D_FF = -(-(8 * D_MODEL) // (3 * 256)) * 256
N_CONV_LAYERS = (DEPTH + N_MIXERS - 1) // N_MIXERS
EPS = 1e-6

kernel_name = "hybrid_shortconv_stickbreaking_memxattn"

def rmsnorm(x, g):
    xf = x.astype(jnp.float32)
    y = xf * lax.rsqrt(jnp.mean(xf * xf, axis=-1, keepdims=True) + EPS)
    return (y * g.astype(jnp.float32)).astype(x.dtype)

def short_conv_mixer(b_gate, c_gate, u, w_conv):
    y = c_gate * u
    y = lax.conv_general_dilated(
        y, w_conv[:, None, :].astype(y.dtype),
        window_strides=(1,),
        padding=[(CONV_WIDTH - 1, 0)],
        dimension_numbers=("NWC", "WIO", "NWC"),
        feature_group_count=y.shape[-1])
    return b_gate * y

def stick_breaking_attention(q, k, v):
    b, h, s, dh = q.shape
    n_blk = s // Q_BLOCK
    scale = dh ** -0.5
    kf = k.astype(jnp.float32)
    vf = v.astype(jnp.float32)
    q_blocks = q.astype(jnp.float32).reshape(b, h, n_blk, Q_BLOCK, dh).transpose(2, 0, 1, 3, 4)
    key_pos = jnp.arange(s)

    def block(args):
        qb, t0 = args
        t = t0 + jnp.arange(Q_BLOCK)
        mask = key_pos[None, :] < t[:, None]
        z = jnp.einsum("bhqd,bhkd->bhqk", qb, kf) * scale
        log_keep = jnp.where(mask, jax.nn.log_sigmoid(-z), 0.0)
        later = lax.cumsum(log_keep, axis=3, reverse=True) - log_keep
        log_a = jax.nn.log_sigmoid(z) + later
        a = jnp.where(mask, jnp.exp(log_a), 0.0)
        return jnp.einsum("bhqk,bhkd->bhqd", a, vf)

    out = lax.map(block, (q_blocks, jnp.arange(n_blk) * Q_BLOCK))
    return out.transpose(1, 2, 0, 3, 4).reshape(b, h, s, dh).astype(q.dtype)

def memory_cross_attention(q, mem_kv, g_q, g_k):
    b, s, _ = q.shape
    m = mem_kv.shape[1]
    k, v = jnp.split(mem_kv, 2, axis=-1)
    qh = rmsnorm(q.reshape(b, s, MEM_HEADS, MEM_HEAD_DIM), g_q)
    kh = rmsnorm(k.reshape(b, m, MEM_HEADS, MEM_HEAD_DIM), g_k)
    vh = v.reshape(b, m, MEM_HEADS, MEM_HEAD_DIM)
    scores = jnp.einsum("bshd,bmhd->bhsm", qh, kh).astype(jnp.float32) * (MEM_HEAD_DIM ** -0.5)
    p = jax.nn.softmax(scores, axis=-1).astype(vh.dtype)
    o = jnp.einsum("bhsm,bmhd->bshd", p, vh)
    return o.reshape(b, s, MEM_WIDTH)

def setup_inputs(seed: int = 0) -> dict:
    key = jax.random.key(seed)
    ks = jax.random.split(key, 13)
    f32 = jnp.float32
    x = jax.random.normal(ks[0], (BATCH, SEQ, D_MODEL), f32)
    mem = jax.random.normal(ks[1], (BATCH, N_MEM, D_MODEL), f32)
    w_in = jax.random.normal(ks[2], (DEPTH, D_MODEL, IN_WIDTH), f32) * D_MODEL ** -0.5
    w_out = jax.random.normal(ks[3], (DEPTH, OUT_WIDTH, D_MODEL), f32) * OUT_WIDTH ** -0.5
    w_mem_kv = jax.random.normal(ks[4], (DEPTH, D_MODEL, 2 * MEM_WIDTH), f32) * D_MODEL ** -0.5
    w_conv = jax.random.normal(ks[5], (N_CONV_LAYERS, CONV_WIDTH, MIX_WIDTH), f32) * CONV_WIDTH ** -0.5
    w_ffn_in = jax.random.normal(ks[6], (DEPTH, D_MODEL, 2 * D_FF), f32) * D_MODEL ** -0.5
    w_ffn_out = jax.random.normal(ks[7], (DEPTH, D_FF, D_MODEL), f32) * D_FF ** -0.5
    g_mix = 1.0 + 0.02 * jax.random.normal(ks[8], (DEPTH, D_MODEL), f32)
    g_mem = 1.0 + 0.02 * jax.random.normal(ks[9], (DEPTH, D_MODEL), f32)
    g_ffn = 1.0 + 0.02 * jax.random.normal(ks[10], (DEPTH, D_MODEL), f32)
    g_q = 1.0 + 0.02 * jax.random.normal(ks[11], (DEPTH, MEM_HEAD_DIM), f32)
    g_k = 1.0 + 0.02 * jax.random.normal(ks[12], (DEPTH, MEM_HEAD_DIM), f32)
    return {"x": x, "mem": mem, "w_in": w_in, "w_out": w_out, "w_mem_kv": w_mem_kv,
            "w_conv": w_conv, "w_ffn_in": w_ffn_in, "w_ffn_out": w_ffn_out,
            "g_mix": g_mix, "g_mem": g_mem, "g_ffn": g_ffn, "g_q": g_q, "g_k": g_k}

def reference(x, mem, w_in, w_out, w_mem_kv, w_conv, w_ffn_in, w_ffn_out,
              g_mix, g_mem, g_ffn, g_q, g_k):
    b, s, _ = x.shape
    for i in range(DEPTH):
        h = rmsnorm(x, g_mix[i])
        proj = h @ w_in[i]
        p0, p1, p2 = jnp.split(proj[..., :3 * MIX_WIDTH], 3, axis=-1)
        q_mem = proj[..., 3 * MIX_WIDTH:]
        if i % N_MIXERS == 0:
            mixed = short_conv_mixer(p0, p1, p2, w_conv[i // N_MIXERS])
        else:
            def heads(t):
                return t.reshape(b, s, SB_HEADS, SB_HEAD_DIM).transpose(0, 2, 1, 3)
            o = stick_breaking_attention(heads(p0), heads(p1), heads(p2))
            mixed = o.transpose(0, 2, 1, 3).reshape(b, s, MIX_WIDTH)
        mem_kv = rmsnorm(mem, g_mem[i]) @ w_mem_kv[i]
        mem_out = memory_cross_attention(q_mem, mem_kv, g_q[i], g_k[i])
        x = x + jnp.concatenate([mixed, mem_out], axis=-1) @ w_out[i]
        h = rmsnorm(x, g_ffn[i])
        gate, up = jnp.split(h @ w_ffn_in[i], 2, axis=-1)
        x = x + (jax.nn.silu(gate) * up) @ w_ffn_out[i]
    return x


_drawn_inputs = setup_inputs


def setup_inputs(seed=0):
    import zlib

    import numpy as np

    out = dict(_drawn_inputs(seed))
    spreads = {}
    factors = {'g_mem': 8.0, 'g_ffn': 3.366, 'g_q': 8.0, 'g_k': 8.0}
    for name, (base, spread) in spreads.items():
        noise = np.random.default_rng([zlib.crc32(name.encode()), seed]).standard_normal(out[name].shape)
        drawn = base * np.exp(spread * noise) if base else spread * noise
        out[name] = __import__('jax').numpy.asarray(drawn.astype(out[name].dtype))
    for name, factor in factors.items():
        out[name] = (out[name] * factor).astype(out[name].dtype)
    return out
```

```python
from contextlib import ExitStack

import numpy as np

import concourse.bass as bass
from concourse import mybir

F32 = mybir.dt.float32
F32R = mybir.dt.float32r
ALU = mybir.AluOpType
ACT = mybir.ActivationFunctionType
AX_X = mybir.AxisListType.X

P = 128
SEQ, DM, LAYERS = 1024, 1024, 2
KB = DM // P
HALF = 512
NMEM, MHEADS = 256, 4
SHEAD = 64
FF = 2816
FBLK = FF // P
FGROUPS = FBLK // 2
EPS = 1e-6
UCOLS = KB * P
WSLOTS = 3
MASKED = -1.0e30

A_UNITS = 2 * MHEADS
B_UNITS = MHEADS
C_UNITS = 3 * KB
E_UNITS = 3 * (KB // 2)
F_UNITS = 6 * FGROUPS
LAYER_UNITS = B_UNITS + C_UNITS + E_UNITS + F_UNITS
UNITS = LAYERS * (A_UNITS + LAYER_UNITS)


def pack_weights(w_in, w_out, w_mem_kv, w_ffn_in, w_ffn_out):
    def cols(w, c0, k0=0, kn=KB, n=P):
        return w[k0 * P:(k0 + kn) * P, c0:c0 + n].reshape(kn, P, n).transpose(1, 0, 2).reshape(P, kn * n)

    units = []
    for i in range(LAYERS):
        units += [cols(w_mem_kv[i], c * P) for c in range(A_UNITS)]
    for i in range(LAYERS):
        units += [cols(w_in[i], 3 * DM + h * P) for h in range(MHEADS)]
        for b in range(KB):
            units += [cols(w_in[i], part * DM + b * P) for part in range(3)]
        for m in range(0, KB, 2):
            units += [cols(w_out[i], m * P), cols(w_out[i], (m + 1) * P),
                      cols(w_out[i], m * P, KB, MHEADS, 2 * P)]

        def gate_up(g, part):
            return [cols(w_ffn_in[i], part * FF + (2 * g + j) * P) for j in range(2)]

        units += gate_up(0, 0) + gate_up(0, 1)
        for g in range(1, FGROUPS):
            units += gate_up(g, 0)
            units += [w_ffn_out[i, (2 * (g - 1) + j) * P:(2 * (g - 1) + j + 1) * P] for j in range(2)]
            units += gate_up(g, 1)
        units += [w_ffn_out[i, (FBLK - 2 + j) * P:(FBLK - 1 + j) * P] for j in range(2)]
    return np.ascontiguousarray(np.stack(units))


def trunk(nc, xT, memT, wpack, vectors, out):
    base = {}
    u = f = v = 0
    for i in range(LAYERS):
        base["A", i] = (u, f, v)
        u, v = u + A_UNITS, v + A_UNITS
    for i in range(LAYERS):
        base["B", i] = (u, f, v)
        u, f, v = u + B_UNITS, f + B_UNITS, v + 2 * B_UNITS
        base["C", i] = (u, f, v)
        u, f, v = u + C_UNITS, f + C_UNITS, v + 2 * C_UNITS
        base["E", i] = (u, f, v)
        u, f, v = u + E_UNITS, f + 3 * (KB // 2), v + 2 * KB
        base["F", i] = (u, f, v)
        u, f, v = u + F_UNITS, f + 4 * FGROUPS + 15 * FGROUPS, v + 24 * FGROUPS
        base["end", i] = (u, f, v)
    assert u == UNITS and u % WSLOTS == 0

    with ExitStack() as ctx:
        arena_bytes = (nc.sbuf_usable_end - nc.sbuf_base) // 32 * 32 - 64
        arena = ctx.enter_context(nc.sbuf_tensor("arena", [P, arena_bytes // 4], F32))
        arena_start = (nc.sbuf_base - arena_bytes)
        cursor = [0]

        def place(name, shape, dt, offset=None):
            size = 4 * int(np.prod(shape[1:]))
            if offset is None:
                offset = cursor[0]
                cursor[0] += (size + 31) // 32 * 32
            assert offset + size <= arena_bytes, (name, offset, size, arena_bytes)
            return nc.alloc_sbuf_tensor_at(name, shape, dt, offset=arena_start + offset)

        def sem(name):
            return ctx.enter_context(nc.semaphore(name))

        x = place("x", [P, KB, SEQ], F32)
        xg_hi = place("xg_hi", [P, KB, SEQ], F32R)
        xg_lo = place("xg_lo", [P, KB, SEQ], F32R)
        raw = place("raw", [P, WSLOTS, UCOLS], F32)
        w_hi = place("w_hi", [P, WSLOTS, UCOLS], F32R)
        w_lo = place("w_lo", [P, WSLOTS, UCOLS], F32R)
        R = place("R", [P, SEQ], F32)
        ident = place("ident", [P, P], F32)
        ident_r = place("ident_r", [P, P], F32R)
        mask_r = place("mask_r", [P, 2 * P], F32R)
        mean_all = place("mean_all", [P, P], F32)
        mean_head = place("mean_head", [P, P], F32)
        gain = place("gain", [P, 3, LAYERS, KB], F32)
        taps = place("taps", [P, 3, KB], F32)
        g_heads = place("g_heads", [P, 2, LAYERS], F32)
        g_qk = place("g_qk", [P, LAYERS], F32)
        eps = place("eps", [P, 1], F32)
        smax = place("smax", [P, 4], F32)
        nbias = place("nbias", [P, 4], F32)
        psums = place("psums", [P, 4], F32)
        rsums = place("rsums", [P, 4], F32)
        rq_v = place("rq_v", [P, KB], F32)
        rq_s = place("rq_s", [P, KB], F32)
        rq_t = place("rq_t", [P, KB], F32)
        rq = place("rq", [P, 2, KB], F32)
        Z = cursor[0]
        K1 = 1024
        sq = place("sq", [P, 2, SEQ], F32, Z + 48 * K1)
        acc = place("acc", [P, SEQ], F32, Z + 56 * K1)
        rtmp = place("rtmp", [P, SEQ], F32, Z + 60 * K1)
        mem = place("mem", [P, KB, NMEM], F32, Z)
        mg_hi = place("mg_hi", [P, KB, NMEM], F32R, Z + 8 * K1)
        mg_lo = place("mg_lo", [P, KB, NMEM], F32R, Z + 16 * K1)
        kf = place("kf", [P, MHEADS * NMEM], F32, Z + 24 * K1)
        ksq = place("ksq", [P, MHEADS * NMEM], F32, Z + 28 * K1)
        kr = place("kr", [P, MHEADS * NMEM], F32, Z + 32 * K1)
        kn = place("kn", [P, MHEADS * NMEM], F32, Z + 36 * K1)
        ka_hi = place("ka_hi", [P, MHEADS * NMEM], F32R, Z + 40 * K1)
        ka_lo = place("ka_lo", [P, MHEADS * NMEM], F32R, Z + 44 * K1)
        va_hi = place("va_hi", [P, 2, MHEADS * P], F32R, Z + 48 * K1)
        va_lo = place("va_lo", [P, 2, MHEADS * P], F32R, Z + 52 * K1)
        msq = place("msq", [P, KB, NMEM], F32, Z + 56 * K1)
        mr = place("mr", [P, NMEM], F32, Z + 64 * K1)
        mrt = place("mrt", [P, NMEM], F32, Z + 65 * K1)
        mask_f = place("mask_f", [P, 2 * P], F32, Z + 66 * K1)
        q_hi = place("q_hi", [P, 2, SEQ], F32R, Z)
        q_lo = place("q_lo", [P, 2, SEQ], F32R, Z + 8 * K1)
        k_hi = place("k_hi", [P, MHEADS * NMEM], F32R, Z + 16 * K1)
        k_lo = place("k_lo", [P, MHEADS * NMEM], F32R, Z + 20 * K1)
        v_hi = place("v_hi", [P, 2, MHEADS * P], F32R, Z + 24 * K1)
        v_lo = place("v_lo", [P, 2, MHEADS * P], F32R, Z + 28 * K1)
        pT_hi = place("pT_hi", [P, 2, HALF], F32R, Z + 32 * K1)
        pT_lo = place("pT_lo", [P, 2, HALF], F32R, Z + 36 * K1)
        mo_hi = place("mo_hi", [P, SEQ], F32R, Z + 40 * K1)
        mo_lo = place("mo_lo", [P, SEQ], F32R, Z + 44 * K1)
        qf = place("qf", [P, SEQ], F32, Z + 48 * K1)
        qsq = place("qsq", [P, SEQ], F32, Z + 52 * K1)
        prob = place("prob", [P, 4, NMEM], F32, Z + 64 * K1)
        cb = place("cb", [P, SEQ], F32, Z)
        cc = place("cc", [P, SEQ], F32, Z + 4 * K1)
        cu = place("cu", [P, SEQ], F32, Z + 8 * K1)
        cy = place("cy", [P, SEQ + 2], F32, Z + 12 * K1)
        cz = place("cz", [P, SEQ], F32, Z + 20 * K1)
        cm_hi = place("cm_hi", [P, SEQ], F32R, Z + 24 * K1)
        cm_lo = place("cm_lo", [P, SEQ], F32R, Z + 28 * K1)
        keep = place("keep", [P, 2, 2, SEQ], F32, 0)
        sig = place("sig", [P, 2, 2, SEQ], F32, 16 * K1)
        sq_hi = place("sq_hi", [P, 2, SEQ], F32R, Z)
        sq_lo = place("sq_lo", [P, 2, SEQ], F32R, Z + 8 * K1)
        sk_hi = place("sk_hi", [P, 2, SEQ], F32R, Z + 16 * K1)
        sk_lo = place("sk_lo", [P, 2, SEQ], F32R, Z + 24 * K1)
        sv = place("sv", [P, 2, KB, 2, P], F32R, Z + 32 * K1)
        aT_hi = place("aT_hi", [P, 2, 2, 2 * P], F32R, Z + 48 * K1)
        aT_lo = place("aT_lo", [P, 2, 2, 2 * P], F32R, Z + 52 * K1)
        tf = place("tf", [P, SEQ], F32, Z + 56 * K1)
        so_hi = place("so_hi", [P, 2, 2 * P], F32R, Z + 60 * K1)
        so_lo = place("so_lo", [P, 2, 2 * P], F32R, Z + 62 * K1)
        o_low = place("o_low", [P, 2 * P], F32, Z + 64 * K1)
        o_sum = place("o_sum", [P, 2 * P], F32, Z + 65 * K1)
        me_hi = place("me_hi", [P, MHEADS, SEQ], F32R, Z)
        me_lo = place("me_lo", [P, MHEADS, SEQ], F32R, Z + 16 * K1)
        act_hi = place("act_hi", [P, 2, SEQ], F32R, Z)
        act_lo = place("act_lo", [P, 2, SEQ], F32R, Z + 8 * K1)
        gate = place("gate", [P, 2, SEQ], F32, Z + 16 * K1)
        up = place("up", [P, 2, SEQ], F32, Z + 24 * K1)

        ps = ctx.enter_context(nc.psum_tensor("ps", [P, 8, HALF], F32))

        def banks(b, n=2):
            return ps[:, b:b + n, :].rearrange("p a c -> p (a c)")

        d_kv = nc.dram_tensor("d_kv", (LAYERS, 4, P, MHEADS * NMEM), F32R, kind="Internal").ap()
        d_mo = nc.dram_tensor("d_mo", (LAYERS, 2, MHEADS, P, SEQ), F32R, kind="Internal").ap()
        d_mix = nc.dram_tensor("d_mix", (LAYERS, 2, KB, P, SEQ), F32R, kind="Internal").ap()
        d_x = nc.dram_tensor("d_x", (P, KB, SEQ), F32, kind="Internal").ap()

        consts_in = sem("consts_in")
        x_in = sem("x_in")
        mem_in = sem("mem_in")
        consts_made = sem("consts_made")
        ident_steps = sem("ident_steps")
        raw_landed = [sem(f"raw_landed{s}") for s in range(WSLOTS)]
        w_hi_ready = sem("w_hi_ready")
        w_lo_ready = sem("w_lo_ready")
        w_used = sem("w_used")
        bank_full = sem("bank_full")
        evacuated = sem("evacuated")
        xg_hi_ready = sem("xg_hi_ready")
        xg_lo_ready = sem("xg_lo_ready")
        sq_ready = sem("sq_ready")
        acc_added = sem("acc_added")
        stat_full = sem("stat_full")
        root_ready = sem("root_ready")
        r_ready = sem("r_ready")
        eps_made = sem("eps_made")
        msq_ready = sem("msq_ready")
        mstat_full = sem("mstat_full")
        mroot_ready = sem("mroot_ready")
        mr_ready = sem("mr_ready")
        mem_normed = sem("mem_normed")
        gqk_ready = sem("gqk_ready")
        mg_hi_ready = sem("mg_hi_ready")
        mg_lo_ready = sem("mg_lo_ready")
        ksq_ready = sem("ksq_ready")
        kstat_full = sem("kstat_full")
        kroot_ready = sem("kroot_ready")
        kr_ready = sem("kr_ready")
        kn_ready = sem("kn_ready")
        ka_hi_ready = sem("ka_hi_ready")
        ka_lo_ready = sem("ka_lo_ready")
        va_hi_ready = sem("va_hi_ready")
        kv_stored = sem("kv_stored")
        kv_loaded = sem("kv_loaded")
        q_hi_ready = sem("q_hi_ready")
        q_lo_ready = sem("q_lo_ready")
        qsq_ready = sem("qsq_ready")
        qstat_full = sem("qstat_full")
        rqv_ready = sem("rqv_ready")
        rqs_ready = sem("rqs_ready")
        rq_step = sem("rq_step")
        rq_ready = sem("rq_ready")
        scores_full = sem("scores_full")
        max_ready = sem("max_ready")
        nbias_ready = sem("nbias_ready")
        exp_done = sem("exp_done")
        rsum_ready = sem("rsum_ready")
        prob_ready = sem("prob_ready")
        pT_full = sem("pT_full")
        pT_hi_ready = sem("pT_hi_ready")
        pT_lo_ready = sem("pT_lo_ready")
        mo_full = sem("mo_full")
        mo_hi_ready = sem("mo_hi_ready")
        mo_lo_ready = sem("mo_lo_ready")
        mo_stored = sem("mo_stored")
        conv_step = sem("conv_step")
        cm_hi_ready = sem("cm_hi_ready")
        cm_lo_ready = sem("cm_lo_ready")
        cm_stored = sem("cm_stored")
        x_spilled = sem("x_spilled")
        x_back = sem("x_back")
        z_full = sem("z_full")
        keep_ready = sem("keep_ready")
        sig_ready = sem("sig_ready")
        scanned = sem("scanned")
        a_ready = sem("a_ready")
        aT_full = sem("aT_full")
        aT_hi_ready = sem("aT_hi_ready")
        aT_lo_ready = sem("aT_lo_ready")
        pv_done = sem("pv_done")
        o_low_ready = sem("o_low_ready")
        o_sum_ready = sem("o_sum_ready")
        so_hi_ready = sem("so_hi_ready")
        so_lo_ready = sem("so_lo_ready")
        so_stored = [sem(f"so_stored{p}") for p in range(2)]
        sqk_hi_ready = sem("sqk_hi_ready")
        sqk_lo_ready = sem("sqk_lo_ready")
        vT_full = sem("vT_full")
        vT_hi_ready = sem("vT_hi_ready")
        vT_lo_ready = sem("vT_lo_ready")
        e_early = sem("e_early")
        e_late = sem("e_late")
        silu_done = sem("silu_done")
        prod_ready = sem("prod_ready")
        act_hi_ready = sem("act_hi_ready")
        act_lo_ready = sem("act_lo_ready")
        out_stored = sem("out_stored")

        block = ctx.enter_context(nc.Block())

        def fp(ap):
            return ap.bitcast(F32)

        def x_visit(nu, m, h):
            if nu in (1, 3):
                return base["E", nu // 2][2] + 2 * m + h
            return base["end", 0][2] - 2 * KB + 2 * m + h

        def split_count(nu, m, h):
            return 2 * KB * nu + (2 * m + h if nu == 2 else KB * h + m) + 1

        def split_order(nu):
            return [(m, h) for m in range(KB) for h in range(2)] if nu == 2 else \
                   [(m, h) for h in range(2) for m in range(KB)]

        CHUNKS_BEFORE = [sum(j % 4 + 1 for j in range(it)) for it in range(9)]
        ITEMS, ROWS, CHUNKS = 8, 16, CHUNKS_BEFORE[8]
        ln = slice(0, HALF), slice(HALF, SEQ)

        @block.sync
        def _(sp):
            sp.dma_start(mem[:], memT).then_inc(mem_in, 16)
            for name, src in vectors:
                dst = {"gain": gain, "taps": taps, "g_heads": g_heads}[name]
                sp.dma_start(dst[:], src).then_inc(consts_in, 16)
            for s in range(WSLOTS):
                sp.dma_start(raw[:, s, :], wpack[s]).then_inc(raw_landed[s], 16)
            for h in range(2):
                sp.dma_start(x[:, :, ln[h]], xT[:, :, ln[h]]).then_inc(x_in, 16)
            with sp.Fori(1, UNITS // WSLOTS) as i:
                for s in range(WSLOTS):
                    sp.wait_ge(w_lo_ready, i * WSLOTS + (s + 1 - WSLOTS))
                    sp.dma_start(raw[:, s, :], wpack[bass.ds(i * WSLOTS + s, 1)].rearrange("a p c -> (a p) c")
                                 ).then_inc(raw_landed[s], 16)
            v_end = base["end", LAYERS - 1][2] - 2 * KB
            for m in range(KB):
                sp.wait_ge(evacuated, v_end + 2 * m + 2)
                sp.dma_start(out[:, m, :], x[:, m, :]).then_inc(out_stored, 16)
            sp.wait_ge(out_stored, 16 * KB)

        @block.gpsimd
        def _(pool):
            pool.memset(ident[:], 0.0).then_inc(ident_steps, 1)
            pool.memset(mask_f[:], MASKED).then_inc(ident_steps, 1)
            pool.memset(mean_all[:], 1.0 / DM).then_inc(consts_made, 1)
            pool.memset(mean_head[:], 1.0 / P).then_inc(consts_made, 1)
            pool.wait_ge(ident_steps, 2)
            pool.affine_select(out=ident[:], in_=ident[:], compare_op=ALU.not_equal, fill=1.0, base=0,
                               pattern=[[-1, P]], channel_multiplier=1).then_inc(ident_steps, 1)
            pool.affine_select(out=mask_f[:], in_=mask_f[:], compare_op=ALU.is_ge,
                               fill=0.0, base=0, pattern=[[1, 2 * P]], channel_multiplier=-1
                               ).then_inc(ident_steps, 1)

            for i in range(LAYERS):
                pool.wait_ge(ka_lo_ready, i + 1)
                pool.wait_ge(evacuated, base["A", i][2] + A_UNITS)
                for n, t in enumerate((ka_hi, ka_lo)):
                    pool.dma_start(d_kv[i, n], t[:]).then_inc(kv_stored, 16)
                for n, t in enumerate((va_hi, va_lo)):
                    pool.dma_start(d_kv[i, 2 + n], t[:].rearrange("p a c -> p (a c)")).then_inc(kv_stored, 16)
                pool.wait_ge(kv_stored, 64 * (i + 1))

            def fetch_mixed(i):
                for n, (t, m) in enumerate(((xg_hi, me_hi), (xg_lo, me_lo))):
                    pool.dma_start(m[:], d_mo[i, n].rearrange("h p c -> p h c")).then_inc(e_early, 16)
                    pool.dma_start(t[:, 0:KB - 1, :], d_mix[i, n, 0:KB - 1].rearrange("b p c -> p b c")
                                   ).then_inc(e_early, 16)
                    pool.dma_start(t[:, KB - 1, :], d_mix[i, n, KB - 1]).then_inc(e_late, 16)

            for i in range(LAYERS):
                if i > 0:
                    pool.wait_ge(evacuated, base["end", i - 1][2])
                for n, t in enumerate((k_hi, k_lo)):
                    pool.dma_start(t[:], d_kv[i, n]).then_inc(kv_loaded, 16)
                for n, t in enumerate((v_hi, v_lo)):
                    pool.dma_start(t[:].rearrange("p a c -> p (a c)"), d_kv[i, 2 + n]).then_inc(kv_loaded, 16)
                if i % 2 == 1:
                    pool.wait_ge(xg_lo_ready, 2 * KB * (2 * i + 1))
                    pool.wait_ge(acc_added, KB * (2 * i + 1))
                    pool.dma_start(d_x, x[:]).then_inc(x_spilled, 16)
                for h in range(MHEADS):
                    pool.wait_ge(mo_lo_ready, 2 * (MHEADS * i + h) + 2)
                    for n, t in enumerate((mo_hi, mo_lo)):
                        pool.dma_start(d_mo[i, n, h], t[:]).then_inc(mo_stored, 16)
                if i % 2 == 0:
                    with pool.Fori(0, KB) as b:
                        pool.wait_ge(cm_lo_ready, b + 1)
                        for n, t in enumerate((cm_hi, cm_lo)):
                            pool.dma_start(d_mix[i, n, bass.ds(b, 1)].rearrange("a p c -> (a p) c"), t[:]
                                           ).then_inc(cm_stored, 16)
                    pool.wait_ge(w_used, base["E", i][0])
                    pool.wait_ge(mo_stored, 32 * MHEADS * (i + 1))
                    pool.wait_ge(cm_stored, 32 * KB)
                    fetch_mixed(i)
                else:
                    def weigh(row, par, r, t):
                        n = 2 * P * (t + 1)
                        pool.wait_ge(scanned, row + 1)
                        pool.wait_ge(sig_ready, row + 1)
                        pool.tensor_tensor(sig[:, par, r, 0:n - 1], sig[:, par, r, 0:n - 1],
                                           keep[:, par, r, 1:n], ALU.mult).then_inc(a_ready, 1)

                    def pair(hp, last):
                        for it in range(ITEMS):
                            if not (last and it == ITEMS - 1):
                                for r in range(2):
                                    weigh(hp * ROWS + (2 * (it + 1) + r), (it + 1) % 2, r, (it + 1) % 4)
                            rows = slice(it // 4 * SHEAD, (it // 4 + 1) * SHEAD)
                            toks = slice(it % 4 * 2 * P, (it % 4 + 1) * 2 * P)
                            pool.wait_ge(so_lo_ready, hp * ITEMS + (it + 1))
                            for n, t in enumerate((so_hi, so_lo)):
                                pool.dma_start(d_mix[i, n, bass.ds(hp, 1), rows, toks].rearrange("a p c -> (a p) c"),
                                               t[rows, it % 2, :]).then_inc(so_stored[it % 2], 16)

                    for r in range(2):
                        weigh(r, 0, r, 0)
                    with pool.Fori(0, KB - 1) as hp:
                        pair(hp, False)
                    pair(KB - 1, True)
                    pool.wait_ge(w_used, base["E", i][0])
                    pool.wait_ge(mo_stored, 32 * MHEADS * (i + 1))
                    for p in range(2):
                        pool.wait_ge(so_stored[p], 32 * ITEMS // 2 * KB)
                    fetch_mixed(i)
                    pool.wait_ge(pv_done, CHUNKS * KB)
                    pool.dma_start(x[:], d_x).then_inc(x_back, 16)

        @block.scalar
        def _(act):
            def prep(u, more=0, rounds=0):
                s = u % WSLOTS
                if u >= UNITS:
                    return
                act.wait_ge(raw_landed[s], rounds * 16 + (u // WSLOTS + 1) * 16)
                if u >= WSLOTS:
                    act.wait_ge(w_used, more + (u - WSLOTS + 1))
                act.activation(w_hi[:, s, :], raw[:, s, :], ACT.Copy).then_inc(w_hi_ready, 1)

            def split(nu, m, h):
                i, g = nu // 2, 2 * (nu % 2)
                if nu == 0:
                    act.wait_ge(x_in, 32)
                elif nu == 2:
                    act.wait_ge(evacuated, base["end", 0][2] - 2 * KB + 2 * m + h + 1)
                else:
                    act.wait_ge(evacuated, base["F", i][2])
                act.activation(xg_hi[:, m, ln[h]], x[:, m, ln[h]], ACT.Copy, scale=gain[:, g, i, m:m + 1]
                               ).then_inc(xg_hi_ready, 1)

            def squares_and_root(nu, u0):
                for m in range(KB):
                    n = KB * nu + m
                    if n >= 2:
                        act.wait_ge(acc_added, n - 1)
                    act.activation(sq[:, m % 2, :], x[:, m, :], ACT.Square).then_inc(sq_ready, 1)
                prep(u0 + 2)
                prep(u0 + 3)
                act.wait_ge(stat_full, 2 * nu + 2)
                act.activation(rtmp[:], banks(4), ACT.Sqrt, bias=eps[:, 0:1]).then_inc(root_ready, 1)

            act.wait_ge(ident_steps, 4)
            act.activation(ident_r[:], ident[:], ACT.Copy).then_inc(consts_made, 1)
            act.activation(mask_r[:], mask_f[:], ACT.Copy).then_inc(consts_made, 1)

            prep(0)
            prep(1)
            act.wait_ge(mem_in, 16)
            act.activation(msq[:], mem[:], ACT.Square).then_inc(msq_ready, 1)
            act.wait_ge(mstat_full, 1)
            act.wait_ge(eps_made, 1)
            act.activation(mrt[:], ps[:, 4, 0:NMEM], ACT.Sqrt, bias=eps[:, 0:1]).then_inc(mroot_ready, 1)
            act.wait_ge(consts_in, 48)
            for i in range(LAYERS):
                u0, f0, v0 = base["A", i]
                act.wait_ge(mem_normed, KB)
                if i > 0:
                    act.wait_ge(w_used, u0)
                for m in range(KB):
                    act.activation(mg_hi[:, m, :], mem[:, m, :], ACT.Copy, scale=gain[:, 1, i, m:m + 1]
                                   ).then_inc(mg_hi_ready, 1)
                for n in range(MHEADS):
                    prep(u0 + n + 2)
                act.wait_ge(evacuated, v0 + MHEADS)
                act.activation(ksq[:], kf[:], ACT.Square).then_inc(ksq_ready, 1)
                for n in range(MHEADS):
                    prep(u0 + MHEADS + n + 2)
                    act.wait_ge(w_used, u0 + MHEADS + n + 1)
                    if i > 0:
                        act.wait_ge(kv_stored, 64 * i)
                    act.activation(va_hi[:, :, n * P:(n + 1) * P],
                                   ps[:, 6 + n % 2, 0:2 * P].rearrange("p (a c) -> p a c", a=2), ACT.Copy
                                   ).then_inc(va_hi_ready, 1)
                act.wait_ge(kstat_full, 2 * (i + 1))
                act.activation(kr[:], banks(4), ACT.Sqrt, bias=eps[:, 0:1]).then_inc(kroot_ready, 1)
                act.wait_ge(kn_ready, i + 1)
                act.activation(ka_hi[:], kn[:], ACT.Copy).then_inc(ka_hi_ready, 1)
            for m, h in split_order(0):
                split(0, m, h)

            for i in range(LAYERS):
                u0, f0, v0 = base["B", i]
                if i == 0:
                    act.wait_ge(kv_stored, 64 * LAYERS)
                squares_and_root(2 * i, u0)

                def query(h):
                    hd = MHEADS * i + h
                    act.wait_ge(evacuated, v0 + 2 * h + 2)
                    if h >= 2:
                        act.wait_ge(scores_full, 2 * (hd - 1))
                    act.activation(q_hi[:, h % 2, :], qf[:], ACT.Copy).then_inc(q_hi_ready, 1)
                    act.activation(qsq[:], qf[:], ACT.Square).then_inc(qsq_ready, 1)
                    act.wait_ge(rqv_ready, hd + 1)
                    act.activation(rq_s[:], rq_v[:], ACT.Sqrt).then_inc(rqs_ready, 1)

                def attend(h):
                    for half in range(2):
                        hd = MHEADS * i + h
                        n = 2 * hd + half
                        act.wait_ge(nbias_ready, n + 1)
                        if n > 0:
                            act.wait_ge(pT_full, n)
                        for j in range(4):
                            act.activation(prob[:, j, :], banks(4)[:, j * NMEM:(j + 1) * NMEM], ACT.Exp,
                                           bias=nbias[:, j:j + 1],
                                           scale=rq[:, h % 2, 4 * half + j:4 * half + j + 1],
                                           accum_out=psums[:, j:j + 1]).then_inc(exp_done, 1)
                        act.wait_ge(pT_full, n + 1)
                        if n > 0:
                            act.wait_ge(mo_full, n)
                        act.activation(pT_hi[:].rearrange("p a c -> p (a c)"), banks(6), ACT.Copy
                                       ).then_inc(pT_hi_ready, 1)
                        act.wait_ge(mo_full, n + 1)
                        if half == 0 and hd > 0:
                            act.wait_ge(mo_stored, 32 * hd)
                        act.activation(mo_hi[:, ln[half]], ps[:, 2, :], ACT.Copy).then_inc(mo_hi_ready, 1)

                query(0)
                prep(u0 + 4)
                query(1)
                attend(0)
                prep(u0 + 5)
                query(2)
                attend(1)
                query(3)
                attend(2)
                attend(3)

                u0, f0, v0 = base["C", i]
                if i % 2 == 0:
                    with act.Fori(0, KB) as b:
                        for j in range(3):
                            prep(u0 + j + 2, b * 3, b)
                        act.wait_ge(conv_step, b * 5 + 6)
                        act.activation(cm_hi[:], cz[:], ACT.Copy).then_inc(cm_hi_ready, 1)
                        act.wait_ge(cm_stored, b * 32 + 32)
                else:
                    def sigmoids(row, par, r, t):
                        n = 2 * P * (t + 1)
                        act.wait_ge(z_full, row + 1)
                        z = banks(2 * r)[:, 0:n]
                        act.activation(keep[:, par, r, 0:n], z, ACT.Sigmoid, scale=-1.0).then_inc(keep_ready, 1)
                        act.activation(sig[:, par, r, 0:n], z, ACT.Sigmoid).then_inc(sig_ready, 1)

                    def project(hp, to, piece):
                        if piece in (1, 3):
                            act.wait_ge(evacuated, hp * 6 + (v0 + piece + 1))
                            dst = (sq_hi, sk_hi)[piece // 2]
                            act.activation(dst[:, to, :], tf[:], ACT.Copy).then_inc(sqk_hi_ready, 1)
                        if piece >= 6:
                            act.wait_ge(vT_full, hp * 2 + (piece - 5))
                            dst = sv[:, to, 4 * (piece - 6):4 * (piece - 5), :, 0:SHEAD]
                            act.activation(dst, ps[:, 7, :].rearrange("p (b h c) -> p b h c", b=4, h=2), ACT.Copy
                                           ).then_inc(vT_hi_ready, 1)

                    def pair(hp, par, last, first=False):
                        for it in range(ITEMS):
                            t, hh = it % 4, it // 4
                            if not last and it % 2 == 1 and it < 6:
                                prep(u0 + 3 + 2 + it // 2, hp * 3, hp)
                            if not (last and it == ITEMS - 1):
                                for r in range(2):
                                    sigmoids(hp * ROWS + (2 * (it + 1) + r), (it + 1) % 2, r, (it + 1) % 4)
                            if not last:
                                project(hp + 1, 1 - par, it)
                            for c in range(t + 1):
                                n = CHUNKS_BEFORE[it] + c
                                act.wait_ge(aT_full, hp * CHUNKS + (n + 1))
                                if not (first and n < 2):
                                    act.wait_ge(pv_done, hp * CHUNKS + (n - 1))
                                act.activation(aT_hi[:, n % 2].rearrange("p a c -> p (a c)"), ps[:, 4 + n % 2, :],
                                               ACT.Copy).then_inc(aT_hi_ready, 1)
                            rows = slice(hh * SHEAD, (hh + 1) * SHEAD)
                            act.wait_ge(pv_done, hp * CHUNKS + CHUNKS_BEFORE[it + 1])
                            if not (first and it == 0):
                                act.wait_ge(o_sum_ready, hp * ITEMS + it)
                            act.activation(o_low[rows, :], ps[SHEAD:P, 6, 0:2 * P], ACT.Copy
                                           ).then_inc(o_low_ready, 1)
                            act.wait_ge(o_sum_ready, hp * ITEMS + (it + 1))
                            if not (first and it < 2):
                                act.wait_ge(so_stored[it % 2], hp * (16 * ITEMS) + 32 * (it // 2))
                            act.activation(so_hi[rows, it % 2, :], o_sum[rows, :], ACT.Copy
                                           ).then_inc(so_hi_ready, 1)

                    for piece in range(ITEMS):
                        if piece % 2 == 1 and piece < 6:
                            prep(u0 + 2 + piece // 2)
                        project(0, 0, piece)
                    act.wait_ge(x_spilled, 16)
                    for r in range(2):
                        sigmoids(r, 0, r, 0)
                    pair(0, 0, False, first=True)
                    with act.Fori(0, KB // 2 - 1) as d:
                        pair(d * 2 + 1, 1, False)
                        pair(d * 2 + 2, 0, False)
                    pair(KB - 1, 1, True)

                u0, f0, v0 = base["E", i]
                with act.Fori(0, KB // 2) as pm:
                    for j in range(3):
                        prep(u0 + j + 2, pm * 3, pm)

                u0, f0, v0 = base["F", i]
                nu, a0 = 2 * i + 1, FBLK * i
                for m, h in split_order(nu):
                    split(nu, m, h)
                squares_and_root(nu, u0)

                def silu(blk, blocks, visits):
                    act.wait_ge(evacuated, visits)
                    act.activation(gate[:, blk, :], gate[:, blk, :], ACT.Silu).then_inc(silu_done, 1)

                def products(blocks):
                    for blk in range(2):
                        act.wait_ge(prod_ready, blocks + (blk + 1))
                        act.activation(act_hi[:, blk, :], up[:, blk, :], ACT.Copy).then_inc(act_hi_ready, 1)

                silu(0, a0, v0 + 2)
                silu(1, a0, v0 + 4)
                prep(u0 + 4)
                prep(u0 + 5)
                products(a0)
                with act.Fori(0, FGROUPS - 1) as g:
                    n, v = u0 + 4, g * 24 + (v0 + 8)
                    prep(n + 2, g * 6, g * 2)
                    silu(0, None, v + 2)
                    prep(n + 3, g * 6, g * 2)
                    silu(1, None, v + 4)
                    for j in (4, 5, 6, 7):
                        prep(n + j, g * 6, g * 2)
                    products(g * 2 + (a0 + 2))
                prep(base["end", i][0])
                if i + 1 < LAYERS:
                    for m, h in split_order(nu + 1):
                        split(nu + 1, m, h)
                    prep(base["end", i][0] + 1)

        @block.vector
        def _(dve):
            def prep(u, more=0, rounds=0):
                s = u % WSLOTS
                if u >= UNITS:
                    return
                dve.wait_ge(w_hi_ready, more + (u + 1))
                dve.tensor_tensor(w_lo[:, s, :], raw[:, s, :], fp(w_hi[:, s, :]), ALU.subtract
                                  ).then_inc(w_lo_ready, 1)

            def split(nu, m, h):
                i, g = nu // 2, 2 * (nu % 2)
                dve.wait_ge(xg_hi_ready, split_count(nu, m, h))
                dve.scalar_tensor_tensor(xg_lo[:, m, ln[h]], x[:, m, ln[h]], gain[:, g, i, m:m + 1],
                                         fp(xg_hi[:, m, ln[h]]), ALU.mult, ALU.subtract).then_inc(xg_lo_ready, 1)

            def norm(nu, u0, v0):
                for m in range(KB):
                    n = KB * nu + m
                    dve.wait_ge(sq_ready, n + 1)
                    if n > 0:
                        dve.wait_ge(acc_added, n)
                    if m == 0:
                        dve.tensor_copy(acc[:], sq[:, 0, :]).then_inc(acc_added, 1)
                    else:
                        dve.tensor_tensor(acc[:], acc[:], sq[:, m % 2, :], ALU.add).then_inc(acc_added, 1)
                prep(u0 + 2)
                prep(u0 + 3)
                dve.wait_ge(root_ready, nu + 1)
                dve.wait_ge(evacuated, v0)
                dve.reciprocal(R[:], rtmp[:]).then_inc(r_ready, 1)
                dve.wait_ge(r_ready, nu + 1)

            def scaled(dst, b, h):
                dve.tensor_tensor(dst, ps[:, b, :], R[:, ln[h]], ALU.mult).then_inc(evacuated, 1)

            dve.memset(eps[:], EPS).then_inc(eps_made, 1)

            prep(0)
            prep(1)
            dve.wait_ge(consts_in, 48)
            dve.scalar_tensor_tensor(g_qk[:], g_heads[:, 0, :], float(P) ** -0.5, g_heads[:, 1, :],
                                     ALU.mult, ALU.mult).then_inc(gqk_ready, 1)
            dve.wait_ge(mroot_ready, 1)
            dve.reciprocal(mr[:], mrt[:]).then_inc(mr_ready, 1)
            dve.wait_ge(mr_ready, 1)
            for m in range(KB):
                dve.tensor_tensor(mem[:, m, :], mem[:, m, :], mr[:], ALU.mult).then_inc(mem_normed, 1)
            dve.wait_ge(mem_normed, KB)
            dve.wait_ge(gqk_ready, 1)
            for i in range(LAYERS):
                u0, f0, v0 = base["A", i]
                for m in range(KB):
                    dve.wait_ge(mg_hi_ready, KB * i + m + 1)
                    dve.scalar_tensor_tensor(mg_lo[:, m, :], mem[:, m, :], gain[:, 1, i, m:m + 1],
                                             fp(mg_hi[:, m, :]), ALU.mult, ALU.subtract).then_inc(mg_lo_ready, 1)
                if i > 0:
                    dve.wait_ge(ka_lo_ready, i)
                for n in range(MHEADS):
                    prep(u0 + n + 2)
                    dve.wait_ge(w_used, u0 + n + 1)
                    dve.tensor_copy(kf[:, n * NMEM:(n + 1) * NMEM], ps[:, n, 0:NMEM]).then_inc(evacuated, 1)
                for n in range(MHEADS):
                    prep(u0 + MHEADS + n + 2)
                    dve.wait_ge(va_hi_ready, MHEADS * i + n + 1)
                    cols = slice(n * P, (n + 1) * P)
                    dve.tensor_tensor(va_lo[:, :, cols], ps[:, 6 + n % 2, 0:2 * P].rearrange("p (a c) -> p a c", a=2),
                                      fp(va_hi[:, :, cols]), ALU.subtract).then_inc(evacuated, 1)
                dve.wait_ge(kroot_ready, i + 1)
                dve.reciprocal(kr[:], kr[:]).then_inc(kr_ready, 1)
                dve.wait_ge(kr_ready, i + 1)
                dve.wait_ge(evacuated, v0 + MHEADS)
                dve.scalar_tensor_tensor(kn[:], kf[:], g_qk[:, i:i + 1], kr[:], ALU.mult, ALU.mult
                                         ).then_inc(kn_ready, 1)
                dve.wait_ge(ka_hi_ready, i + 1)
                if i > 0:
                    dve.wait_ge(kv_stored, 64 * i)
                dve.tensor_tensor(ka_lo[:], kn[:], fp(ka_hi[:]), ALU.subtract).then_inc(ka_lo_ready, 1)
            for m, h in split_order(0):
                split(0, m, h)

            for i in range(LAYERS):
                u0, f0, v0 = base["B", i]
                norm(2 * i, u0, v0)

                def query(h):
                    hd = MHEADS * i + h
                    if hd > 0:
                        dve.wait_ge(q_lo_ready, hd)
                        dve.wait_ge(qsq_ready, hd)
                    for half in range(2):
                        if half == 0:
                            dve.wait_ge(bank_full, f0 + h + 1)
                        else:
                            dve.wait_ge(w_used, u0 + h + 1)
                        scaled(qf[:, ln[half]], (6 if h == 1 else 0) + half, half)
                    dve.wait_ge(q_hi_ready, hd + 1)
                    dve.tensor_tensor(q_lo[:, h % 2, :], qf[:], fp(q_hi[:, h % 2, :]), ALU.subtract
                                      ).then_inc(q_lo_ready, 1)
                    dve.wait_ge(qstat_full, hd + 1)
                    if hd > 0:
                        dve.wait_ge(rq_ready, hd)
                    dve.tensor_scalar(rq_v[:], ps[:, 3, 0:KB], EPS, None, ALU.add).then_inc(rqv_ready, 1)
                    dve.wait_ge(rqs_ready, hd + 1)
                    y, s0 = rq[:, h % 2, :], 4 * hd
                    dve.reciprocal(y, rq_s[:]).then_inc(rq_step, 1)
                    dve.wait_ge(rq_step, s0 + 1)
                    dve.tensor_tensor(rq_t[:], rq_v[:], y, ALU.mult).then_inc(rq_step, 1)
                    dve.wait_ge(rq_step, s0 + 2)
                    dve.tensor_tensor(rq_t[:], rq_t[:], y, ALU.mult).then_inc(rq_step, 1)
                    dve.wait_ge(rq_step, s0 + 3)
                    dve.tensor_scalar(rq_t[:], rq_t[:], -0.5, 1.5, ALU.mult, ALU.add).then_inc(rq_step, 1)
                    dve.wait_ge(rq_step, s0 + 4)
                    dve.tensor_tensor(y, y, rq_t[:], ALU.mult).then_inc(rq_ready, 1)
                    dve.wait_ge(rq_ready, hd + 1)

                def attend(h):
                    for half in range(2):
                        n = 2 * (MHEADS * i + h) + half
                        dve.wait_ge(scores_full, n + 1)
                        if n > 0:
                            dve.wait_ge(nbias_ready, n)
                        dve.tensor_reduce(smax[:], banks(4).rearrange("p (j c) -> p j c", j=4), AX_X, ALU.max
                                          ).then_inc(max_ready, 1)
                        dve.wait_ge(max_ready, n + 1)
                        if n > 0:
                            dve.wait_ge(exp_done, 4 * n)
                        dve.scalar_tensor_tensor(nbias[:], smax[:], -1.0, rq[:, h % 2, 4 * half:4 * half + 4],
                                                 ALU.mult, ALU.mult).then_inc(nbias_ready, 1)
                        dve.wait_ge(exp_done, 4 * n + 4)
                        if n > 0:
                            dve.wait_ge(prob_ready, n)
                        dve.reciprocal(rsums[:], psums[:]).then_inc(rsum_ready, 1)
                        dve.wait_ge(rsum_ready, n + 1)
                        dve.tensor_tensor(prob[:], prob[:], rsums[:].unsqueeze(2).to_broadcast([P, 4, NMEM]),
                                          ALU.mult).then_inc(prob_ready, 1)
                        dve.wait_ge(pT_hi_ready, n + 1)
                        dve.tensor_tensor(pT_lo[:].rearrange("p a c -> p (a c)"), banks(6),
                                          fp(pT_hi[:].rearrange("p a c -> p (a c)")), ALU.subtract
                                          ).then_inc(pT_lo_ready, 1)
                        dve.wait_ge(mo_hi_ready, n + 1)
                        dve.tensor_tensor(mo_lo[:, ln[half]], ps[:, 2, :], fp(mo_hi[:, ln[half]]), ALU.subtract
                                          ).then_inc(mo_lo_ready, 1)

                query(0)
                prep(u0 + 4)
                query(1)
                attend(0)
                prep(u0 + 5)
                query(2)
                attend(1)
                query(3)
                attend(2)
                attend(3)

                u0, f0, v0 = base["C", i]
                if i % 2 == 0:
                    dve.memset(cy[:, 0:2], 0.0).then_inc(conv_step, 1)
                    with dve.Fori(0, KB) as b:
                        dve.wait_ge(conv_step, b * 5 + 1)
                        for j, dst in enumerate((cb, cc, cu)):
                            prep(u0 + j + 2, b * 3)
                            for h in range(2):
                                if h == 0:
                                    dve.wait_ge(bank_full, b * 3 + (f0 + j + 1))
                                else:
                                    dve.wait_ge(w_used, b * 3 + (u0 + j + 1))
                                scaled(dst[:, ln[h]], 2 * j + h, h)
                        dve.wait_ge(evacuated, b * 6 + (v0 + 6))
                        dve.tensor_tensor(cy[:, 2:], cu[:], cc[:], ALU.mult).then_inc(conv_step, 1)
                        dve.wait_ge(conv_step, b * 5 + 2)
                        dve.tensor_scalar(cz[:], cy[:, 2:], taps[:, 2, bass.ds(b, 1)], None, ALU.mult
                                          ).then_inc(conv_step, 1)
                        for j in (1, 0):
                            dve.wait_ge(conv_step, b * 5 + (4 - j))
                            dve.scalar_tensor_tensor(cz[:], cy[:, j:j + SEQ], taps[:, j, bass.ds(b, 1)], cz[:],
                                                     ALU.mult, ALU.add).then_inc(conv_step, 1)
                        dve.wait_ge(conv_step, b * 5 + 5)
                        dve.tensor_tensor(cz[:], cz[:], cb[:], ALU.mult).then_inc(conv_step, 1)
                        dve.wait_ge(cm_hi_ready, b + 1)
                        dve.tensor_tensor(cm_lo[:], cz[:], fp(cm_hi[:]), ALU.subtract).then_inc(cm_lo_ready, 1)
                        dve.wait_ge(cm_lo_ready, b + 1)
                else:
                    def scan(row, par, r, t):
                        n = 2 * P * (t + 1)
                        dve.wait_ge(keep_ready, row + 1)
                        k = keep[:, par, r, 0:n][:, ::-1]
                        dve.tensor_tensor_scan(k, k, k, 1.0, ALU.mult, ALU.bypass).then_inc(scanned, 1)

                    def project(hp, to, piece):
                        if piece < 6:
                            part, h = piece // 2, piece % 2
                            if h == 0:
                                dve.wait_ge(bank_full, hp * 3 + (f0 + part + 1))
                                if part > 0:
                                    dve.wait_ge(sqk_lo_ready, hp * 2 + part)
                            else:
                                dve.wait_ge(w_used, hp * 3 + (u0 + part + 1))
                            if part == 0:
                                dve.scalar_tensor_tensor(tf[:, ln[h]], ps[:, 7, :], float(SHEAD) ** -0.5,
                                                         R[:, ln[h]], ALU.mult, ALU.mult).then_inc(evacuated, 1)
                            else:
                                scaled(tf[:, ln[h]], 7, h)
                        if piece in (1, 3):
                            hi, lo = ((sq_hi, sq_lo), (sk_hi, sk_lo))[piece // 2]
                            dve.wait_ge(sqk_hi_ready, hp * 2 + (piece // 2 + 1))
                            dve.tensor_tensor(lo[:, to, :], tf[:], fp(hi[:, to, :]), ALU.subtract
                                              ).then_inc(sqk_lo_ready, 1)
                        if piece >= 6:
                            blocks = slice(4 * (piece - 6), 4 * (piece - 5))
                            dve.wait_ge(vT_hi_ready, hp * 2 + (piece - 5))
                            dve.tensor_tensor(sv[:, to, blocks, :, SHEAD:], ps[:, 7, :].rearrange(
                                "p (b h c) -> p b h c", b=4, h=2), fp(sv[:, to, blocks, :, 0:SHEAD]), ALU.subtract
                                              ).then_inc(vT_lo_ready, 1)

                    def pair(hp, par, last, first=False):
                        for it in range(ITEMS):
                            t, hh = it % 4, it // 4
                            if not last and it % 2 == 1 and it < 6:
                                prep(u0 + 3 + 2 + it // 2, hp * 3)
                            if not (last and it == ITEMS - 1):
                                for r in range(2):
                                    scan(hp * ROWS + (2 * (it + 1) + r), (it + 1) % 2, r, (it + 1) % 4)
                            if not last:
                                project(hp + 1, 1 - par, it)
                            for c in range(t + 1):
                                n = CHUNKS_BEFORE[it] + c
                                dve.wait_ge(aT_hi_ready, hp * CHUNKS + (n + 1))
                                dve.tensor_tensor(aT_lo[:, n % 2].rearrange("p a c -> p (a c)"), ps[:, 4 + n % 2, :],
                                                  fp(aT_hi[:, n % 2].rearrange("p a c -> p (a c)")), ALU.subtract
                                                  ).then_inc(aT_lo_ready, 1)
                            rows = slice(hh * SHEAD, (hh + 1) * SHEAD)
                            dve.wait_ge(o_low_ready, hp * ITEMS + (it + 1))
                            if not (first and it == 0):
                                dve.wait_ge(so_lo_ready, hp * ITEMS + it)
                            dve.tensor_tensor(o_sum[rows, :], ps[0:SHEAD, 6, 0:2 * P], o_low[rows, :], ALU.add
                                              ).then_inc(o_sum_ready, 1)
                            dve.wait_ge(so_hi_ready, hp * ITEMS + (it + 1))
                            dve.tensor_tensor(so_lo[rows, it % 2, :], o_sum[rows, :], fp(so_hi[rows, it % 2, :]),
                                              ALU.subtract).then_inc(so_lo_ready, 1)

                    for piece in range(ITEMS):
                        if piece % 2 == 1 and piece < 6:
                            prep(u0 + 2 + piece // 2)
                        project(0, 0, piece)
                    for r in range(2):
                        scan(r, 0, r, 0)
                    pair(0, 0, False, first=True)
                    with dve.Fori(0, KB // 2 - 1) as d:
                        pair(d * 2 + 1, 1, False)
                        pair(d * 2 + 2, 0, False)
                    pair(KB - 1, 1, True)

                u0, f0, v0 = base["E", i]
                if i % 2 == 1:
                    dve.wait_ge(x_back, 16)
                with dve.Fori(0, KB // 2) as pm:
                    for j in range(3):
                        prep(u0 + j + 2, pm * 3)
                    for j in range(4):
                        if j < 3:
                            dve.wait_ge(bank_full, pm * 3 + (f0 + j + 1))
                        else:
                            dve.wait_ge(w_used, pm * 3 + (u0 + 3))
                        xs = x[:, bass.ds(pm * 2 + j // 2, 1), ln[j % 2]].rearrange("p a c -> p (a c)")
                        dve.tensor_tensor(xs, xs, ps[:, j, :], ALU.add).then_inc(evacuated, 1)

                u0, f0, v0 = base["F", i]
                nu, a0 = 2 * i + 1, FBLK * i
                for m, h in split_order(nu):
                    split(nu, m, h)
                norm(nu, u0, v0)

                def fill(dst, blk, f, u, b0):
                    for h in range(2):
                        if h == 0:
                            dve.wait_ge(bank_full, f)
                        else:
                            dve.wait_ge(w_used, u)
                        scaled(dst[:, blk, ln[h]], (b0 + h) % 8, h)

                def product(blk, blocks, visits):
                    dve.wait_ge(evacuated, visits)
                    dve.wait_ge(silu_done, blocks + (blk + 1))
                    dve.tensor_tensor(up[:, blk, :], gate[:, blk, :], up[:, blk, :], ALU.mult
                                      ).then_inc(prod_ready, 1)
                    dve.wait_ge(act_hi_ready, blocks + (blk + 1))
                    dve.tensor_tensor(act_lo[:, blk, :], up[:, blk, :], fp(act_hi[:, blk, :]), ALU.subtract
                                      ).then_inc(act_lo_ready, 1)

                def down(f, u, v, j0, after=None):
                    dve.wait_ge(evacuated, v)
                    for n in range(2 * KB):
                        m, h = n // 2, n % 2
                        if n < 2 * KB - 1:
                            dve.wait_ge(bank_full, f + (n + 1))
                        else:
                            dve.wait_ge(w_used, u)
                        dve.tensor_tensor(x[:, m, ln[h]], x[:, m, ln[h]], ps[:, (j0 + n) % 8, :], ALU.add
                                          ).then_inc(evacuated, 1)
                        if after and h == 1 and m > 0:
                            after(m - 1)
                    if after:
                        after(KB - 1)

                fill(gate, 0, f0 + 1, u0 + 1, 0)
                fill(gate, 1, f0 + 2, u0 + 2, 2)
                prep(u0 + 4)
                fill(up, 0, f0 + 3, u0 + 3, 6)
                prep(u0 + 5)
                fill(up, 1, f0 + 4, u0 + 4, 0)
                product(0, a0, v0 + 6)
                product(1, a0, v0 + 8)
                with dve.Fori(0, FGROUPS - 1) as g:
                    n, f, v, b = u0 + 4, g * 19 + (f0 + 4), g * 24 + (v0 + 8), g * 2 + (a0 + 2)
                    more = g * 6
                    dve.wait_ge(act_lo_ready, b)
                    prep(n + 2, more)
                    fill(gate, 0, f + 1, more + (n + 1), 2)
                    prep(n + 3, more)
                    fill(gate, 1, f + 2, more + (n + 2), 4)
                    prep(n + 4, more)
                    down(f + 2, more + (n + 4), v + 4, 6)
                    prep(n + 5, more)
                    prep(n + 6, more)
                    fill(up, 0, f + 18, more + (n + 5), 22)
                    prep(n + 7, more)
                    fill(up, 1, f + 19, more + (n + 6), 24)
                    product(0, b, v + 22)
                    product(1, b, v + 24)
                ue, fe, ve = base["end", i]
                prep(ue)
                if i + 1 < LAYERS:
                    down(fe - 15, ue, ve - 16, 2, after=lambda m: [split(nu + 1, m, h) for h in range(2)])
                    prep(ue + 1)
                else:
                    down(fe - 15, ue, ve - 16, 2)

        @block.tensor
        def _(pe):
            def three(out, whi, wlo, mhi, mlo, start, stop):
                pe.matmul(out, whi, mhi, start=start, stop=False)
                pe.matmul(out, whi, mlo, start=False, stop=False)
                return pe.matmul(out, wlo, mhi, start=False, stop=stop)

            def unit(u, more, bank_of, waits, full, first=None):
                s = u % WSLOTS
                pe.wait_ge(w_lo_ready, more + (u + 1))
                for h in range(2):
                    if waits[h] is not None:
                        pe.wait_ge(evacuated, waits[h])
                    for k in range(KB):
                        if first is not None:
                            pe.wait_ge(xg_lo_ready, split_count(first, k, h))
                        c = slice(k * P, (k + 1) * P)
                        last = three(ps[:, bank_of(h), :], w_hi[:, s, c], w_lo[:, s, c],
                                     xg_hi[:, k, ln[h]], xg_lo[:, k, ln[h]], k == 0, k == KB - 1)
                    last.then_inc(bank_full if h == 0 else w_used, 1)

            def norm(nu):
                pe.wait_ge(acc_added, KB * (nu + 1))
                for h in range(2):
                    pe.matmul(ps[:, 4 + h, :], mean_all[:], acc[:, ln[h]], start=True, stop=True
                              ).then_inc(stat_full, 1)

            pe.wait_ge(consts_made, 4)
            pe.wait_ge(msq_ready, 1)
            for k in range(KB):
                last = pe.matmul(ps[:, 4, 0:NMEM], mean_all[:], msq[:, k, :], start=(k == 0), stop=(k == KB - 1))
            last.then_inc(mstat_full, 1)
            for i in range(LAYERS):
                u0, f0, v0 = base["A", i]
                if i > 0:
                    pe.wait_ge(evacuated, v0)
                for n in range(MHEADS):
                    u = u0 + n
                    s = u % WSLOTS
                    pe.wait_ge(w_lo_ready, u + 1)
                    for k in range(KB):
                        if n == 0:
                            pe.wait_ge(mg_lo_ready, KB * i + k + 1)
                        c = slice(k * P, (k + 1) * P)
                        last = three(ps[:, n, 0:NMEM], w_hi[:, s, c], w_lo[:, s, c], mg_hi[:, k, :], mg_lo[:, k, :],
                                     k == 0, k == KB - 1)
                    last.then_inc(w_used, 1)
                for n in range(MHEADS):
                    u = u0 + MHEADS + n
                    s = u % WSLOTS
                    pe.wait_ge(w_lo_ready, u + 1)
                    if n >= 2:
                        pe.wait_ge(evacuated, v0 + MHEADS + n - 1)
                    for mb in range(2):
                        tok = slice(mb * P, (mb + 1) * P)
                        for k in range(KB):
                            c = slice(k * P, (k + 1) * P)
                            last = three(ps[:, 6 + n % 2, tok], mg_hi[:, k, tok], mg_lo[:, k, tok],
                                         w_hi[:, s, c], w_lo[:, s, c], k == 0, k == KB - 1)
                    last.then_inc(w_used, 1)
                pe.wait_ge(ksq_ready, i + 1)
                pe.wait_ge(mroot_ready, 1)
                if i > 0:
                    pe.wait_ge(kroot_ready, i)
                for h in range(2):
                    pe.matmul(ps[:, 4 + h, :], mean_head[:], ksq[:, ln[h]], start=True, stop=True
                              ).then_inc(kstat_full, 1)

            for i in range(LAYERS):
                u0, f0, v0 = base["B", i]
                pe.wait_ge(evacuated, v0)
                if i == 0:
                    pe.wait_ge(kroot_ready, LAYERS)

                def qstat(h):
                    hd = MHEADS * i + h
                    pe.wait_ge(qsq_ready, hd + 1)
                    if hd > 0:
                        pe.wait_ge(rqv_ready, hd)
                    for b in range(KB):
                        last = pe.matmul(ps[:, 3, b:b + 1], qsq[:, b * P:(b + 1) * P], mean_head[:, 0:1],
                                         start=True, stop=True)
                    last.then_inc(qstat_full, 1)

                def scores(n):
                    h, half, g = n // 2, n % 2, 8 * i + n
                    pe.wait_ge(q_lo_ready, MHEADS * i + h + 1)
                    if n == 0:
                        pe.wait_ge(kv_loaded, 64 * (i + 1))
                        pe.wait_ge(root_ready, 2 * i + 1)
                    else:
                        pe.wait_ge(exp_done, 4 * g)
                    ks = slice(h * NMEM, (h + 1) * NMEM)
                    for j in range(4):
                        tok = slice((4 * half + j) * P, (4 * half + j + 1) * P)
                        last = three(banks(4)[:, j * NMEM:(j + 1) * NMEM], q_hi[:, h % 2, tok], q_lo[:, h % 2, tok],
                                     k_hi[:, ks], k_lo[:, ks], True, True)
                    last.then_inc(scores_full, 1)

                def batch(n):
                    h, g = n // 2, 8 * i + n
                    pe.wait_ge(prob_ready, g + 1)
                    if n == 0:
                        pe.wait_ge(evacuated, v0 + 4)
                    else:
                        pe.wait_ge(pT_lo_ready, g)
                    for mb in range(2):
                        for j in range(4):
                            last = pe.transpose(ps[:, 6 + mb, j * P:(j + 1) * P],
                                                prob[:, j, mb * P:(mb + 1) * P], ident[:])
                    last.then_inc(pT_full, 1)
                    if n < 7:
                        scores(n + 1)
                    pe.wait_ge(pT_lo_ready, g + 1)
                    if g > 0:
                        pe.wait_ge(mo_lo_ready, g)
                    for mb in range(2):
                        hs = slice(h * P, (h + 1) * P)
                        last = three(ps[:, 2, :], v_hi[:, mb, hs], v_lo[:, mb, hs], pT_hi[:, mb, :], pT_lo[:, mb, :],
                                     mb == 0, mb == 1)
                    last.then_inc(mo_full, 1)

                unit(u0, 0, lambda h: h, (None, None), None, first=2 * i)
                unit(u0 + 1, 0, lambda h: 6 + h, (None, None), None)
                norm(2 * i)
                qstat(0)
                scores(0)
                qstat(1)
                unit(u0 + 2, 0, lambda h: h, (v0 + 1, v0 + 2), None)
                batch(0)
                batch(1)
                qstat(2)
                unit(u0 + 3, 0, lambda h: h, (v0 + 5, v0 + 6), None)
                batch(2)
                batch(3)
                qstat(3)
                for n in range(4, 8):
                    batch(n)

                u0, f0, v0 = base["C", i]
                pe.wait_ge(evacuated, v0)
                pe.wait_ge(mo_lo_ready, 8 * (i + 1))
                if i % 2 == 0:
                    with pe.Fori(0, KB) as b:
                        for j in range(3):
                            v = b * 6 + (v0 + 2 * j - 5)
                            unit(u0 + j, b * 3, lambda h: 2 * j + h, (v, v + 1), None)
                else:
                    def z(row, par, p0, r, t, first):
                        if not first:
                            pe.wait_ge(sig_ready, row - 1)
                        hd = slice(p0, p0 + SHEAD)
                        q = slice((2 * t + r) * P, (2 * t + r + 1) * P)
                        n = 2 * P * (t + 1)
                        for c in range(0, n, HALF):
                            w = min(HALF, n - c)
                            o = ps[:, 2 * r + c // HALF, :]
                            final = c + w == n
                            three(o[:, 0:w], sq_hi[hd, par, q], sq_lo[hd, par, q],
                                  sk_hi[hd, par, c:c + w], sk_lo[hd, par, c:c + w], True, not final)
                        m = (2 - r) * P
                        pe.matmul(o[:, w - m:w], ident_r[:], mask_r[:, 0:m], start=False, stop=True
                                  ).then_inc(z_full, 1)

                    def project(hp, piece, first=False):
                        if piece < 6:
                            part, h = piece // 2, piece % 2
                            s = (u0 + part) % WSLOTS
                            if h == 0:
                                pe.wait_ge(w_lo_ready, hp * 3 + (u0 + part + 1))
                            pe.wait_ge(evacuated, hp * 6 + (v0 + piece))
                            if piece == 0 and not first:
                                pe.wait_ge(vT_lo_ready, hp * 2)
                            for k in range(KB):
                                c = slice(k * P, (k + 1) * P)
                                last = three(ps[:, 7, :], w_hi[:, s, c], w_lo[:, s, c],
                                             xg_hi[:, k, ln[h]], xg_lo[:, k, ln[h]], k == 0, k == KB - 1)
                            last.then_inc(bank_full if h == 0 else w_used, 1)
                        else:
                            pe.wait_ge(evacuated, hp * 6 + (v0 + 6))
                            if piece == 7:
                                pe.wait_ge(vT_lo_ready, hp * 2 + 1)
                            for b in range(4):
                                tok = slice((4 * (piece - 6) + b) * P, (4 * (piece - 6) + b + 1) * P)
                                last = pe.transpose(ps[:, 7, b * P:(b + 1) * P], tf[:, tok], ident[:])
                            last.then_inc(vT_full, 1)

                    def turn(hp, it, c, par, first):
                        n = CHUNKS_BEFORE[it] + c
                        if c == 0:
                            pe.wait_ge(a_ready, hp * ROWS + (2 * it + 2))
                        if not (first and n < 2):
                            pe.wait_ge(aT_lo_ready, hp * CHUNKS + (n - 1))
                        for kk in range(2):
                            for r in range(2):
                                k = 2 * c + kk
                                last = pe.transpose(ps[:, 4 + n % 2, (2 * kk + r) * P:(2 * kk + r + 1) * P],
                                                    sig[:, it % 2, r, k * P:(k + 1) * P], ident[:])
                        last.then_inc(aT_full, 1)

                    def weighted(hp, it, c, par, first):
                        n, t = CHUNKS_BEFORE[it] + c, it % 4
                        pe.wait_ge(aT_lo_ready, hp * CHUNKS + (n + 1))
                        if c == 0 and not (first and it == 0):
                            pe.wait_ge(o_sum_ready, hp * ITEMS + it)
                        for kk in range(2):
                            v = sv[:, par, 2 * c + kk, it // 4, :]
                            o = ps[:, 6, 0:2 * P]
                            pe.matmul(o, v, aT_hi[:, n % 2, kk, :], start=(c == 0 and kk == 0), stop=False)
                            last = pe.matmul(o, v, aT_lo[:, n % 2, kk, :], start=False, stop=(c == t and kk == 1))
                        last.then_inc(pv_done, 1)

                    def pair(hp, par, last, first=False):
                        for it in range(ITEMS):
                            t = it % 4
                            if it < ITEMS - 1:
                                for r in range(2):
                                    z(hp * ROWS + (2 * (it + 1) + r), par, (it + 1) // 4 * SHEAD, r, (it + 1) % 4,
                                      False)
                            elif not last:
                                pe.wait_ge(sqk_lo_ready, hp * 2 + 4)
                                for r in range(2):
                                    z(hp * ROWS + (ROWS + r), 1 - par, 0, r, 0, False)
                            if not last:
                                project(hp + 1, it)
                            if it == 0:
                                pe.wait_ge(vT_lo_ready, hp * 2 + 2)
                            turn(hp, it, 0, par, first)
                            for c in range(t + 1):
                                if c < t:
                                    turn(hp, it, c + 1, par, first)
                                weighted(hp, it, c, par, first)

                    for piece in range(ITEMS):
                        project(0, piece, first=True)
                    pe.wait_ge(sqk_lo_ready, 2)
                    for r in range(2):
                        z(r, 0, 0, r, 0, True)
                    pair(0, 0, False, first=True)
                    with pe.Fori(0, KB // 2 - 1) as d:
                        pair(d * 2 + 1, 1, False)
                        pair(d * 2 + 2, 0, False)
                    pair(KB - 1, 1, True)

                u0, f0, v0 = base["E", i]
                pe.wait_ge(evacuated, v0)
                pe.wait_ge(e_early, 64 * (i + 1))
                pe.wait_ge(e_late, 32 * (i + 1))
                with pe.Fori(0, KB // 2) as pm:
                    for a in range(2):
                        s = (u0 + a) % WSLOTS
                        pe.wait_ge(w_lo_ready, pm * 3 + (u0 + a + 1))
                        for h in range(2):
                            pe.wait_ge(evacuated, pm * 4 + (v0 + 2 * a + h - 3))
                            for k in range(KB):
                                c = slice(k * P, (k + 1) * P)
                                last = three(ps[:, 2 * a + h, :], w_hi[:, s, c], w_lo[:, s, c],
                                             xg_hi[:, k, ln[h]], xg_lo[:, k, ln[h]], k == 0, False)
                        last.then_inc(w_used, 1)
                    s = (u0 + 2) % WSLOTS
                    pe.wait_ge(w_lo_ready, pm * 3 + (u0 + 3))
                    for a in range(2):
                        for h in range(2):
                            for k in range(MHEADS):
                                c = slice((2 * k + a) * P, (2 * k + a + 1) * P)
                                last = three(ps[:, 2 * a + h, :], w_hi[:, s, c], w_lo[:, s, c],
                                             me_hi[:, k, ln[h]], me_lo[:, k, ln[h]], False, k == MHEADS - 1)
                            last.then_inc(w_used if a == 1 and h == 1 else bank_full, 1)

                u0, f0, v0 = base["F", i]
                pe.wait_ge(evacuated, v0)

                def down(n, more, blocks, v, j0):
                    for j in range(2):
                        pe.wait_ge(w_lo_ready, more + (n + j + 1))
                    pe.wait_ge(act_lo_ready, blocks)
                    for q in range(2 * KB):
                        m, h = q // 2, q % 2
                        pe.wait_ge(evacuated, v + (q - 5))
                        for j in range(2):
                            s, c = (n + j) % WSLOTS, slice(m * P, (m + 1) * P)
                            last = three(ps[:, (j0 + q) % 8, :], w_hi[:, s, c], w_lo[:, s, c],
                                         act_hi[:, j, ln[h]], act_lo[:, j, ln[h]], j == 0, j == 1)
                        if q < 2 * KB - 1:
                            last.then_inc(bank_full, 1)
                        else:
                            last.then_inc(w_used, 2)

                unit(u0, 0, lambda h: h, (None, None), None, first=2 * i + 1)
                unit(u0 + 1, 0, lambda h: 2 + h, (None, None), None)
                norm(2 * i + 1)
                unit(u0 + 2, 0, lambda h: 6 + h, (None, None), None)
                unit(u0 + 3, 0, lambda h: h, (v0 + 1, v0 + 2), None)
                with pe.Fori(0, FGROUPS - 1) as g:
                    n, more, v = u0 + 4, g * 6, g * 24 + (v0 + 8)
                    unit(n, more, lambda h: 2 + h, (v - 5, v - 4), None)
                    unit(n + 1, more, lambda h: 4 + h, (v - 3, v - 2), None)
                    down(n + 2, more, g * 2 + (FBLK * i + 2), v + 4, 6)
                    unit(n + 4, more, lambda h: (22 + h) % 8, (v + 15, v + 16), None)
                    unit(n + 5, more, lambda h: (24 + h) % 8, (v + 17, v + 18), None)
                ue, fe, ve = base["end", i]
                down(ue - 2, 0, FBLK * (i + 1), ve - 16, 2)


def kernel(x, mem, w_in, w_out, w_mem_kv, w_conv, w_ffn_in, w_ffn_out, g_mix, g_mem, g_ffn, g_q, g_k):
    import concourse.bacc as bacc
    from concourse.bass_utils import run_bass_kernel_spmd

    def blocks(v):
        v = np.asarray(v)
        return np.ascontiguousarray(np.moveaxis(v.reshape(*v.shape[:-1], KB, P), -1, 0))

    weights = [np.asarray(w) for w in (w_in, w_out, w_mem_kv, w_ffn_in, w_ffn_out)]
    arrays = {
        "xT": np.ascontiguousarray(np.asarray(x)[0].reshape(SEQ, KB, P).transpose(2, 1, 0)),
        "memT": np.ascontiguousarray(np.asarray(mem)[0].reshape(NMEM, KB, P).transpose(2, 1, 0)),
        "wpack": pack_weights(*weights),
        "gain": blocks(np.stack([np.asarray(g) for g in (g_mix, g_mem, g_ffn)])),
        "taps": blocks(np.asarray(w_conv)[0]),
        "g_heads": np.ascontiguousarray(np.stack([np.asarray(g_q), np.asarray(g_k)]).transpose(2, 0, 1)),
    }
    nc = bacc.Bacc("TRN2", target_bir_lowering=False, num_devices=1)
    ap = {n: nc.dram_tensor(n, a.shape, F32, kind="ExternalInput").ap() for n, a in arrays.items()}
    out = nc.dram_tensor("out", (P, KB, SEQ), F32, kind="ExternalOutput").ap()
    trunk(nc, ap["xT"], ap["memT"], ap["wpack"], [(n, ap[n]) for n in ("gain", "taps", "g_heads")], out)
    r = run_bass_kernel_spmd(nc, [arrays], core_ids=[0])
    got = np.asarray(r.results[0]["out"])
    return np.ascontiguousarray(got.transpose(2, 1, 0).reshape(1, SEQ, DM))
```

```python
from contextlib import ExitStack

import numpy as np

import concourse.bass as bass
from concourse import mybir

F32 = mybir.dt.float32
F32R = mybir.dt.float32r
ALU = mybir.AluOpType
ACT = mybir.ActivationFunctionType
AX_X = mybir.AxisListType.X

P = 128
SEQ, DM, LAYERS = 1024, 1024, 2
KB = DM // P
HALF = 512
NMEM, MHEADS = 256, 4
SHEAD = 64
FF = 2816
FBLK = FF // P
FGROUPS = FBLK // 2
EPS = 1e-6
UCOLS = KB * P
WSLOTS = 3
MASKED = -1.0e30

A_UNITS = 2 * MHEADS
B_UNITS = MHEADS
C_UNITS = 3 * KB
E_UNITS = 3 * (KB // 2)
F_UNITS = 6 * FGROUPS
LAYER_UNITS = B_UNITS + C_UNITS + E_UNITS + F_UNITS
UNITS = LAYERS * (A_UNITS + LAYER_UNITS)


def pack_weights(w_in, w_out, w_mem_kv, w_ffn_in, w_ffn_out):
    def cols(w, c0, k0=0, kn=KB, n=P):
        return w[k0 * P:(k0 + kn) * P, c0:c0 + n].reshape(kn, P, n).transpose(1, 0, 2).reshape(P, kn * n)

    units = []
    for i in range(LAYERS):
        units += [cols(w_mem_kv[i], c * P) for c in range(A_UNITS)]
    for i in range(LAYERS):
        units += [cols(w_in[i], 3 * DM + h * P) for h in range(MHEADS)]
        for b in range(KB):
            units += [cols(w_in[i], part * DM + b * P) for part in range(3)]
        for m in range(0, KB, 2):
            units += [cols(w_out[i], m * P), cols(w_out[i], (m + 1) * P),
                      cols(w_out[i], m * P, KB, MHEADS, 2 * P)]

        def gate_up(g, part):
            return [cols(w_ffn_in[i], part * FF + (2 * g + j) * P) for j in range(2)]

        units += gate_up(0, 0) + gate_up(0, 1)
        for g in range(1, FGROUPS):
            units += gate_up(g, 0)
            units += [w_ffn_out[i, (2 * (g - 1) + j) * P:(2 * (g - 1) + j + 1) * P] for j in range(2)]
            units += gate_up(g, 1)
        units += [w_ffn_out[i, (FBLK - 2 + j) * P:(FBLK - 1 + j) * P] for j in range(2)]
    return np.ascontiguousarray(np.stack(units))


def trunk(nc, xT, memT, wpack, vectors, out):
    base = {}
    u = f = v = 0
    for i in range(LAYERS):
        base["A", i] = (u, f, v)
        u, v = u + A_UNITS, v + A_UNITS
    for i in range(LAYERS):
        base["B", i] = (u, f, v)
        u, f, v = u + B_UNITS, f + B_UNITS, v + 2 * B_UNITS
        base["C", i] = (u, f, v)
        u, f, v = u + C_UNITS, f + C_UNITS, v + 2 * C_UNITS
        base["E", i] = (u, f, v)
        u, f, v = u + E_UNITS, f + 3 * (KB // 2), v + 2 * KB
        base["F", i] = (u, f, v)
        u, f, v = u + F_UNITS, f + 4 * FGROUPS + 15 * FGROUPS, v + 24 * FGROUPS
        base["end", i] = (u, f, v)
    assert u == UNITS and u % WSLOTS == 0

    with ExitStack() as ctx:
        arena_bytes = (nc.sbuf_usable_end - nc.sbuf_base) // 32 * 32 - 64
        arena = ctx.enter_context(nc.sbuf_tensor("arena", [P, arena_bytes // 4], F32))
        arena_start = (nc.sbuf_base - arena_bytes)
        cursor = [0]

        def place(name, shape, dt, offset=None):
            size = 4 * int(np.prod(shape[1:]))
            if offset is None:
                offset = cursor[0]
                cursor[0] += (size + 31) // 32 * 32
            assert offset + size <= arena_bytes, (name, offset, size, arena_bytes)
            return nc.alloc_sbuf_tensor_at(name, shape, dt, offset=arena_start + offset)

        def sem(name):
            return ctx.enter_context(nc.semaphore(name))

        x = place("x", [P, KB, SEQ], F32)
        xg_hi = place("xg_hi", [P, KB, SEQ], F32R)
        xg_lo = place("xg_lo", [P, KB, SEQ], F32R)
        raw = place("raw", [P, WSLOTS, UCOLS], F32)
        w_hi = place("w_hi", [P, WSLOTS, UCOLS], F32R)
        w_lo = place("w_lo", [P, WSLOTS, UCOLS], F32R)
        R = place("R", [P, SEQ], F32)
        ident = place("ident", [P, P], F32)
        ident_r = place("ident_r", [P, P], F32R)
        mask_r = place("mask_r", [P, 2 * P], F32R)
        mean_all = place("mean_all", [P, P], F32)
        mean_head = place("mean_head", [P, P], F32)
        gain = place("gain", [P, 3, LAYERS, KB], F32)
        taps = place("taps", [P, 3, KB], F32)
        g_heads = place("g_heads", [P, 2, LAYERS], F32)
        g_qk = place("g_qk", [P, LAYERS], F32)
        eps = place("eps", [P, 1], F32)
        smax = place("smax", [P, 2, 2], F32)
        nbias = place("nbias", [P, 2, 2], F32)
        psums = place("psums", [P, 2, 2], F32)
        rsums = place("rsums", [P, 2, 2], F32)
        mcol = place("mcol", [P, 2], F32)
        mcol_t = place("mcol_t", [P, 2], F32)
        rq_v = place("rq_v", [P, KB], F32)
        rq_s = place("rq_s", [P, KB], F32)
        rq_t = place("rq_t", [P, KB], F32)
        rq = place("rq", [P, 2, KB], F32)
        Z = cursor[0]
        K1 = 1024
        sq = place("sq", [P, 2, SEQ], F32, Z + 48 * K1)
        acc = place("acc", [P, SEQ], F32, Z + 56 * K1)
        rtmp = place("rtmp", [P, SEQ], F32, Z + 60 * K1)
        mem = place("mem", [P, KB, NMEM], F32, Z)
        mg_hi = [place("mg_hi0", [P, KB, NMEM], F32R, Z + 8 * K1), place("mg_hi1", [P, KB, NMEM], F32R, 32 * K1)]
        mg_lo = [place("mg_lo0", [P, KB, NMEM], F32R, Z + 16 * K1), place("mg_lo1", [P, KB, NMEM], F32R, 40 * K1)]
        kf = place("kf", [P, MHEADS * NMEM], F32, Z + 24 * K1)
        ksq = place("ksq", [P, MHEADS * NMEM], F32, Z + 28 * K1)
        kr = place("kr", [P, MHEADS * NMEM], F32, Z + 32 * K1)
        kn = place("kn", [P, MHEADS * NMEM], F32, Z + 36 * K1)
        ka_hi = place("ka_hi", [P, MHEADS * NMEM], F32R, Z + 40 * K1)
        ka_lo = place("ka_lo", [P, MHEADS * NMEM], F32R, Z + 44 * K1)
        va_hi = place("va_hi", [P, 2, MHEADS * P], F32R, Z + 48 * K1)
        va_lo = place("va_lo", [P, 2, MHEADS * P], F32R, Z + 52 * K1)
        msq = place("msq", [P, KB, NMEM], F32, Z + 56 * K1)
        mr = place("mr", [P, NMEM], F32, Z + 64 * K1)
        mrt = place("mrt", [P, NMEM], F32, Z + 65 * K1)
        mask_f = place("mask_f", [P, 2 * P], F32, Z + 66 * K1)
        q_hi = place("q_hi", [P, 2, SEQ], F32R, Z)
        q_lo = place("q_lo", [P, 2, SEQ], F32R, Z + 8 * K1)
        k_hi = place("k_hi", [P, MHEADS * NMEM], F32R, Z + 16 * K1)
        k_lo = place("k_lo", [P, MHEADS * NMEM], F32R, Z + 20 * K1)
        v_hi = place("v_hi", [P, 2, MHEADS * P], F32R, Z + 24 * K1)
        v_lo = place("v_lo", [P, 2, MHEADS * P], F32R, Z + 28 * K1)
        pT_hi = place("pT_hi", [P, 2, 2, 2 * P], F32R, Z + 32 * K1)
        pT_lo = place("pT_lo", [P, 2, 2, 2 * P], F32R, Z + 36 * K1)
        qf = place("qf", [P, SEQ], F32, Z + 40 * K1)
        qsq = place("qsq", [P, SEQ], F32, Z + 44 * K1)
        ME = Z + 48 * K1 + 32
        me_f = place("me_f", [P, MHEADS, SEQ], F32, ME)
        prob = place("prob", [P, 2, 2, NMEM], F32, ME + 16 * K1)
        cb = place("cb", [P, SEQ], F32, Z)
        cc = place("cc", [P, SEQ], F32, Z + 4 * K1)
        cu = place("cu", [P, SEQ], F32, Z + 8 * K1)
        cy = place("cy", [P, SEQ + 2], F32, Z + 12 * K1)
        mix_f = place("mix_f", [P, KB, SEQ], F32, Z + 16 * K1 + 32)
        keep = place("keep", [P, 2, 2, SEQ], F32, 0)
        sig = place("sig", [P, 2, 2, SEQ], F32, 16 * K1)
        sq_hi = place("sq_hi", [P, 2, SEQ], F32R, Z)
        sq_lo = place("sq_lo", [P, 2, SEQ], F32R, Z + 8 * K1)
        sk_hi = place("sk_hi", [P, 2, SEQ], F32R, Z + 16 * K1)
        sk_lo = place("sk_lo", [P, 2, SEQ], F32R, Z + 24 * K1)
        sv = place("sv", [P, 2, KB, 2, P], F32R, Z + 32 * K1)
        aT_hi = place("aT_hi", [P, 2, 2, 2 * P], F32R, ME)
        aT_lo = place("aT_lo", [P, 2, 2, 2 * P], F32R, ME + 4 * K1)
        o_sum = place("o_sum", [P, 2, 2 * P], F32, ME + 8 * K1)
        o_low = place("o_low", [P, 2 * P], F32, ME + 10 * K1)
        tf = place("tf", [P, SEQ], F32, ME + 16 * K1)
        mx = place("mx", [P, KB, SEQ], F32, 64 * K1)
        me_hi = place("me_hi", [P, MHEADS, SEQ], F32R, Z)
        me_lo = place("me_lo", [P, MHEADS, SEQ], F32R, Z + 16 * K1 + 32)
        act_hi = place("act_hi", [P, 2, SEQ], F32R, Z)
        act_lo = place("act_lo", [P, 2, SEQ], F32R, Z + 8 * K1)
        gate = place("gate", [P, 2, SEQ], F32, Z + 16 * K1)
        up = place("up", [P, 2, SEQ], F32, Z + 24 * K1)

        ps = ctx.enter_context(nc.psum_tensor("ps", [P, 8, HALF], F32))

        def banks(b, n=2):
            return ps[:, b:b + n, :].rearrange("p a c -> p (a c)")

        d_kv = nc.dram_tensor("d_kv", (LAYERS, 4, P, MHEADS * NMEM), F32R, kind="Internal").ap()
        d_me = nc.dram_tensor("d_me", (P, MHEADS, SEQ), F32, kind="Internal").ap()
        d_mix = nc.dram_tensor("d_mix", (KB - 1, P, SEQ), F32, kind="Internal").ap()
        d_x = nc.dram_tensor("d_x", (P, KB, SEQ), F32, kind="Internal").ap()

        consts_in = sem("consts_in")
        x_in = sem("x_in")
        mem_in = sem("mem_in")
        consts_made = sem("consts_made")
        ident_steps = sem("ident_steps")
        raw_landed = [sem(f"raw_landed{s}") for s in range(WSLOTS)]
        w_hi_ready = sem("w_hi_ready")
        w_lo_ready = sem("w_lo_ready")
        w_used = sem("w_used")
        bank_full = sem("bank_full")
        evacuated = sem("evacuated")
        xg_hi_ready = sem("xg_hi_ready")
        xg_lo_ready = sem("xg_lo_ready")
        sq_ready = sem("sq_ready")
        acc_added = sem("acc_added")
        stat_full = sem("stat_full")
        root_ready = sem("root_ready")
        r_ready = sem("r_ready")
        eps_made = sem("eps_made")
        msq_ready = sem("msq_ready")
        mstat_full = sem("mstat_full")
        mroot_ready = sem("mroot_ready")
        mr_ready = sem("mr_ready")
        gqk_ready = sem("gqk_ready")
        mg_hi_ready = sem("mg_hi_ready")
        mg_lo_ready = sem("mg_lo_ready")
        ksq_ready = sem("ksq_ready")
        kstat_full = sem("kstat_full")
        kroot_ready = sem("kroot_ready")
        kr_ready = sem("kr_ready")
        kn_ready = sem("kn_ready")
        ka_hi_ready = sem("ka_hi_ready")
        ka_lo_ready = sem("ka_lo_ready")
        va_hi_ready = sem("va_hi_ready")
        kv_stored = sem("kv_stored")
        kv_loaded = sem("kv_loaded")
        q_hi_ready = sem("q_hi_ready")
        q_lo_ready = sem("q_lo_ready")
        qsq_ready = sem("qsq_ready")
        qstat_full = sem("qstat_full")
        rqv_ready = sem("rqv_ready")
        rqs_ready = sem("rqs_ready")
        rq_step = sem("rq_step")
        rq_ready = sem("rq_ready")
        scores_full = sem("scores_full")
        max_ready = sem("max_ready")
        nbias_ready = sem("nbias_ready")
        exp_done = sem("exp_done")
        rsum_ready = sem("rsum_ready")
        prob_ready = sem("prob_ready")
        pT_full = sem("pT_full")
        pT_hi_ready = sem("pT_hi_ready")
        pT_lo_ready = sem("pT_lo_ready")
        mo_full = sem("mo_full")
        mo_ready = sem("mo_ready")
        me_stored = sem("me_stored")
        conv_step = sem("conv_step")
        x_spilled = sem("x_spilled")
        x_back = sem("x_back")
        z_full = sem("z_full")
        keep_ready = sem("keep_ready")
        sig_ready = sem("sig_ready")
        scanned = sem("scanned")
        a_ready = sem("a_ready")
        aT_full = sem("aT_full")
        aT_hi_ready = sem("aT_hi_ready")
        aT_lo_ready = sem("aT_lo_ready")
        pv_done = sem("pv_done")
        o_low_ready = sem("o_low_ready")
        o_sum_ready = sem("o_sum_ready")
        so_stored = [sem(f"so_stored{p}") for p in range(2)]
        sqk_hi_ready = sem("sqk_hi_ready")
        sqk_lo_ready = sem("sqk_lo_ready")
        vT_full = sem("vT_full")
        vT_hi_ready = sem("vT_hi_ready")
        vT_lo_ready = sem("vT_lo_ready")
        mx_loaded = sem("mx_loaded")
        me_loaded = sem("me_loaded")
        mx_hi_ready = sem("mx_hi_ready")
        mx_lo_ready = sem("mx_lo_ready")
        me_hi_ready = sem("me_hi_ready")
        me_lo_ready = sem("me_lo_ready")
        silu_done = sem("silu_done")
        prod_ready = sem("prod_ready")
        act_hi_ready = sem("act_hi_ready")
        act_lo_ready = sem("act_lo_ready")
        out_stored = sem("out_stored")

        block = ctx.enter_context(nc.Block())

        def fp(ap):
            return ap.bitcast(F32)

        def x_visit(nu, m, h):
            if nu in (1, 3):
                return base["E", nu // 2][2] + 2 * m + h
            return base["end", 0][2] - 2 * KB + 2 * m + h

        def split_count(nu, m, h):
            return 2 * KB * nu + (2 * m + h if nu == 2 else KB * h + m) + 1

        def split_order(nu):
            return [(m, h) for m in range(KB) for h in range(2)] if nu == 2 else \
                   [(m, h) for h in range(2) for m in range(KB)]

        CHUNKS_BEFORE = [sum(j % 4 + 1 for j in range(it)) for it in range(9)]
        ITEMS, ROWS, CHUNKS = 8, 16, CHUNKS_BEFORE[8]
        FILL = [(3, 3), (2, 2, 2), (4, 1, 1, 1), (0, 2, 1, 1, 1), (3, 3), (2, 2, 2), (4, 2, 1, 1), (0, 4, 0, 0, 0)]
        assert sum(map(sum, FILL)) == 6 * KB
        ENDS = {}
        steps = 0
        for it, counts in enumerate(FILL):
            for place_, n in enumerate(counts):
                for piece in range(6):
                    if steps < KB * (piece + 1) <= steps + n:
                        ENDS[it, place_] = piece
                steps += n
        assert len(ENDS) == 6
        ln = slice(0, HALF), slice(HALF, SEQ)
        BATCHES = 4 * MHEADS

        @block.sync
        def _(sp):
            sp.dma_start(mem[:], memT).then_inc(mem_in, 16)
            for name, src in vectors:
                dst = {"gain": gain, "taps": taps, "g_heads": g_heads}[name]
                sp.dma_start(dst[:], src).then_inc(consts_in, 16)
            for s in range(WSLOTS):
                sp.dma_start(raw[:, s, :], wpack[s]).then_inc(raw_landed[s], 16)
            for h in range(2):
                sp.dma_start(x[:, :, ln[h]], xT[:, :, ln[h]]).then_inc(x_in, 16)
            with sp.Fori(1, UNITS // WSLOTS) as i:
                for s in range(WSLOTS):
                    sp.wait_ge(w_lo_ready, i * WSLOTS + (s + 1 - WSLOTS))
                    sp.dma_start(raw[:, s, :], wpack[bass.ds(i * WSLOTS + s, 1)].rearrange("a p c -> (a p) c")
                                 ).then_inc(raw_landed[s], 16)
            v_end = base["end", LAYERS - 1][2] - 2 * KB
            for m in range(KB):
                sp.wait_ge(evacuated, v_end + 2 * m + 2)
                sp.dma_start(out[:, m, :], x[:, m, :]).then_inc(out_stored, 16)
            sp.wait_ge(out_stored, 16 * KB)

        @block.gpsimd
        def _(pool):
            pool.memset(ident[:], 0.0).then_inc(ident_steps, 1)
            pool.memset(mask_f[:], MASKED).then_inc(ident_steps, 1)
            pool.memset(mean_all[:], 1.0 / DM).then_inc(consts_made, 1)
            pool.memset(mean_head[:], 1.0 / P).then_inc(consts_made, 1)
            pool.wait_ge(ident_steps, 2)
            pool.affine_select(out=ident[:], in_=ident[:], compare_op=ALU.not_equal, fill=1.0, base=0,
                               pattern=[[-1, P]], channel_multiplier=1).then_inc(ident_steps, 1)
            pool.affine_select(out=mask_f[:], in_=mask_f[:], compare_op=ALU.is_ge,
                               fill=0.0, base=0, pattern=[[1, 2 * P]], channel_multiplier=-1
                               ).then_inc(ident_steps, 1)

            for i in range(LAYERS):
                pool.wait_ge(ka_lo_ready, i + 1)
                pool.wait_ge(evacuated, base["A", i][2] + A_UNITS)
                for n, t in enumerate((ka_hi, ka_lo)):
                    pool.dma_start(d_kv[i, n], t[:]).then_inc(kv_stored, 16)
                for n, t in enumerate((va_hi, va_lo)):
                    pool.dma_start(d_kv[i, 2 + n], t[:].rearrange("p a c -> p (a c)")).then_inc(kv_stored, 16)
                pool.wait_ge(kv_stored, 64 * (i + 1))

            for i in range(LAYERS):
                if i > 0:
                    pool.wait_ge(evacuated, base["end", i - 1][2])
                for n, t in enumerate((k_hi, k_lo)):
                    pool.dma_start(t[:], d_kv[i, n]).then_inc(kv_loaded, 16)
                for n, t in enumerate((v_hi, v_lo)):
                    pool.dma_start(t[:].rearrange("p a c -> p (a c)"), d_kv[i, 2 + n]).then_inc(kv_loaded, 16)
                if i % 2 == 1:
                    pool.wait_ge(xg_lo_ready, 2 * KB * (2 * i + 1))
                    pool.wait_ge(acc_added, KB * (2 * i + 1))
                    pool.dma_start(d_x, x[:]).then_inc(x_spilled, 16)
                    for h in range(MHEADS):
                        pool.wait_ge(mo_ready, BATCHES * i + 4 * h + 4)
                        pool.dma_start(d_me[:, h, :], me_f[:, h, :]).then_inc(me_stored, 16)

                    def weigh(row, par, r, t):
                        n = 2 * P * (t + 1)
                        pool.wait_ge(scanned, row + 1)
                        pool.wait_ge(sig_ready, row + 1)
                        pool.tensor_tensor(sig[:, par, r, 0:n - 1], sig[:, par, r, 0:n - 1],
                                           keep[:, par, r, 1:n], ALU.mult).then_inc(a_ready, 1)

                    def pair(hp, last):
                        for it in range(ITEMS):
                            if not (last and it == ITEMS - 1):
                                for r in range(2):
                                    weigh(hp * ROWS + (2 * (it + 1) + r), (it + 1) % 2, r, (it + 1) % 4)
                            if not last:
                                rows = slice(it // 4 * SHEAD, (it // 4 + 1) * SHEAD)
                                toks = slice(it % 4 * 2 * P, (it % 4 + 1) * 2 * P)
                                pool.wait_ge(o_sum_ready, hp * ITEMS + (it + 1))
                                pool.dma_start(d_mix[bass.ds(hp, 1), rows, toks].rearrange("a p c -> (a p) c"),
                                               o_sum[rows, it % 2, :]).then_inc(so_stored[it % 2], 16)
                            elif it == 1:
                                for p in range(2):
                                    pool.wait_ge(so_stored[p], 16 * ITEMS // 2 * (KB - 1))
                                pool.wait_ge(w_used, base["E", i][0])
                                pool.dma_start(mx[:, 0:KB - 1, :], d_mix.rearrange("b p c -> p b c")
                                               ).then_inc(mx_loaded, 16)

                    for r in range(2):
                        weigh(r, 0, r, 0)
                    with pool.Fori(0, KB - 1) as hp:
                        pair(hp, False)
                    pair(KB - 1, True)

        @block.scalar
        def _(act):
            def prep(u, more=0, rounds=0):
                s = u % WSLOTS
                if u >= UNITS:
                    return
                act.wait_ge(raw_landed[s], rounds * 16 + (u // WSLOTS + 1) * 16)
                if u >= WSLOTS:
                    act.wait_ge(w_used, more + (u - WSLOTS + 1))
                act.activation(w_hi[:, s, :], raw[:, s, :], ACT.Copy).then_inc(w_hi_ready, 1)

            def split(nu, m, h):
                i, g = nu // 2, 2 * (nu % 2)
                if nu == 0:
                    act.wait_ge(x_in, 32)
                elif nu == 2:
                    act.wait_ge(evacuated, base["end", 0][2] - 2 * KB + 2 * m + h + 1)
                else:
                    act.wait_ge(evacuated, base["F", i][2])
                act.activation(xg_hi[:, m, ln[h]], x[:, m, ln[h]], ACT.Copy, scale=gain[:, g, i, m:m + 1]
                               ).then_inc(xg_hi_ready, 1)

            def squares_and_root(nu, u0):
                for m in range(KB):
                    n = KB * nu + m
                    if n >= 2:
                        act.wait_ge(acc_added, n - 1)
                    act.activation(sq[:, m % 2, :], x[:, m, :], ACT.Square).then_inc(sq_ready, 1)
                prep(u0 + 2)
                prep(u0 + 3)
                act.wait_ge(stat_full, 2 * nu + 2)
                act.activation(rtmp[:], banks(4), ACT.Sqrt, bias=eps[:, 0:1]).then_inc(root_ready, 1)

            act.wait_ge(ident_steps, 4)
            act.activation(ident_r[:], ident[:], ACT.Copy).then_inc(consts_made, 1)
            act.activation(mask_r[:], mask_f[:], ACT.Copy).then_inc(consts_made, 1)

            act.wait_ge(mem_in, 16)
            act.wait_ge(consts_in, 48)
            for m in range(KB):
                act.activation(mg_hi[0][:, m, :], mem[:, m, :], ACT.Copy, scale=gain[:, 1, 0, m:m + 1]
                               ).then_inc(mg_hi_ready, 1)
            prep(0)
            prep(1)
            act.activation(msq[:], mem[:], ACT.Square).then_inc(msq_ready, 1)
            prep(2)
            act.wait_ge(mstat_full, 1)
            act.wait_ge(eps_made, 1)
            act.activation(mrt[:], ps[:, 4, 0:NMEM], ACT.Sqrt, bias=eps[:, 0:1]).then_inc(mroot_ready, 1)
            act.activation(mcol_t[:], ps[:, 5, 0:2], ACT.Sqrt, bias=eps[:, 0:1]).then_inc(mroot_ready, 1)
            for m in range(KB):
                act.activation(mg_hi[1][:, m, :], mem[:, m, :], ACT.Copy, scale=gain[:, 1, 1, m:m + 1]
                               ).then_inc(mg_hi_ready, 1)
            act.wait_ge(mr_ready, 2)
            for i in range(LAYERS):
                u0, f0, v0 = base["A", i]
                for n in range(MHEADS):
                    if i > 0 or n > 0:
                        prep(u0 + n + 2)
                act.wait_ge(evacuated, v0 + MHEADS)
                act.activation(ksq[:], kf[:], ACT.Square).then_inc(ksq_ready, 1)
                for n in range(MHEADS):
                    prep(u0 + MHEADS + n + 2)
                    act.wait_ge(w_used, u0 + MHEADS + n + 1)
                    if i > 0:
                        act.wait_ge(kv_stored, 64 * i)
                    for mb in range(2):
                        act.activation(va_hi[:, mb, n * P:(n + 1) * P], ps[:, 6 + n % 2, mb * P:(mb + 1) * P],
                                       ACT.Copy, scale=mcol[:, mb:mb + 1]).then_inc(va_hi_ready, 1)
                act.wait_ge(kstat_full, 2 * (i + 1))
                act.activation(kr[:], banks(4), ACT.Sqrt, bias=eps[:, 0:1]).then_inc(kroot_ready, 1)
                act.wait_ge(kn_ready, i + 1)
                act.activation(ka_hi[:], kn[:], ACT.Copy).then_inc(ka_hi_ready, 1)
            act.wait_ge(w_used, base["B", 0][0])
            for m, h in split_order(0):
                split(0, m, h)

            for i in range(LAYERS):
                u0, f0, v0 = base["B", i]
                if i == 0:
                    act.wait_ge(kv_stored, 64 * LAYERS)
                squares_and_root(2 * i, u0)

                def query(h):
                    hd = MHEADS * i + h
                    act.wait_ge(evacuated, v0 + 2 * h + 2)
                    if h >= 2:
                        act.wait_ge(scores_full, BATCHES * i + 4 * (h - 1))
                    act.activation(q_hi[:, h % 2, :], qf[:], ACT.Copy).then_inc(q_hi_ready, 1)
                    if hd > 0:
                        act.wait_ge(qstat_full, hd)
                    act.activation(qsq[:], qf[:], ACT.Square).then_inc(qsq_ready, 1)

                def query_root(h):
                    act.wait_ge(rqv_ready, MHEADS * i + h + 1)
                    act.activation(rq_s[:], rq_v[:], ACT.Sqrt).then_inc(rqs_ready, 1)

                def exps(n):
                    h, b, g = n // 4, n % 2, BATCHES * i + n
                    act.wait_ge(nbias_ready, g + 1)
                    if g >= 2:
                        act.wait_ge(pT_full, g - 1)
                    for j in range(2):
                        tb = 2 * (n % 4) + j
                        act.activation(prob[:, b, j, :], ps[:, 4 + b, j * NMEM:(j + 1) * NMEM], ACT.Exp,
                                       bias=nbias[:, b, j:j + 1], scale=rq[:, h % 2, tb:tb + 1],
                                       accum_out=psums[:, b, j:j + 1]).then_inc(exp_done, 1)

                query(0)
                query(1)
                query_root(0)
                query_root(1)
                prep(u0 + 4)
                exps(0)
                for n in range(BATCHES):
                    b, g = n % 2, BATCHES * i + n
                    if n in (4, 8):
                        if n == 4:
                            prep(u0 + 5)
                        query(1 + n // 4)
                    if n in (6, 10):
                        query_root(n // 4 + 1)
                    if n + 1 < BATCHES:
                        exps(n + 1)
                    act.wait_ge(pT_full, g + 1)
                    if g >= 2:
                        act.wait_ge(mo_full, g - 1)
                    act.activation(pT_hi[:, b].rearrange("p a c -> p (a c)"), ps[:, 6 + b, :], ACT.Copy
                                   ).then_inc(pT_hi_ready, 1)
                    for done in ([n - 1] if n > 0 else []) + ([n] if n == BATCHES - 1 else []):
                        act.wait_ge(mo_full, BATCHES * i + done + 1)
                        act.activation(me_f[:, done // 4, done % 4 * 2 * P:(done % 4 + 1) * 2 * P], ps[:, 2, 0:2 * P],
                                       ACT.Copy).then_inc(mo_ready, 1)

                u0, f0, v0 = base["C", i]
                if i % 2 == 0:
                    with act.Fori(0, KB) as b:
                        for j in range(3):
                            prep(u0 + j + 2, b * 3, b)
                else:
                    def sigmoids(row, par, r, t):
                        n = 2 * P * (t + 1)
                        act.wait_ge(z_full, row + 1)
                        z = banks(2 * r)[:, 0:n]
                        act.activation(keep[:, par, r, 0:n], z, ACT.Sigmoid, scale=-1.0).then_inc(keep_ready, 1)
                        act.activation(sig[:, par, r, 0:n], z, ACT.Sigmoid).then_inc(sig_ready, 1)

                    def project(hp, to, piece):
                        if piece in (1, 3):
                            act.wait_ge(evacuated, hp * 6 + (v0 + piece + 1))
                            dst = (sq_hi, sk_hi)[piece // 2]
                            act.activation(dst[:, to, :], tf[:], ACT.Copy).then_inc(sqk_hi_ready, 1)
                        if piece >= 6:
                            act.wait_ge(vT_full, hp * 2 + (piece - 5))
                            dst = sv[:, to, 4 * (piece - 6):4 * (piece - 5), :, 0:SHEAD]
                            act.activation(dst, ps[:, 7, :].rearrange("p (b h c) -> p b h c", b=4, h=2), ACT.Copy
                                           ).then_inc(vT_hi_ready, 1)

                    def chunk(hp, it, c, first):
                        n = CHUNKS_BEFORE[it] + c
                        act.wait_ge(aT_full, hp * CHUNKS + (n + 1))
                        if not (first and n < 2):
                            act.wait_ge(pv_done, hp * CHUNKS + (n - 1))
                        act.activation(aT_hi[:, n % 2].rearrange("p a c -> p (a c)"), ps[:, 4 + n % 2, :],
                                       ACT.Copy).then_inc(aT_hi_ready, 1)

                    def pair(hp, par, last, first=False):
                        for it in range(ITEMS):
                            t, hh = it % 4, it // 4
                            for c in range(min(t + 1, 2)):
                                chunk(hp, it, c, first)
                            if not (last and it == ITEMS - 1):
                                for r in range(2):
                                    sigmoids(hp * ROWS + (2 * (it + 1) + r), (it + 1) % 2, r, (it + 1) % 4)
                            if not last and it in (0, 3, 7):
                                prep(u0 + 5 + (it + 1) // 4, hp * 3, hp)
                            for c in range(2, t + 1):
                                chunk(hp, it, c, first)
                                if it == ITEMS - 1 and not last:
                                    project(hp + 1, 1 - par, 4 + c)
                            rows = slice(hh * SHEAD, (hh + 1) * SHEAD)
                            act.wait_ge(pv_done, hp * CHUNKS + CHUNKS_BEFORE[it + 1])
                            if not (first and it == 0):
                                act.wait_ge(o_sum_ready, hp * ITEMS + it)
                            act.activation(o_low[rows, :], ps[SHEAD:P, 6, 0:2 * P], ACT.Copy
                                           ).then_inc(o_low_ready, 1)
                            if not last and it in (2, 5):
                                project(hp + 1, 1 - par, 1 if it == 2 else 3)

                    for piece in range(8):
                        if piece in (0, 2, 4):
                            prep(u0 + 2 + piece // 2)
                        project(0, 0, piece)
                    act.wait_ge(x_spilled, 16)
                    for r in range(2):
                        sigmoids(r, 0, r, 0)
                    act.wait_ge(me_stored, 16 * MHEADS)
                    pair(0, 0, False, first=True)
                    with act.Fori(0, KB // 2 - 1) as d:
                        pair(d * 2 + 1, 1, False)
                        pair(d * 2 + 2, 0, False)
                    pair(KB - 1, 1, True)

                u0, f0, v0 = base["E", i]
                if i % 2 == 0:
                    source = mix_f
                    act.wait_ge(conv_step, 5 * KB + 1)
                    act.wait_ge(w_used, u0)
                else:
                    source = mx
                    act.wait_ge(o_sum_ready, ITEMS * KB)
                    act.dma_start(me_f[:], d_me).then_inc(me_loaded, 16)
                    act.dma_start(x[:], d_x).then_inc(x_back, 16)
                    act.wait_ge(mx_loaded, 16)
                for h in range(2):
                    for m in range(KB):
                        act.activation(xg_hi[:, m, ln[h]], source[:, m, ln[h]], ACT.Copy).then_inc(mx_hi_ready, 1)
                prep(u0 + 2)
                if i % 2 == 1:
                    act.wait_ge(me_loaded, 16)
                for m in range(MHEADS):
                    act.activation(me_hi[:, m, :], me_f[:, m, :], ACT.Copy).then_inc(me_hi_ready, 1)
                prep(u0 + 3)
                prep(u0 + 4)
                with act.Fori(1, KB // 2) as pm:
                    for j in range(3):
                        prep(u0 + j + 2, pm * 3, pm)

                u0, f0, v0 = base["F", i]
                nu, a0 = 2 * i + 1, FBLK * i
                for m, h in split_order(nu):
                    split(nu, m, h)
                squares_and_root(nu, u0)

                def silu(blk, blocks, visits):
                    act.wait_ge(evacuated, visits)
                    act.activation(gate[:, blk, :], gate[:, blk, :], ACT.Silu).then_inc(silu_done, 1)

                def products(blocks):
                    for blk in range(2):
                        act.wait_ge(prod_ready, blocks + (blk + 1))
                        act.activation(act_hi[:, blk, :], up[:, blk, :], ACT.Copy).then_inc(act_hi_ready, 1)

                silu(0, a0, v0 + 2)
                silu(1, a0, v0 + 4)
                prep(u0 + 4)
                prep(u0 + 5)
                products(a0)
                with act.Fori(0, FGROUPS - 1) as g:
                    n, v = u0 + 4, g * 24 + (v0 + 8)
                    prep(n + 2, g * 6, g * 2)
                    silu(0, None, v + 2)
                    prep(n + 3, g * 6, g * 2)
                    silu(1, None, v + 4)
                    for j in (4, 5, 6, 7):
                        prep(n + j, g * 6, g * 2)
                    products(g * 2 + (a0 + 2))
                prep(base["end", i][0])
                if i + 1 < LAYERS:
                    for m, h in split_order(nu + 1):
                        split(nu + 1, m, h)
                    prep(base["end", i][0] + 1)

        @block.vector
        def _(dve):
            def prep(u, more=0, rounds=0):
                s = u % WSLOTS
                if u >= UNITS:
                    return
                dve.wait_ge(w_hi_ready, more + (u + 1))
                dve.tensor_tensor(w_lo[:, s, :], raw[:, s, :], fp(w_hi[:, s, :]), ALU.subtract
                                  ).then_inc(w_lo_ready, 1)

            def split(nu, m, h):
                i, g = nu // 2, 2 * (nu % 2)
                dve.wait_ge(xg_hi_ready, split_count(nu, m, h))
                dve.scalar_tensor_tensor(xg_lo[:, m, ln[h]], x[:, m, ln[h]], gain[:, g, i, m:m + 1],
                                         fp(xg_hi[:, m, ln[h]]), ALU.mult, ALU.subtract).then_inc(xg_lo_ready, 1)

            def norm(nu, u0, v0):
                for m in range(KB):
                    n = KB * nu + m
                    dve.wait_ge(sq_ready, n + 1)
                    if n > 0:
                        dve.wait_ge(acc_added, n)
                    if m == 0:
                        dve.tensor_copy(acc[:], sq[:, 0, :]).then_inc(acc_added, 1)
                    else:
                        dve.tensor_tensor(acc[:], acc[:], sq[:, m % 2, :], ALU.add).then_inc(acc_added, 1)
                prep(u0 + 2)
                prep(u0 + 3)
                dve.wait_ge(root_ready, nu + 1)
                dve.wait_ge(evacuated, v0)
                dve.reciprocal(R[:], rtmp[:]).then_inc(r_ready, 1)
                dve.wait_ge(r_ready, nu + 1)

            def scaled(dst, b, h):
                dve.tensor_tensor(dst, ps[:, b, :], R[:, ln[h]], ALU.mult).then_inc(evacuated, 1)

            dve.memset(eps[:], EPS).then_inc(eps_made, 1)

            dve.wait_ge(consts_in, 48)

            def memory_lo(i):
                for m in range(KB):
                    dve.wait_ge(mg_hi_ready, KB * i + m + 1)
                    dve.scalar_tensor_tensor(mg_lo[i][:, m, :], mem[:, m, :], gain[:, 1, i, m:m + 1],
                                             fp(mg_hi[i][:, m, :]), ALU.mult, ALU.subtract).then_inc(mg_lo_ready, 1)

            memory_lo(0)
            prep(0)
            prep(1)
            dve.scalar_tensor_tensor(g_qk[:], g_heads[:, 0, :], float(P) ** -0.5, g_heads[:, 1, :],
                                     ALU.mult, ALU.mult).then_inc(gqk_ready, 1)
            prep(2)
            dve.wait_ge(mroot_ready, 2)
            dve.reciprocal(mr[:], mrt[:]).then_inc(mr_ready, 1)
            dve.reciprocal(mcol[:], mcol_t[:]).then_inc(mr_ready, 1)
            memory_lo(1)
            dve.wait_ge(mr_ready, 2)
            dve.wait_ge(gqk_ready, 1)
            for i in range(LAYERS):
                u0, f0, v0 = base["A", i]
                if i > 0:
                    dve.wait_ge(ka_lo_ready, i)
                for n in range(MHEADS):
                    if i > 0 or n > 0:
                        prep(u0 + n + 2)
                    dve.wait_ge(w_used, u0 + n + 1)
                    dve.tensor_tensor(kf[:, n * NMEM:(n + 1) * NMEM], ps[:, n, 0:NMEM], mr[:], ALU.mult
                                      ).then_inc(evacuated, 1)
                for n in range(MHEADS):
                    prep(u0 + MHEADS + n + 2)
                    dve.wait_ge(va_hi_ready, 2 * (MHEADS * i + n) + 2)
                    cols = slice(n * P, (n + 1) * P)
                    for mb in range(2):
                        last = dve.scalar_tensor_tensor(
                            va_lo[:, mb, cols], ps[:, 6 + n % 2, mb * P:(mb + 1) * P], mcol[:, mb:mb + 1],
                            fp(va_hi[:, mb, cols]), ALU.mult, ALU.subtract)
                    last.then_inc(evacuated, 1)
                dve.wait_ge(kroot_ready, i + 1)
                dve.reciprocal(kr[:], kr[:]).then_inc(kr_ready, 1)
                dve.wait_ge(kr_ready, i + 1)
                dve.wait_ge(evacuated, v0 + MHEADS)
                dve.scalar_tensor_tensor(kn[:], kf[:], g_qk[:, i:i + 1], kr[:], ALU.mult, ALU.mult
                                         ).then_inc(kn_ready, 1)
                dve.wait_ge(ka_hi_ready, i + 1)
                if i > 0:
                    dve.wait_ge(kv_stored, 64 * i)
                dve.tensor_tensor(ka_lo[:], kn[:], fp(ka_hi[:]), ALU.subtract).then_inc(ka_lo_ready, 1)
            for m, h in split_order(0):
                split(0, m, h)

            for i in range(LAYERS):
                u0, f0, v0 = base["B", i]
                norm(2 * i, u0, v0)

                def query_half(h, half):
                    hd = MHEADS * i + h
                    if hd > 0:
                        dve.wait_ge(q_lo_ready, hd)
                        dve.wait_ge(qsq_ready, hd)
                    if half == 0:
                        dve.wait_ge(bank_full, f0 + h + 1)
                    else:
                        dve.wait_ge(w_used, u0 + h + 1)
                    scaled(qf[:, ln[half]], (6 if h == 1 else 0) + half, half)

                def query(h):
                    hd = MHEADS * i + h
                    dve.wait_ge(q_hi_ready, hd + 1)
                    dve.tensor_tensor(q_lo[:, h % 2, :], qf[:], fp(q_hi[:, h % 2, :]), ALU.subtract
                                      ).then_inc(q_lo_ready, 1)

                def query_root(h):
                    hd = MHEADS * i + h
                    dve.wait_ge(qstat_full, hd + 1)
                    if hd > 0:
                        dve.wait_ge(rq_ready, hd)
                    dve.tensor_scalar(rq_v[:], ps[:, 3, 0:KB], EPS, None, ALU.add).then_inc(rqv_ready, 1)
                    dve.wait_ge(rqs_ready, hd + 1)
                    y, s0 = rq[:, h % 2, :], 4 * hd
                    dve.reciprocal(y, rq_s[:]).then_inc(rq_step, 1)
                    dve.wait_ge(rq_step, s0 + 1)
                    dve.tensor_tensor(rq_t[:], rq_v[:], y, ALU.mult).then_inc(rq_step, 1)
                    dve.wait_ge(rq_step, s0 + 2)
                    dve.tensor_tensor(rq_t[:], rq_t[:], y, ALU.mult).then_inc(rq_step, 1)
                    dve.wait_ge(rq_step, s0 + 3)
                    dve.tensor_scalar(rq_t[:], rq_t[:], -0.5, 1.5, ALU.mult, ALU.add).then_inc(rq_step, 1)
                    dve.wait_ge(rq_step, s0 + 4)
                    dve.tensor_tensor(y, y, rq_t[:], ALU.mult).then_inc(rq_ready, 1)
                    dve.wait_ge(rq_ready, hd + 1)

                def maxima(n):
                    h, b, g = n // 4, n % 2, BATCHES * i + n
                    dve.wait_ge(scores_full, g + 1)
                    if g >= 2:
                        dve.wait_ge(nbias_ready, g - 1)
                    dve.tensor_reduce(smax[:, b, :], ps[:, 4 + b, :].rearrange("p (j c) -> p j c", j=2), AX_X, ALU.max
                                      ).then_inc(max_ready, 1)
                    dve.wait_ge(max_ready, g + 1)
                    if g >= 2:
                        dve.wait_ge(exp_done, 2 * (g - 1))
                    tb = 2 * (n % 4)
                    dve.scalar_tensor_tensor(nbias[:, b, :], smax[:, b, :], -1.0, rq[:, h % 2, tb:tb + 2],
                                             ALU.mult, ALU.mult).then_inc(nbias_ready, 1)

                def normalize(n):
                    b, g = n % 2, BATCHES * i + n
                    dve.wait_ge(exp_done, 2 * g + 2)
                    if g >= 2:
                        dve.wait_ge(prob_ready, g - 1)
                    dve.reciprocal(rsums[:, b, :], psums[:, b, :]).then_inc(rsum_ready, 1)
                    dve.wait_ge(rsum_ready, g + 1)
                    dve.tensor_tensor(prob[:, b], prob[:, b], rsums[:, b, :].unsqueeze(2).to_broadcast([P, 2, NMEM]),
                                      ALU.mult).then_inc(prob_ready, 1)

                for h in range(2):
                    query_half(h, 0)
                    query_half(h, 1)
                    query(h)
                query_root(0)
                query_root(1)
                prep(u0 + 4)
                maxima(0)
                maxima(1)
                normalize(0)
                for n in range(BATCHES):
                    b, g = n % 2, BATCHES * i + n
                    if n in (2, 6):
                        query_half(2 + n // 4, 0)
                    if n in (4, 8):
                        if n == 4:
                            prep(u0 + 5)
                        query_half(1 + n // 4, 1)
                        query(1 + n // 4)
                    if n in (6, 10):
                        query_root(n // 4 + 1)
                    if n + 2 < BATCHES:
                        maxima(n + 2)
                    if n + 1 < BATCHES:
                        normalize(n + 1)
                    dve.wait_ge(pT_hi_ready, g + 1)
                    dve.tensor_tensor(pT_lo[:, b].rearrange("p a c -> p (a c)"), ps[:, 6 + b, :],
                                      fp(pT_hi[:, b].rearrange("p a c -> p (a c)")), ALU.subtract
                                      ).then_inc(pT_lo_ready, 1)

                u0, f0, v0 = base["C", i]
                if i % 2 == 0:
                    dve.memset(cy[:, 0:2], 0.0).then_inc(conv_step, 1)
                    with dve.Fori(0, KB) as b:
                        dve.wait_ge(conv_step, b * 5 + 1)
                        for j, dst in enumerate((cb, cc, cu)):
                            prep(u0 + j + 2, b * 3)
                            for h in range(2):
                                if h == 0:
                                    dve.wait_ge(bank_full, b * 3 + (f0 + j + 1))
                                else:
                                    dve.wait_ge(w_used, b * 3 + (u0 + j + 1))
                                scaled(dst[:, ln[h]], 2 * j + h, h)
                        dve.wait_ge(evacuated, b * 6 + (v0 + 6))
                        dve.tensor_tensor(cy[:, 2:], cu[:], cc[:], ALU.mult).then_inc(conv_step, 1)
                        dve.wait_ge(conv_step, b * 5 + 2)
                        mixed = mix_f[:, bass.ds(b, 1), :].rearrange("p a c -> p (a c)")
                        dve.tensor_scalar(mixed, cy[:, 2:], taps[:, 2, bass.ds(b, 1)], None, ALU.mult
                                          ).then_inc(conv_step, 1)
                        for j in (1, 0):
                            dve.wait_ge(conv_step, b * 5 + (4 - j))
                            dve.scalar_tensor_tensor(mixed, cy[:, j:j + SEQ], taps[:, j, bass.ds(b, 1)], mixed,
                                                     ALU.mult, ALU.add).then_inc(conv_step, 1)
                        dve.wait_ge(conv_step, b * 5 + 5)
                        dve.tensor_tensor(mixed, mixed, cb[:], ALU.mult).then_inc(conv_step, 1)
                else:
                    def scan(row, par, r, t):
                        n = 2 * P * (t + 1)
                        dve.wait_ge(keep_ready, row + 1)
                        k = keep[:, par, r, 0:n][:, ::-1]
                        dve.tensor_tensor_scan(k, k, k, 1.0, ALU.mult, ALU.bypass).then_inc(scanned, 1)

                    def project(hp, piece):
                        part, h = piece // 2, piece % 2
                        if h == 0:
                            dve.wait_ge(bank_full, hp * 3 + (f0 + part + 1))
                            if part > 0:
                                dve.wait_ge(sqk_lo_ready, hp * 2 + part)
                        else:
                            dve.wait_ge(w_used, hp * 3 + (u0 + part + 1))
                        if part == 0:
                            dve.scalar_tensor_tensor(tf[:, ln[h]], ps[:, 7, :], float(SHEAD) ** -0.5,
                                                     R[:, ln[h]], ALU.mult, ALU.mult).then_inc(evacuated, 1)
                        else:
                            scaled(tf[:, ln[h]], 7, h)

                    def lo_part(hp, to, part):
                        hi, lo = ((sq_hi, sq_lo), (sk_hi, sk_lo))[part]
                        dve.wait_ge(sqk_hi_ready, hp * 2 + (part + 1))
                        dve.tensor_tensor(lo[:, to, :], tf[:], fp(hi[:, to, :]), ALU.subtract
                                          ).then_inc(sqk_lo_ready, 1)

                    def values(hp, to, n):
                        blocks = slice(4 * n, 4 * n + 4)
                        dve.wait_ge(vT_hi_ready, hp * 2 + (n + 1))
                        dve.tensor_tensor(sv[:, to, blocks, :, SHEAD:], ps[:, 7, :].rearrange(
                            "p (b h c) -> p b h c", b=4, h=2), fp(sv[:, to, blocks, :, 0:SHEAD]), ALU.subtract
                                          ).then_inc(vT_lo_ready, 1)

                    def chunk(hp, it, c):
                        n = CHUNKS_BEFORE[it] + c
                        dve.wait_ge(aT_hi_ready, hp * CHUNKS + (n + 1))
                        dve.tensor_tensor(aT_lo[:, n % 2].rearrange("p a c -> p (a c)"), ps[:, 4 + n % 2, :],
                                          fp(aT_hi[:, n % 2].rearrange("p a c -> p (a c)")), ALU.subtract
                                          ).then_inc(aT_lo_ready, 1)

                    def pair(hp, par, last, first=False):
                        for it in range(ITEMS):
                            t, hh = it % 4, it // 4

                            def finished(n):
                                if not last and (it, n) in ENDS:
                                    project(hp + 1, ENDS[it, n])

                            for c in range(min(t + 1, 2)):
                                chunk(hp, it, c)
                            if not (last and it == ITEMS - 1):
                                for r in range(2):
                                    scan(hp * ROWS + (2 * (it + 1) + r), (it + 1) % 2, r, (it + 1) % 4)
                                    finished(r)
                            if not last and it in (0, 3, 7):
                                prep(u0 + 5 + (it + 1) // 4, hp * 3)
                            for c in range(2, t + 1):
                                finished(c)
                                chunk(hp, it, c)
                                if it == ITEMS - 1 and not last:
                                    values(hp + 1, 1 - par, c - 2)
                            if t >= 1:
                                finished(t + 1)
                            rows = slice(hh * SHEAD, (hh + 1) * SHEAD)
                            if last:
                                dst = mx[rows, KB - 1, t * 2 * P:(t + 1) * 2 * P]
                            else:
                                dst = o_sum[rows, it % 2, :]
                                if not (first and it < 2):
                                    dve.wait_ge(so_stored[it % 2], hp * (8 * ITEMS) + 16 * (it // 2))
                            dve.wait_ge(o_low_ready, hp * ITEMS + (it + 1))
                            dve.tensor_tensor(dst, ps[0:SHEAD, 6, 0:2 * P], o_low[rows, :], ALU.add
                                              ).then_inc(o_sum_ready, 1)
                            if not last and it in (2, 5):
                                lo_part(hp + 1, 1 - par, it // 4)

                    for piece in range(6):
                        if piece in (0, 2, 4):
                            prep(u0 + 2 + piece // 2)
                        project(0, piece)
                        if piece in (1, 3):
                            lo_part(0, 0, piece // 2)
                    for n in range(2):
                        values(0, 0, n)
                    for r in range(2):
                        scan(r, 0, r, 0)
                    pair(0, 0, False, first=True)
                    with dve.Fori(0, KB // 2 - 1) as d:
                        pair(d * 2 + 1, 1, False)
                        pair(d * 2 + 2, 0, False)
                    pair(KB - 1, 1, True)

                u0, f0, v0 = base["E", i]
                source = mix_f if i % 2 == 0 else mx
                for h in range(2):
                    for m in range(KB):
                        dve.wait_ge(mx_hi_ready, 2 * KB * i + KB * h + m + 1)
                        dve.tensor_tensor(xg_lo[:, m, ln[h]], source[:, m, ln[h]], fp(xg_hi[:, m, ln[h]]), ALU.subtract
                                          ).then_inc(mx_lo_ready, 1)
                prep(u0 + 2)
                dve.wait_ge(mx_lo_ready, 2 * KB * (i + 1))
                for m in range(MHEADS):
                    dve.wait_ge(me_hi_ready, MHEADS * i + m + 1)
                    dve.tensor_tensor(me_lo[:, m, :], me_f[:, m, :], fp(me_hi[:, m, :]), ALU.subtract
                                      ).then_inc(me_lo_ready, 1)
                if i % 2 == 1:
                    dve.wait_ge(x_back, 16)
                prep(u0 + 3)
                prep(u0 + 4)

                def add_pair(pm, block):
                    for j in range(4):
                        if j < 3:
                            dve.wait_ge(bank_full, pm * 3 + (f0 + j + 1))
                        else:
                            dve.wait_ge(w_used, pm * 3 + (u0 + 3))
                        xs = block(j // 2)[:, ln[j % 2]]
                        dve.tensor_tensor(xs, xs, ps[:, j, :], ALU.add).then_inc(evacuated, 1)

                add_pair(0, lambda a: x[:, a, :])
                with dve.Fori(1, KB // 2) as pm:
                    for j in range(3):
                        prep(u0 + j + 2, pm * 3)
                    add_pair(pm, lambda a: x[:, bass.ds(pm * 2 + a, 1), :].rearrange("p a c -> p (a c)"))

                u0, f0, v0 = base["F", i]
                nu, a0 = 2 * i + 1, FBLK * i
                for m, h in split_order(nu):
                    split(nu, m, h)
                norm(nu, u0, v0)

                def fill(dst, blk, f, u, b0):
                    for h in range(2):
                        if h == 0:
                            dve.wait_ge(bank_full, f)
                        else:
                            dve.wait_ge(w_used, u)
                        scaled(dst[:, blk, ln[h]], (b0 + h) % 8, h)

                def product(blk, blocks, visits):
                    dve.wait_ge(evacuated, visits)
                    dve.wait_ge(silu_done, blocks + (blk + 1))
                    dve.tensor_tensor(up[:, blk, :], gate[:, blk, :], up[:, blk, :], ALU.mult
                                      ).then_inc(prod_ready, 1)
                    dve.wait_ge(act_hi_ready, blocks + (blk + 1))
                    dve.tensor_tensor(act_lo[:, blk, :], up[:, blk, :], fp(act_hi[:, blk, :]), ALU.subtract
                                      ).then_inc(act_lo_ready, 1)

                def down(f, u, v, j0, after=None):
                    dve.wait_ge(evacuated, v)
                    for n in range(2 * KB):
                        m, h = n // 2, n % 2
                        if n < 2 * KB - 1:
                            dve.wait_ge(bank_full, f + (n + 1))
                        else:
                            dve.wait_ge(w_used, u)
                        dve.tensor_tensor(x[:, m, ln[h]], x[:, m, ln[h]], ps[:, (j0 + n) % 8, :], ALU.add
                                          ).then_inc(evacuated, 1)
                        if after and h == 1 and m > 0:
                            after(m - 1)
                    if after:
                        after(KB - 1)

                fill(gate, 0, f0 + 1, u0 + 1, 0)
                fill(gate, 1, f0 + 2, u0 + 2, 2)
                prep(u0 + 4)
                fill(up, 0, f0 + 3, u0 + 3, 6)
                prep(u0 + 5)
                fill(up, 1, f0 + 4, u0 + 4, 0)
                product(0, a0, v0 + 6)
                product(1, a0, v0 + 8)
                with dve.Fori(0, FGROUPS - 1) as g:
                    n, f, v, b = u0 + 4, g * 19 + (f0 + 4), g * 24 + (v0 + 8), g * 2 + (a0 + 2)
                    more = g * 6
                    dve.wait_ge(act_lo_ready, b)
                    prep(n + 2, more)
                    fill(gate, 0, f + 1, more + (n + 1), 2)
                    prep(n + 3, more)
                    fill(gate, 1, f + 2, more + (n + 2), 4)
                    prep(n + 4, more)
                    down(f + 2, more + (n + 4), v + 4, 6)
                    prep(n + 5, more)
                    prep(n + 6, more)
                    fill(up, 0, f + 18, more + (n + 5), 22)
                    prep(n + 7, more)
                    fill(up, 1, f + 19, more + (n + 6), 24)
                    product(0, b, v + 22)
                    product(1, b, v + 24)
                ue, fe, ve = base["end", i]
                prep(ue)
                if i + 1 < LAYERS:
                    down(fe - 15, ue, ve - 16, 2, after=lambda m: [split(nu + 1, m, h) for h in range(2)])
                    prep(ue + 1)
                else:
                    down(fe - 15, ue, ve - 16, 2)

        @block.tensor
        def _(pe):
            def three(out, whi, wlo, mhi, mlo, start, stop):
                pe.matmul(out, whi, mhi, start=start, stop=False)
                pe.matmul(out, whi, mlo, start=False, stop=False)
                return pe.matmul(out, wlo, mhi, start=False, stop=stop)

            def unit(u, more, bank_of, waits, first=None):
                s = u % WSLOTS
                pe.wait_ge(w_lo_ready, more + (u + 1))
                for h in range(2):
                    if waits[h] is not None:
                        pe.wait_ge(evacuated, waits[h])
                    for k in range(KB):
                        if first is not None:
                            pe.wait_ge(xg_lo_ready, split_count(first, k, h))
                        c = slice(k * P, (k + 1) * P)
                        last = three(ps[:, bank_of(h), :], w_hi[:, s, c], w_lo[:, s, c],
                                     xg_hi[:, k, ln[h]], xg_lo[:, k, ln[h]], k == 0, k == KB - 1)
                    last.then_inc(bank_full if h == 0 else w_used, 1)

            def norm(nu):
                pe.wait_ge(acc_added, KB * (nu + 1))
                for h in range(2):
                    pe.matmul(ps[:, 4 + h, :], mean_all[:], acc[:, ln[h]], start=True, stop=True
                              ).then_inc(stat_full, 1)

            def memory_keys(i, n):
                u = base["A", i][0] + n
                s = u % WSLOTS
                pe.wait_ge(w_lo_ready, u + 1)
                for k in range(KB):
                    if n == 0:
                        pe.wait_ge(mg_lo_ready, KB * i + k + 1)
                    c = slice(k * P, (k + 1) * P)
                    last = three(ps[:, n, 0:NMEM], w_hi[:, s, c], w_lo[:, s, c], mg_hi[i][:, k, :], mg_lo[i][:, k, :],
                                 k == 0, k == KB - 1)
                last.then_inc(w_used, 1)

            memory_keys(0, 0)
            pe.wait_ge(consts_made, 4)
            pe.wait_ge(msq_ready, 1)
            for k in range(KB):
                pe.matmul(ps[:, 4, 0:NMEM], mean_all[:], msq[:, k, :], start=(k == 0), stop=(k == KB - 1))
            for mb in range(2):
                for k in range(KB):
                    last = pe.matmul(ps[:, 5, mb:mb + 1], msq[:, k, mb * P:(mb + 1) * P], mean_all[:, 0:1],
                                     start=(k == 0), stop=(k == KB - 1))
            last.then_inc(mstat_full, 1)
            for i in range(LAYERS):
                u0, f0, v0 = base["A", i]
                if i > 0:
                    pe.wait_ge(evacuated, v0)
                for n in range(MHEADS):
                    if i > 0 or n > 0:
                        memory_keys(i, n)
                for n in range(MHEADS):
                    u = u0 + MHEADS + n
                    s = u % WSLOTS
                    pe.wait_ge(w_lo_ready, u + 1)
                    if n >= 2:
                        pe.wait_ge(evacuated, v0 + MHEADS + n - 1)
                    for mb in range(2):
                        tok = slice(mb * P, (mb + 1) * P)
                        for k in range(KB):
                            c = slice(k * P, (k + 1) * P)
                            last = three(ps[:, 6 + n % 2, tok], mg_hi[i][:, k, tok], mg_lo[i][:, k, tok],
                                         w_hi[:, s, c], w_lo[:, s, c], k == 0, k == KB - 1)
                    last.then_inc(w_used, 1)
                pe.wait_ge(ksq_ready, i + 1)
                pe.wait_ge(mroot_ready, 2)
                if i > 0:
                    pe.wait_ge(kroot_ready, i)
                for h in range(2):
                    pe.matmul(ps[:, 4 + h, :], mean_head[:], ksq[:, ln[h]], start=True, stop=True
                              ).then_inc(kstat_full, 1)

            for i in range(LAYERS):
                u0, f0, v0 = base["B", i]
                pe.wait_ge(evacuated, v0)
                if i == 0:
                    pe.wait_ge(kroot_ready, LAYERS)

                def qstat(h):
                    hd = MHEADS * i + h
                    pe.wait_ge(qsq_ready, hd + 1)
                    if hd > 0:
                        pe.wait_ge(rqv_ready, hd)
                    for b in range(KB):
                        last = pe.matmul(ps[:, 3, b:b + 1], qsq[:, b * P:(b + 1) * P], mean_head[:, 0:1],
                                         start=True, stop=True)
                    last.then_inc(qstat_full, 1)

                def scores(n):
                    h, b, g = n // 4, n % 2, BATCHES * i + n
                    pe.wait_ge(q_lo_ready, MHEADS * i + h + 1)
                    if n == 0:
                        pe.wait_ge(kv_loaded, 64 * (i + 1))
                        pe.wait_ge(root_ready, 2 * i + 1)
                    if n >= 2:
                        pe.wait_ge(exp_done, 2 * (g - 1))
                    ks = slice(h * NMEM, (h + 1) * NMEM)
                    for j in range(2):
                        tok = slice((2 * (n % 4) + j) * P, (2 * (n % 4) + j + 1) * P)
                        last = three(ps[:, 4 + b, j * NMEM:(j + 1) * NMEM], q_hi[:, h % 2, tok], q_lo[:, h % 2, tok],
                                     k_hi[:, ks], k_lo[:, ks], True, True)
                    last.then_inc(scores_full, 1)

                def turn_probs(n):
                    b, g = n % 2, BATCHES * i + n
                    pe.wait_ge(prob_ready, g + 1)
                    if n < 2:
                        pe.wait_ge(evacuated, v0 + 4)
                    else:
                        pe.wait_ge(pT_lo_ready, g - 1)
                    for mb in range(2):
                        for j in range(2):
                            last = pe.transpose(ps[:, 6 + b, (2 * mb + j) * P:(2 * mb + j + 1) * P],
                                                prob[:, b, j, mb * P:(mb + 1) * P], ident[:])
                    last.then_inc(pT_full, 1)

                def attended(n):
                    h, b, g = n // 4, n % 2, BATCHES * i + n
                    pe.wait_ge(pT_lo_ready, g + 1)
                    if g > 0:
                        pe.wait_ge(mo_ready, g)
                    hs = slice(h * P, (h + 1) * P)
                    for mb in range(2):
                        last = three(ps[:, 2, 0:2 * P], v_hi[:, mb, hs], v_lo[:, mb, hs],
                                     pT_hi[:, b, mb, :], pT_lo[:, b, mb, :], mb == 0, mb == 1)
                    last.then_inc(mo_full, 1)

                def quarter_unit(h, q):
                    u, half = u0 + h, q // 2
                    s = u % WSLOTS
                    if q == 0:
                        pe.wait_ge(w_lo_ready, u + 1)
                    if q % 2 == 0:
                        pe.wait_ge(evacuated, v0 + (1 if h == 2 else 5) + half)
                    for k in range(4 * (q % 2), 4 * (q % 2) + 4):
                        c = slice(k * P, (k + 1) * P)
                        last = three(ps[:, half, :], w_hi[:, s, c], w_lo[:, s, c],
                                     xg_hi[:, k, ln[half]], xg_lo[:, k, ln[half]], k == 0, k == KB - 1)
                    if q % 2 == 1:
                        last.then_inc(bank_full if half == 0 else w_used, 1)

                unit(u0, 0, lambda h: h, (None, None), first=2 * i)
                unit(u0 + 1, 0, lambda h: 6 + h, (None, None))
                norm(2 * i)
                qstat(0)
                scores(0)
                scores(1)
                qstat(1)
                for n in range(BATCHES):
                    if n in (5, 9):
                        qstat(1 + n // 4)
                    if n + 2 < BATCHES:
                        scores(n + 2)
                    turn_probs(n)
                    if n > 0:
                        attended(n - 1)
                    if n < 8:
                        quarter_unit(2 + n // 4, n % 4)
                attended(BATCHES - 1)

                u0, f0, v0 = base["C", i]
                pe.wait_ge(evacuated, v0)
                pe.wait_ge(mo_ready, BATCHES * (i + 1))
                if i % 2 == 0:
                    with pe.Fori(0, KB) as b:
                        for j in range(3):
                            v = b * 6 + (v0 + 2 * j - 5)
                            unit(u0 + j, b * 3, lambda h: 2 * j + h, (v, v + 1))
                else:
                    def z(row, par, p0, r, t, first):
                        if not first:
                            pe.wait_ge(sig_ready, row - 1)
                        hd = slice(p0, p0 + SHEAD)
                        q = slice((2 * t + r) * P, (2 * t + r + 1) * P)
                        n = 2 * P * (t + 1)
                        for c in range(0, n, HALF):
                            w = min(HALF, n - c)
                            o = ps[:, 2 * r + c // HALF, :]
                            final = c + w == n
                            three(o[:, 0:w], sq_hi[hd, par, q], sq_lo[hd, par, q],
                                  sk_hi[hd, par, c:c + w], sk_lo[hd, par, c:c + w], True, not final)
                        m = (2 - r) * P
                        pe.matmul(o[:, w - m:w], ident_r[:], mask_r[:, 0:m], start=False, stop=True
                                  ).then_inc(z_full, 1)

                    def project(hp, piece, ks=range(KB), first=False):
                        part, h = piece // 2, piece % 2
                        s = (u0 + part) % WSLOTS
                        if 0 in ks:
                            if h == 0:
                                pe.wait_ge(w_lo_ready, hp * 3 + (u0 + part + 1))
                            pe.wait_ge(evacuated, hp * 6 + (v0 + piece))
                            if piece == 0 and not first:
                                pe.wait_ge(vT_lo_ready, hp * 2)
                        for k in ks:
                            c = slice(k * P, (k + 1) * P)
                            last = three(ps[:, 7, :], w_hi[:, s, c], w_lo[:, s, c],
                                         xg_hi[:, k, ln[h]], xg_lo[:, k, ln[h]], k == 0, k == KB - 1)
                            if k == KB - 1:
                                last.then_inc(bank_full if h == 0 else w_used, 1)

                    def turn_values(hp, n):
                        pe.wait_ge(evacuated, hp * 6 + (v0 + 6))
                        if n == 1:
                            pe.wait_ge(vT_lo_ready, hp * 2 + 1)
                        for b in range(4):
                            tok = slice((4 * n + b) * P, (4 * n + b + 1) * P)
                            last = pe.transpose(ps[:, 7, b * P:(b + 1) * P], tf[:, tok], ident[:])
                        last.then_inc(vT_full, 1)

                    def turn(hp, it, c, par, first):
                        n = CHUNKS_BEFORE[it] + c
                        if c == 0:
                            pe.wait_ge(a_ready, hp * ROWS + (2 * it + 2))
                        if not (first and n < 2):
                            pe.wait_ge(aT_lo_ready, hp * CHUNKS + (n - 1))
                        for kk in range(2):
                            for r in range(2):
                                k = 2 * c + kk
                                last = pe.transpose(ps[:, 4 + n % 2, (2 * kk + r) * P:(2 * kk + r + 1) * P],
                                                    sig[:, it % 2, r, k * P:(k + 1) * P], ident[:])
                        last.then_inc(aT_full, 1)

                    def weighted(hp, it, c, par, first):
                        n, t = CHUNKS_BEFORE[it] + c, it % 4
                        pe.wait_ge(aT_lo_ready, hp * CHUNKS + (n + 1))
                        if c == 0 and not (first and it == 0):
                            pe.wait_ge(o_sum_ready, hp * ITEMS + it)
                        for kk in range(2):
                            v = sv[:, par, 2 * c + kk, it // 4, :]
                            o = ps[:, 6, 0:2 * P]
                            pe.matmul(o, v, aT_hi[:, n % 2, kk, :], start=(c == 0 and kk == 0), stop=False)
                            last = pe.matmul(o, v, aT_lo[:, n % 2, kk, :], start=False, stop=(c == t and kk == 1))
                        last.then_inc(pv_done, 1)

                    def pair(hp, par, last, first=False):
                        steps = [0]

                        def fill(n):
                            while n > 0 and not last:
                                piece, k = divmod(steps[0], KB)
                                k1 = min(k + n, KB)
                                project(hp + 1, piece, range(k, k1))
                                steps[0] += k1 - k
                                n -= k1 - k

                        for it in range(ITEMS):
                            t = it % 4
                            for c in range(min(t + 1, 2)):
                                turn(hp, it, c, par, first)
                            if it == ITEMS - 1 and not last:
                                pe.wait_ge(sqk_lo_ready, hp * 2 + 4)
                            for r in range(2):
                                if it < ITEMS - 1:
                                    z(hp * ROWS + (2 * (it + 1) + r), par, (it + 1) // 4 * SHEAD, r, (it + 1) % 4,
                                      False)
                                elif not last:
                                    z(hp * ROWS + (ROWS + r), 1 - par, 0, r, 0, False)
                                fill(FILL[it][r])
                            if it == 0:
                                pe.wait_ge(vT_lo_ready, hp * 2 + 2)
                            for c in range(t + 1):
                                if c > 0:
                                    fill(FILL[it][c + 1])
                                    if it == ITEMS - 1 and not last and c % 2 == 1:
                                        turn_values(hp + 1, c // 2)
                                weighted(hp, it, c, par, first)
                                if c + 2 <= t:
                                    turn(hp, it, c + 2, par, first)

                    for piece in range(6):
                        project(0, piece, first=True)
                    for n in range(2):
                        turn_values(0, n)
                    pe.wait_ge(sqk_lo_ready, 2)
                    for r in range(2):
                        z(r, 0, 0, r, 0, True)
                    pair(0, 0, False, first=True)
                    with pe.Fori(0, KB // 2 - 1) as d:
                        pair(d * 2 + 1, 1, False)
                        pair(d * 2 + 2, 0, False)
                    pair(KB - 1, 1, True)

                u0, f0, v0 = base["E", i]
                pe.wait_ge(evacuated, v0)

                def out_pair(pm, first):
                    for a in range(2):
                        s = (u0 + a) % WSLOTS
                        pe.wait_ge(w_lo_ready, pm * 3 + (u0 + a + 1))
                        for h in range(2):
                            if not first:
                                pe.wait_ge(evacuated, pm * 4 + (v0 + 2 * a + h - 3))
                            for k in range(KB):
                                if first and a == 0:
                                    pe.wait_ge(mx_lo_ready, 2 * KB * i + KB * h + k + 1)
                                c = slice(k * P, (k + 1) * P)
                                last = three(ps[:, 2 * a + h, :], w_hi[:, s, c], w_lo[:, s, c],
                                             xg_hi[:, k, ln[h]], xg_lo[:, k, ln[h]], k == 0, False)
                        last.then_inc(w_used, 1)
                    s = (u0 + 2) % WSLOTS
                    pe.wait_ge(w_lo_ready, pm * 3 + (u0 + 3))
                    if first:
                        pe.wait_ge(me_lo_ready, MHEADS * (i + 1))
                    for a in range(2):
                        for h in range(2):
                            for k in range(MHEADS):
                                c = slice((2 * k + a) * P, (2 * k + a + 1) * P)
                                last = three(ps[:, 2 * a + h, :], w_hi[:, s, c], w_lo[:, s, c],
                                             me_hi[:, k, ln[h]], me_lo[:, k, ln[h]], False, k == MHEADS - 1)
                            last.then_inc(w_used if a == 1 and h == 1 else bank_full, 1)

                out_pair(0, True)
                with pe.Fori(1, KB // 2) as pm:
                    out_pair(pm, False)

                u0, f0, v0 = base["F", i]
                pe.wait_ge(evacuated, v0)

                def down(n, more, blocks, v, j0):
                    for j in range(2):
                        pe.wait_ge(w_lo_ready, more + (n + j + 1))
                    pe.wait_ge(act_lo_ready, blocks)
                    for q in range(2 * KB):
                        m, h = q // 2, q % 2
                        pe.wait_ge(evacuated, v + (q - 5))
                        for j in range(2):
                            s, c = (n + j) % WSLOTS, slice(m * P, (m + 1) * P)
                            last = three(ps[:, (j0 + q) % 8, :], w_hi[:, s, c], w_lo[:, s, c],
                                         act_hi[:, j, ln[h]], act_lo[:, j, ln[h]], j == 0, j == 1)
                        if q < 2 * KB - 1:
                            last.then_inc(bank_full, 1)
                        else:
                            last.then_inc(w_used, 2)

                unit(u0, 0, lambda h: h, (None, None), first=2 * i + 1)
                unit(u0 + 1, 0, lambda h: 2 + h, (None, None))
                norm(2 * i + 1)
                unit(u0 + 2, 0, lambda h: 6 + h, (None, None))
                unit(u0 + 3, 0, lambda h: h, (v0 + 1, v0 + 2))
                with pe.Fori(0, FGROUPS - 1) as g:
                    n, more, v = u0 + 4, g * 6, g * 24 + (v0 + 8)
                    unit(n, more, lambda h: 2 + h, (v - 5, v - 4))
                    unit(n + 1, more, lambda h: 4 + h, (v - 3, v - 2))
                    down(n + 2, more, g * 2 + (FBLK * i + 2), v + 4, 6)
                    unit(n + 4, more, lambda h: (22 + h) % 8, (v + 15, v + 16))
                    unit(n + 5, more, lambda h: (24 + h) % 8, (v + 17, v + 18))
                ue, fe, ve = base["end", i]
                down(ue - 2, 0, FBLK * (i + 1), ve - 16, 2)


def kernel(x, mem, w_in, w_out, w_mem_kv, w_conv, w_ffn_in, w_ffn_out, g_mix, g_mem, g_ffn, g_q, g_k):
    import concourse.bacc as bacc
    from concourse.bass_utils import run_bass_kernel_spmd

    def blocks(v):
        v = np.asarray(v)
        return np.ascontiguousarray(np.moveaxis(v.reshape(*v.shape[:-1], KB, P), -1, 0))

    weights = [np.asarray(w) for w in (w_in, w_out, w_mem_kv, w_ffn_in, w_ffn_out)]
    arrays = {
        "xT": np.ascontiguousarray(np.asarray(x)[0].reshape(SEQ, KB, P).transpose(2, 1, 0)),
        "memT": np.ascontiguousarray(np.asarray(mem)[0].reshape(NMEM, KB, P).transpose(2, 1, 0)),
        "wpack": pack_weights(*weights),
        "gain": blocks(np.stack([np.asarray(g) for g in (g_mix, g_mem, g_ffn)])),
        "taps": blocks(np.asarray(w_conv)[0]),
        "g_heads": np.ascontiguousarray(np.stack([np.asarray(g_q), np.asarray(g_k)]).transpose(2, 0, 1)),
    }
    nc = bacc.Bacc("TRN2", target_bir_lowering=False, num_devices=1)
    ap = {n: nc.dram_tensor(n, a.shape, F32, kind="ExternalInput").ap() for n, a in arrays.items()}
    out = nc.dram_tensor("out", (P, KB, SEQ), F32, kind="ExternalOutput").ap()
    trunk(nc, ap["xT"], ap["memT"], ap["wpack"], [(n, ap[n]) for n in ("gain", "taps", "g_heads")], out)
    r = run_bass_kernel_spmd(nc, [arrays], core_ids=[0])
    got = np.asarray(r.results[0]["out"])
    return np.ascontiguousarray(got.transpose(2, 1, 0).reshape(1, SEQ, DM))
```

```python
from contextlib import ExitStack

import numpy as np

import concourse.bass as bass
from concourse import mybir

F32 = mybir.dt.float32
F32R = mybir.dt.float32r
ALU = mybir.AluOpType
ACT = mybir.ActivationFunctionType
AX_X = mybir.AxisListType.X

P = 128
SEQ, DM, LAYERS = 1024, 1024, 2
KB = DM // P
HALF = 512
NMEM, MHEADS = 256, 4
SHEAD = 64
FF = 2816
FBLK = FF // P
FGROUPS = FBLK // 2
EPS = 1e-6
UCOLS = KB * P
WSLOTS = 3
MASKED = -1.0e30

A_UNITS = 2 * MHEADS
B_UNITS = MHEADS
C_UNITS = 3 * KB
E_UNITS = 3 * (KB // 2)
F_UNITS = 6 * FGROUPS
LAYER_UNITS = B_UNITS + C_UNITS + E_UNITS + F_UNITS
UNITS = LAYERS * (A_UNITS + LAYER_UNITS)


def pack_weights(w_in, w_out, w_mem_kv, w_ffn_in, w_ffn_out):
    def cols(w, c0, k0=0, kn=KB, n=P):
        return w[k0 * P:(k0 + kn) * P, c0:c0 + n].reshape(kn, P, n).transpose(1, 0, 2).reshape(P, kn * n)

    units = []
    for i in range(LAYERS):
        units += [cols(w_mem_kv[i], c * P) for c in range(MHEADS)]
        units += [cols(w_mem_kv[i], MHEADS * P + g * 2 * P, k0, 4, 2 * P) for g in range(2) for k0 in (0, 4)]
    for i in range(LAYERS):
        units += [cols(w_in[i], 3 * DM + h * P) for h in range(MHEADS)]
        for b in range(KB):
            units += [cols(w_in[i], part * DM + b * P) for part in range(3)]
        for m in range(0, KB, 2):
            units += [cols(w_out[i], m * P), cols(w_out[i], (m + 1) * P),
                      cols(w_out[i], m * P, KB, MHEADS, 2 * P)]

        def gate_up(g, part):
            return [cols(w_ffn_in[i], part * FF + (2 * g + j) * P) for j in range(2)]

        units += gate_up(0, 0) + gate_up(0, 1)
        down = [[w_ffn_out[i, (2 * g + j) * P:(2 * g + j + 1) * P] for j in range(2)] for g in range(FGROUPS)]
        for g in range(1, FGROUPS - 1):
            units += gate_up(g, 0) + down[g - 1] + gate_up(g, 1)
        units += gate_up(FGROUPS - 1, 0) + gate_up(FGROUPS - 1, 1) + down[-2] + down[-1]
    return np.ascontiguousarray(np.stack(units))


def trunk(nc, xT, memT, wpack, vectors, out):
    base = {}
    u = f = v = 0
    for i in range(LAYERS):
        base["A", i] = (u, f, v)
        u, v = u + A_UNITS, v + A_UNITS
    for i in range(LAYERS):
        base["B", i] = (u, f, v)
        u, f, v = u + B_UNITS, f + B_UNITS, v + 2 * B_UNITS
        base["C", i] = (u, f, v)
        u, f, v = u + C_UNITS, f + C_UNITS, v + 2 * C_UNITS
        base["E", i] = (u, f, v)
        u, f, v = u + E_UNITS, f + 3 * (KB // 2), v + 2 * KB
        base["F", i] = (u, f, v)
        u, f, v = u + F_UNITS, f + 4 * FGROUPS + 15 * FGROUPS, v + 24 * FGROUPS
        base["end", i] = (u, f, v)
    assert u == UNITS and u % WSLOTS == 0

    with ExitStack() as ctx:
        arena_bytes = (nc.sbuf_usable_end - nc.sbuf_base) // 32 * 32 - 32
        arena = ctx.enter_context(nc.sbuf_tensor("arena", [P, arena_bytes // 4], F32))
        arena_start = (nc.sbuf_base - arena_bytes)
        cursor = [0]

        def place(name, shape, dt, offset=None):
            size = 4 * int(np.prod(shape[1:]))
            if offset is None:
                offset = cursor[0]
                cursor[0] += (size + 31) // 32 * 32
            assert offset + size <= arena_bytes, (name, offset, size, arena_bytes)
            return nc.alloc_sbuf_tensor_at(name, shape, dt, offset=arena_start + offset)

        def sem(name):
            return ctx.enter_context(nc.semaphore(name))

        x = place("x", [P, KB, SEQ], F32)
        xg_hi = place("xg_hi", [P, KB, SEQ], F32R)
        xg_lo = place("xg_lo", [P, KB, SEQ], F32R)
        raw = place("raw", [P, WSLOTS, UCOLS], F32)
        w_hi = place("w_hi", [P, WSLOTS, UCOLS], F32R)
        w_lo = place("w_lo", [P, WSLOTS, UCOLS], F32R)
        R = place("R", [P, SEQ], F32)
        ident = place("ident", [P, P], F32)
        ident_r = place("ident_r", [P, P], F32R)
        mask_r = place("mask_r", [P, 2 * P], F32R)
        mean_all = place("mean_all", [P, P], F32)
        mean_head = place("mean_head", [P, P], F32)
        gain = place("gain", [P, 3, LAYERS, KB], F32)
        taps = place("taps", [P, 3, KB], F32)
        g_heads = place("g_heads", [P, 2, LAYERS], F32)
        g_qk = place("g_qk", [P, LAYERS], F32)
        eps = place("eps", [P, 1], F32)
        smax = place("smax", [P, 2, 2], F32)
        nbias = place("nbias", [P, 2, 2], F32)
        psums = place("psums", [P, 2, 2], F32)
        rsums = place("rsums", [P, 2, 2], F32)
        mcol = place("mcol", [P, 2], F32)
        mcol_t = place("mcol_t", [P, 2], F32)
        rq_v = place("rq_v", [P, KB], F32)
        rq_s = place("rq_s", [P, KB], F32)
        rq_t = place("rq_t", [P, KB], F32)
        rq = place("rq", [P, 2, KB], F32)
        root = place("root", [P, KB], F32)
        recip = place("recip", [P, KB], F32)
        eps_r2 = place("eps_r2", [P, KB], F32)
        Z = cursor[0]
        K1 = 1024
        squares = [place(f"squares{i}", [P, 2, HALF], F32, Z + (36 if i == 0 else 48) * K1) for i in range(2)]
        diag = place("diag", [P, KB, P], F32, Z + 60 * K1)
        mem = place("mem", [P, KB, NMEM], F32, Z)
        mg_hi = [place("mg_hi0", [P, KB, NMEM], F32R, Z + 8 * K1), place("mg_hi1", [P, KB, NMEM], F32R, Z + 56 * K1)]
        mg_lo = [place("mg_lo0", [P, KB, NMEM], F32R, Z + 16 * K1), place("mg_lo1", [P, KB, NMEM], F32R, Z)]
        kf = place("kf", [P, MHEADS * NMEM], F32, Z + 24 * K1)
        ksq = place("ksq", [P, MHEADS * NMEM], F32, Z + 28 * K1)
        kdiag = place("kdiag", [P, KB, P], F32, Z + 32 * K1)
        ka_hi = place("ka_hi", [P, MHEADS * NMEM], F32R, Z + 40 * K1)
        ka_lo = place("ka_lo", [P, MHEADS * NMEM], F32R, Z + 44 * K1)
        va_hi = place("va_hi", [P, 2, MHEADS * P], F32R, Z + 48 * K1)
        va_lo = place("va_lo", [P, 2, MHEADS * P], F32R, Z + 52 * K1)
        msq = place("msq", [P, KB, NMEM], F32, Z + 56 * K1)
        mr = place("mr", [P, NMEM], F32, Z + 64 * K1)
        mrt = place("mrt", [P, NMEM], F32, Z + 65 * K1)
        mask_f = place("mask_f", [P, 2 * P], F32, Z + 66 * K1)
        q_hi = place("q_hi", [P, 2, SEQ], F32R, Z)
        q_lo = place("q_lo", [P, 2, SEQ], F32R, Z + 8 * K1)
        k_hi = place("k_hi", [P, MHEADS * NMEM], F32R, Z + 16 * K1)
        k_lo = place("k_lo", [P, MHEADS * NMEM], F32R, Z + 20 * K1)
        v_hi = place("v_hi", [P, 2, MHEADS * P], F32R, Z + 24 * K1)
        v_lo = place("v_lo", [P, 2, MHEADS * P], F32R, Z + 28 * K1)
        pT_hi = place("pT_hi", [P, 2, 2, 2 * P], F32R, Z + 32 * K1)
        pT_lo = place("pT_lo", [P, 2, 2, 2 * P], F32R, Z + 36 * K1)
        qsq = place("qsq", [P, 2, SEQ], F32, Z + 40 * K1)
        ME = Z + 48 * K1 + 32
        me_f = place("me_f", [P, MHEADS, SEQ], F32, ME)
        prob = place("prob", [P, 2, 2, NMEM], F32, ME + 16 * K1)
        cb = place("cb", [P, SEQ], F32, Z)
        cc = place("cc", [P, SEQ], F32, Z + 4 * K1)
        cu = place("cu", [P, SEQ], F32, Z + 8 * K1)
        cy = place("cy", [P, SEQ + 2], F32, Z + 12 * K1)
        mix_f = place("mix_f", [P, KB, SEQ], F32, Z + 16 * K1 + 32)
        keep = place("keep", [P, 2, 2, SEQ], F32, 0)
        sig = place("sig", [P, 2, 2, SEQ], F32, 16 * K1)
        sq = place("sq", [P, 3, SEQ], F32R, Z)
        sk = place("sk", [P, 3, SEQ], F32R, Z + 12 * K1)
        sk_lo = place("sk_lo", [P, 2, SEQ], F32R, Z + 24 * K1)
        sv = place("sv", [P, 2, KB, 2, P], F32R, Z + 32 * K1)
        aT_hi = place("aT_hi", [P, 2, 2, 2 * P], F32R, ME)
        aT_lo = place("aT_lo", [P, 2, 2, 2 * P], F32R, ME + 4 * K1)
        o_sum = place("o_sum", [P, 2, 2 * P], F32, ME + 8 * K1)
        o_low = place("o_low", [P, 2 * P], F32, ME + 10 * K1)
        tf = place("tf", [P, SEQ], F32, ME + 16 * K1)
        mx = place("mx", [P, KB, SEQ], F32, 64 * K1)
        me_hi = place("me_hi", [P, MHEADS, SEQ], F32R, Z)
        me_lo = place("me_lo", [P, MHEADS, SEQ], F32R, Z + 16 * K1 + 32)
        act_hi = place("act_hi", [P, 2, SEQ], F32R, Z)
        act_lo = place("act_lo", [P, 2, SEQ], F32R, Z + 8 * K1)
        gate = place("gate", [P, 2, SEQ], F32, Z + 16 * K1)
        up = place("up", [P, 2, SEQ], F32, Z + 24 * K1)
        act_hi2 = place("act_hi2", [P, 2, SEQ], F32R, Z + 32 * K1)
        act_lo2 = place("act_lo2", [P, 2, SEQ], F32R, Z + 40 * K1)

        ps = ctx.enter_context(nc.psum_tensor("ps", [P, 8, HALF], F32))

        def banks(b, n=2):
            return ps[:, b:b + n, :].rearrange("p a c -> p (a c)")

        d_kv = nc.dram_tensor("d_kv", (LAYERS, 4, P, MHEADS * NMEM), F32R, kind="Internal").ap()
        d_me = nc.dram_tensor("d_me", (P, MHEADS, SEQ), F32, kind="Internal").ap()
        d_mix = nc.dram_tensor("d_mix", (KB - 1, P, SEQ), F32, kind="Internal").ap()
        d_x = nc.dram_tensor("d_x", (P, KB, SEQ), F32, kind="Internal").ap()

        consts_in = sem("consts_in")
        x_in = sem("x_in")
        mem_in = [sem(f"mem_in{h}") for h in range(2)]
        consts_made = sem("consts_made")
        ident_steps = sem("ident_steps")
        raw_landed = [sem(f"raw_landed{s}") for s in range(WSLOTS)]
        w_hi_ready = sem("w_hi_ready")
        w_lo_ready = sem("w_lo_ready")
        w_used = sem("w_used")
        bank_full = sem("bank_full")
        evacuated = sem("evacuated")
        xg_hi_ready = sem("xg_hi_ready")
        xg_lo_ready = sem("xg_lo_ready")
        sq_ready = sem("sq_ready")
        acc_added = sem("acc_added")
        stat_full = sem("stat_full")
        root_ready = sem("root_ready")
        recip_ready = sem("recip_ready")
        diag_ready = sem("diag_ready")
        spread = sem("spread")
        r_ready = sem("r_ready")
        eps_r2_ready = sem("eps_r2_ready")
        eps_made = sem("eps_made")
        msq_ready = sem("msq_ready")
        mstat_full = sem("mstat_full")
        mroot_ready = sem("mroot_ready")
        mr_ready = sem("mr_ready")
        gqk_ready = sem("gqk_ready")
        mg_hi_ready = sem("mg_hi_ready")
        mg_lo_ready = sem("mg_lo_ready")
        ksq_ready = sem("ksq_ready")
        kstat_full = sem("kstat_full")
        kroot_ready = sem("kroot_ready")
        kdiag_ready = sem("kdiag_ready")
        kspread = sem("kspread")
        kn_ready = sem("kn_ready")
        ka_hi_ready = sem("ka_hi_ready")
        ka_lo_ready = sem("ka_lo_ready")
        va_hi_ready = sem("va_hi_ready")
        kv_stored = sem("kv_stored")
        kv_loaded = sem("kv_loaded")
        q_hi_ready = sem("q_hi_ready")
        qsq_ready = sem("qsq_ready")
        qstat_full = sem("qstat_full")
        rqv_ready = sem("rqv_ready")
        rqs_ready = sem("rqs_ready")
        rq_step = sem("rq_step")
        rq_ready = sem("rq_ready")
        scores_full = sem("scores_full")
        max_ready = sem("max_ready")
        nbias_ready = sem("nbias_ready")
        exp_done = sem("exp_done")
        rsum_ready = sem("rsum_ready")
        prob_ready = sem("prob_ready")
        pT_full = sem("pT_full")
        pT_hi_ready = sem("pT_hi_ready")
        pT_lo_ready = sem("pT_lo_ready")
        mo_full = sem("mo_full")
        mo_ready = sem("mo_ready")
        me_stored = sem("me_stored")
        conv_step = sem("conv_step")
        x_spilled = sem("x_spilled")
        x_back = sem("x_back")
        z_full = sem("z_full")
        keep_ready = sem("keep_ready")
        sig_ready = sem("sig_ready")
        scanned = sem("scanned")
        a_ready = sem("a_ready")
        aT_full = sem("aT_full")
        aT_hi_ready = sem("aT_hi_ready")
        aT_lo_ready = sem("aT_lo_ready")
        pv_done = sem("pv_done")
        o_low_ready = sem("o_low_ready")
        o_sum_ready = sem("o_sum_ready")
        so_stored = [sem(f"so_stored{p}") for p in range(2)]
        sqk_hi_ready = sem("sqk_hi_ready")
        sqk_lo_ready = sem("sqk_lo_ready")
        vT_full = sem("vT_full")
        vT_hi_ready = sem("vT_hi_ready")
        vT_lo_ready = sem("vT_lo_ready")
        mx_loaded = sem("mx_loaded")
        me_loaded = sem("me_loaded")
        mx_hi_ready = sem("mx_hi_ready")
        mx_lo_ready = sem("mx_lo_ready")
        me_hi_ready = sem("me_hi_ready")
        me_lo_ready = sem("me_lo_ready")
        silu_done = sem("silu_done")
        prod_ready = sem("prod_ready")
        act_hi_ready = sem("act_hi_ready")
        act_lo_ready = sem("act_lo_ready")
        out_stored = sem("out_stored")

        block = ctx.enter_context(nc.Block())

        def fp(ap):
            return ap.bitcast(F32)

        def x_visit(nu, m, h):
            if nu in (1, 3):
                return base["E", nu // 2][2] + 2 * m + h
            return base["end", 0][2] - 2 * KB + 2 * m + h

        def split_order(nu):
            if nu % 2 == 0:
                return [(m, h) for m in range(KB) for h in range(2)]
            return [(m, h) for h in range(2) for m in range(KB - 2)] + \
                   [(m, h) for h in range(2) for m in (KB - 2, KB - 1)]

        def split_count(nu, m, h):
            return 2 * KB * nu + split_order(nu).index((m, h)) + 1

        def head_place(hh, par):
            rows = slice(0, SHEAD), slice(SHEAD, P)
            return (1 + par if hh else 0), rows[hh], rows[1 - hh]

        CHUNKS_BEFORE = [sum(j % 4 + 1 for j in range(it)) for it in range(9)]
        ITEMS, ROWS, CHUNKS = 8, 16, CHUNKS_BEFORE[8]
        FILL = [(3, 3), (2, 2, 2), (4, 1, 1, 1), (0, 2, 1, 1, 1), (3, 3), (2, 2, 2), (4, 2, 1, 1), (0, 4, 0, 0, 0)]
        assert sum(map(sum, FILL)) == 6 * KB
        ENDS = {}
        steps = 0
        for it, counts in enumerate(FILL):
            for place_, n in enumerate(counts):
                for piece in range(6):
                    if steps < KB * (piece + 1) <= steps + n:
                        ENDS[it, place_] = piece
                steps += n
        assert len(ENDS) == 6
        ln = slice(0, HALF), slice(HALF, SEQ)
        mix_order = [(m, h) for h in range(2) for m in range(KB - 1)] + [(KB - 1, h) for h in range(2)]
        BATCHES = 4 * MHEADS

        @block.sync
        def _(sp):
            for name, src in vectors:
                dst = {"gain": gain, "taps": taps, "g_heads": g_heads}[name]
                sp.dma_start(dst[:], src).then_inc(consts_in, 16)
            for s in range(WSLOTS):
                sp.dma_start(raw[:, s, :], wpack[s]).then_inc(raw_landed[s], 16)
                if s == 0:
                    for h in range(2):
                        sp.dma_start(mem[:, 4 * h:4 * h + 4, :], memT[:, 4 * h:4 * h + 4, :]).then_inc(mem_in[h], 16)
            with sp.Fori(1, UNITS // WSLOTS) as i:
                for s in range(WSLOTS):
                    sp.wait_ge(w_lo_ready, i * WSLOTS + (s + 1 - WSLOTS))
                    sp.dma_start(raw[:, s, :], wpack[bass.ds(i * WSLOTS + s, 1)].rearrange("a p c -> (a p) c")
                                 ).then_inc(raw_landed[s], 16)
            v_end = base["end", LAYERS - 1][2] - 2 * KB
            for m in range(KB):
                sp.wait_ge(evacuated, v_end + 2 * m + 2)
                sp.dma_start(out[:, m, :], x[:, m, :]).then_inc(out_stored, 16)
            sp.wait_ge(out_stored, 16 * KB)

        @block.gpsimd
        def _(pool):
            pool.memset(ident[:], 0.0).then_inc(ident_steps, 1)
            pool.memset(mask_f[:], MASKED).then_inc(ident_steps, 1)
            pool.memset(mean_all[:], 1.0 / DM).then_inc(consts_made, 1)
            pool.memset(mean_head[:], 1.0 / P).then_inc(consts_made, 1)
            pool.wait_ge(ident_steps, 2)
            pool.affine_select(out=ident[:], in_=ident[:], compare_op=ALU.not_equal, fill=1.0, base=0,
                               pattern=[[-1, P]], channel_multiplier=1).then_inc(ident_steps, 1)
            pool.affine_select(out=mask_f[:], in_=mask_f[:], compare_op=ALU.is_ge,
                               fill=0.0, base=0, pattern=[[1, 2 * P]], channel_multiplier=-1
                               ).then_inc(ident_steps, 1)

            pool.wait_ge(w_hi_ready, 3)
            for h in range(2):
                pool.dma_start(x[:, :, ln[h]], xT[:, :, ln[h]]).then_inc(x_in, 16)

            def add_squares(nu, m):
                for h in range(2):
                    n = 2 * KB * nu + 2 * m + h
                    pool.wait_ge(sq_ready, n + 1)
                    if m > 0:
                        pool.wait_ge(acc_added, n - 1)
                        pool.tensor_tensor(R[:, ln[h]], R[:, ln[h]], squares[min(nu, 1)][:, h, :], ALU.add
                                           ).then_inc(acc_added, 1)
                    else:
                        if nu % 2 == 1:
                            pool.wait_ge(evacuated, base["E", nu // 2][2])
                        pool.tensor_copy(R[:, ln[h]], squares[min(nu, 1)][:, h, :]).then_inc(acc_added, 1)

            for i in range(LAYERS):
                for m in range(MHEADS * i, MHEADS * (i + 1)):
                    add_squares(0, m)
                pool.wait_ge(ka_lo_ready, i + 1)
                pool.wait_ge(evacuated, base["A", i][2] + A_UNITS)
                for n, t in enumerate((ka_hi, ka_lo)):
                    pool.dma_start(d_kv[i, n], t[:]).then_inc(kv_stored, 16)
                for n, t in enumerate((va_hi, va_lo)):
                    pool.dma_start(d_kv[i, 2 + n], t[:].rearrange("p a c -> p (a c)")).then_inc(kv_stored, 16)
                pool.wait_ge(kv_stored, 64 * (i + 1))

            for i in range(LAYERS):
                if i > 0:
                    for m in range(KB):
                        add_squares(2 * i, m)
                    pool.wait_ge(evacuated, base["end", i - 1][2])
                for n, t in enumerate((k_hi, k_lo)):
                    pool.dma_start(t[:], d_kv[i, n]).then_inc(kv_loaded, 16)
                for n, t in enumerate((v_hi, v_lo)):
                    pool.dma_start(t[:].rearrange("p a c -> p (a c)"), d_kv[i, 2 + n]).then_inc(kv_loaded, 16)
                if i % 2 == 1:
                    pool.wait_ge(xg_lo_ready, 2 * KB * (2 * i + 1))
                    pool.wait_ge(acc_added, 2 * KB * (2 * i + 1))
                    pool.dma_start(d_x, x[:]).then_inc(x_spilled, 16)
                    for h in range(MHEADS):
                        pool.wait_ge(mo_ready, BATCHES * i + 4 * h + 4)
                        pool.dma_start(d_me[:, h, :], me_f[:, h, :]).then_inc(me_stored, 16)

                    def weigh(row, par, r, t):
                        n = 2 * P * (t + 1)
                        pool.wait_ge(scanned, row + 1)
                        pool.wait_ge(sig_ready, row + 1)
                        pool.tensor_tensor(sig[:, par, r, 0:n - 1], sig[:, par, r, 0:n - 1],
                                           keep[:, par, r, 1:n], ALU.mult).then_inc(a_ready, 1)

                    def pair(hp, last):
                        for it in range(ITEMS):
                            if not (last and it == ITEMS - 1):
                                for r in range(1 if last else 2):
                                    weigh(hp * ROWS + (2 * (it + 1) + r), (it + 1) % 2, r, (it + 1) % 4)
                            if not last:
                                rows = slice(it // 4 * SHEAD, (it // 4 + 1) * SHEAD)
                                toks = slice(it % 4 * 2 * P, (it % 4 + 1) * 2 * P)
                                pool.wait_ge(o_sum_ready, hp * ITEMS + (it + 1))
                                pool.dma_start(d_mix[bass.ds(hp, 1), rows, toks].rearrange("a p c -> (a p) c"),
                                               o_sum[rows, it % 2, :]).then_inc(so_stored[it % 2], 16)
                            elif it == 1:
                                for p in range(2):
                                    pool.wait_ge(so_stored[p], 16 * ITEMS // 2 * (KB - 1))
                                pool.wait_ge(w_used, base["E", i][0])
                                pool.dma_start(mx[:, 0:KB - 1, :], d_mix.rearrange("b p c -> p b c")
                                               ).then_inc(mx_loaded, 16)

                    for r in range(2):
                        weigh(r, 0, r, 0)
                    with pool.Fori(0, KB - 1) as hp:
                        pair(hp, False)
                    pair(KB - 1, True)

                for m in range(KB - 2):
                    add_squares(2 * i + 1, m)

        @block.scalar
        def _(act):
            def prep(u, more=0, rounds=0):
                s = u % WSLOTS
                if u >= UNITS:
                    return
                act.wait_ge(raw_landed[s], rounds * 16 + (u // WSLOTS + 1) * 16)
                if u >= WSLOTS:
                    act.wait_ge(w_used, more + (u - WSLOTS + 1))
                act.activation(w_hi[:, s, :], raw[:, s, :], ACT.Copy).then_inc(w_hi_ready, 1)

            def split(nu, m, h):
                i, g = nu // 2, 2 * (nu % 2)
                if nu == 0:
                    act.wait_ge(x_in, 32)
                elif nu == 2:
                    act.wait_ge(evacuated, base["end", 0][2] - 2 * KB + 2 * m + h + 1)
                else:
                    act.wait_ge(w_used, base["F", i][0] - 1)
                    act.wait_ge(evacuated, base["E", i][2] + 2 * m + h + 1)
                act.activation(xg_hi[:, m, ln[h]], x[:, m, ln[h]], ACT.Copy, scale=gain[:, g, i, m:m + 1]
                               ).then_inc(xg_hi_ready, 1)

            def square(nu, m):
                for h in range(2):
                    n = 2 * KB * nu + 2 * m + h
                    if n >= 2:
                        act.wait_ge(acc_added, n - 1)
                    act.activation(squares[min(nu, 1)][:, h, :], x[:, m, ln[h]], ACT.Square).then_inc(sq_ready, 1)

            def norm_root(nu):
                act.wait_ge(stat_full, nu + 1)
                act.activation(root[:], ps[:, 5, 0:KB], ACT.Sqrt, bias=eps[:, 0:1]).then_inc(root_ready, 1)

            def norm_spread(nu):
                act.wait_ge(spread, nu + 1)
                act.activation(R[:], banks(4), ACT.Copy, scale=float(P)).then_inc(r_ready, 1)

            act.wait_ge(ident_steps, 4)
            act.activation(ident_r[:], ident[:], ACT.Copy).then_inc(consts_made, 1)
            act.activation(mask_r[:], mask_f[:], ACT.Copy).then_inc(consts_made, 1)

            prep(0)
            act.wait_ge(consts_in, 48)
            for m in range(KB):
                if m % 4 == 0:
                    act.wait_ge(mem_in[m // 4], 16)
                act.activation(mg_hi[0][:, m, :], mem[:, m, :], ACT.Copy, scale=gain[:, 1, 0, m:m + 1]
                               ).then_inc(mg_hi_ready, 1)
            prep(1)
            act.activation(msq[:], mem[:], ACT.Square).then_inc(msq_ready, 1)
            prep(2)
            act.wait_ge(mstat_full, 1)
            act.wait_ge(eps_made, 1)
            act.activation(mrt[:], ps[:, 4, 0:NMEM], ACT.Sqrt, bias=eps[:, 0:1]).then_inc(mroot_ready, 1)
            act.activation(mcol_t[:], ps[:, 5, 0:2], ACT.Sqrt, bias=eps[:, 0:1]).then_inc(mroot_ready, 1)
            for m in range(KB):
                act.activation(mg_hi[1][:, m, :], mem[:, m, :], ACT.Copy, scale=gain[:, 1, 1, m:m + 1]
                               ).then_inc(mg_hi_ready, 1)
            act.wait_ge(mr_ready, 2)

            def key_hi(i):
                act.wait_ge(kn_ready, i + 1)
                act.activation(ka_hi[:], kf[:], ACT.Copy).then_inc(ka_hi_ready, 1)

            for i in range(LAYERS):
                u0, f0, v0 = base["A", i]
                for n in range(MHEADS):
                    if i > 0 or n > 0:
                        prep(u0 + n + 2)
                    if i > 0:
                        for h in range(2):
                            split(0, MHEADS + n, h)
                        square(0, n)
                if i > 0:
                    key_hi(i - 1)
                act.wait_ge(evacuated, v0 + MHEADS)
                act.activation(ksq[:], kf[:], ACT.Square).then_inc(ksq_ready, 1)
                for g in range(2):
                    for n in (2 * g, 2 * g + 1):
                        prep(u0 + MHEADS + n + 2)
                        if i == 0:
                            for h in range(2):
                                split(0, n, h)
                        else:
                            square(0, MHEADS + n)
                    act.wait_ge(w_used, u0 + MHEADS + 2 * g + 2)
                    if i > 0:
                        act.wait_ge(kv_stored, 64 * i)
                    for mb in range(2):
                        act.activation(va_hi[:, mb, g * 2 * P:(g + 1) * 2 * P], ps[:, 6 - 2 * g + mb, 0:2 * P],
                                       ACT.Copy, scale=mcol[:, mb:mb + 1]).then_inc(va_hi_ready, 1)
                act.wait_ge(kstat_full, i + 1)
                act.activation(root[:], ps[:, 6, 0:KB], ACT.Sqrt, bias=eps[:, 0:1]).then_inc(kroot_ready, 1)

            for i in range(LAYERS):
                u0, f0, v0 = base["B", i]
                if i == 0:
                    key_hi(LAYERS - 1)
                else:
                    for m in range(KB):
                        square(2 * i, m)
                        if m in (2, 4):
                            prep(u0 + 1 + m // 2)
                if i == 0:
                    prep(u0 + 2)
                    prep(u0 + 3)

                def query_half(h, half):
                    hd = MHEADS * i + h
                    if half == 0:
                        act.wait_ge(bank_full, f0 + h + 1)
                    else:
                        act.wait_ge(w_used, u0 + h + 1)
                    if h >= 2:
                        act.wait_ge(scores_full, BATCHES * i + 4 * (h - 1))
                    if hd >= 2:
                        act.wait_ge(qstat_full, hd - 1)
                    b = (6 if h == 1 else 0) + half
                    act.activation(q_hi[:, h % 2, ln[half]], ps[:, b, :], ACT.Copy).then_inc(q_hi_ready, 1)
                    act.activation(qsq[:, h % 2, ln[half]], ps[:, b, :], ACT.Square).then_inc(qsq_ready, 1)

                def query_root(h):
                    act.wait_ge(rqv_ready, MHEADS * i + h + 1)
                    act.activation(rq_s[:], rq_v[:], ACT.Sqrt).then_inc(rqs_ready, 1)

                def exps(n):
                    h, b, g = n // 4, n % 2, BATCHES * i + n
                    act.wait_ge(nbias_ready, g + 1)
                    if g >= 2:
                        act.wait_ge(pT_full, g - 1)
                    for j in range(2):
                        tb = 2 * (n % 4) + j
                        act.activation(prob[:, b, j, :], ps[:, 4 + b, j * NMEM:(j + 1) * NMEM], ACT.Exp,
                                       bias=nbias[:, b, j:j + 1], scale=rq[:, h % 2, tb:tb + 1],
                                       accum_out=psums[:, b, j:j + 1]).then_inc(exp_done, 1)

                if i == 0:
                    act.wait_ge(kv_stored, 64 * LAYERS)
                for h in range(2):
                    for half in range(2):
                        query_half(h, half)
                norm_root(2 * i)
                query_root(0)
                query_root(1)
                norm_spread(2 * i)
                prep(u0 + 4)
                exps(0)
                for n in range(BATCHES):
                    b, g = n % 2, BATCHES * i + n
                    if n in (2, 4, 6, 8):
                        query_half(2 + (n - 2) // 4, (n // 2 + 1) % 2)
                    if n == 5:
                        prep(u0 + 5)
                    if n in (6, 10):
                        query_root(n // 4 + 1)
                    if n + 1 < BATCHES:
                        exps(n + 1)
                    act.wait_ge(pT_full, g + 1)
                    if g >= 2:
                        act.wait_ge(mo_full, g - 1)
                    act.activation(pT_hi[:, b].rearrange("p a c -> p (a c)"), ps[:, 6 + b, :], ACT.Copy
                                   ).then_inc(pT_hi_ready, 1)
                    for done in ([n - 1] if n > 0 else []) + ([n] if n == BATCHES - 1 else []):
                        act.wait_ge(mo_full, BATCHES * i + done + 1)
                        act.activation(me_f[:, done // 4, done % 4 * 2 * P:(done % 4 + 1) * 2 * P], ps[:, 2, 0:2 * P],
                                       ACT.Copy).then_inc(mo_ready, 1)

                u0, f0, v0 = base["C", i]
                if i % 2 == 0:
                    with act.Fori(0, KB) as b:
                        for j in range(3):
                            prep(u0 + j + 2, b * 3, b)
                else:
                    def sigmoids(row, par, r, t):
                        n = 2 * P * (t + 1)
                        act.wait_ge(z_full, row + 1)
                        z = banks(2 * r)[:, 0:n]
                        act.activation(keep[:, par, r, 0:n], z, ACT.Sigmoid, scale=-1.0).then_inc(keep_ready, 1)
                        act.activation(sig[:, par, r, 0:n], z, ACT.Sigmoid).then_inc(sig_ready, 1)

                    def project(hp, to, piece, b=7):
                        if piece < 4:
                            act.wait_ge(evacuated, hp * 6 + (v0 + piece + 1))
                            half = ln[piece % 2]
                            for other in range(1 + piece // 2):
                                for hh in range(2):
                                    slot, rows, twin = head_place(hh, to)
                                    dst = (sq, sk)[piece // 2]
                                    act.activation(dst[twin if other else rows, slot, half], tf[rows, half], ACT.Copy
                                                   ).then_inc(sqk_hi_ready, 1)
                        if piece >= 6:
                            act.wait_ge(vT_full, hp * 2 + (piece - 5))
                            dst = sv[:, to, 4 * (piece - 6):4 * (piece - 5), :, 0:SHEAD]
                            act.activation(dst, ps[:, b, :].rearrange("p (b h c) -> p b h c", b=4, h=2), ACT.Copy
                                           ).then_inc(vT_hi_ready, 1)

                    def chunk(hp, it, c, first):
                        n = CHUNKS_BEFORE[it] + c
                        act.wait_ge(aT_full, hp * CHUNKS + (n + 1))
                        if not (first and n < 2):
                            act.wait_ge(pv_done, hp * CHUNKS + (n - 1))
                        act.activation(aT_hi[:, n % 2].rearrange("p a c -> p (a c)"), ps[:, 4 + n % 2, :],
                                       ACT.Copy).then_inc(aT_hi_ready, 1)

                    def pair(hp, par, last, first=False):
                        for it in range(ITEMS):
                            t, hh = it % 4, it // 4
                            for c in range(min(t + 1, 2)):
                                chunk(hp, it, c, first)
                            if not (last and it == ITEMS - 1):
                                for r in range(2):
                                    sigmoids(hp * ROWS + (2 * (it + 1) + r), (it + 1) % 2, r, (it + 1) % 4)
                            if not last and it in (0, 3, 7):
                                prep(u0 + 5 + (it + 1) // 4, hp * 3, hp)
                            if not last and it in (4, 5):
                                project(hp + 1, 1 - par, it - 2)
                            for c in range(2, t + 1):
                                chunk(hp, it, c, first)
                                if it == ITEMS - 1 and not last:
                                    project(hp + 1, 1 - par, 4 + c)
                            rows = slice(hh * SHEAD, (hh + 1) * SHEAD)
                            act.wait_ge(pv_done, hp * CHUNKS + CHUNKS_BEFORE[it + 1])
                            if not (first and it == 0):
                                act.wait_ge(o_sum_ready, hp * ITEMS + it)
                            act.activation(o_low[rows, :], ps[SHEAD:P, 6, 0:2 * P], ACT.Copy
                                           ).then_inc(o_low_ready, 1)
                            if not last and it in (1, 2):
                                project(hp + 1, 1 - par, it - 1)

                    for piece in range(4):
                        if piece in (0, 2):
                            prep(u0 + 2 + piece // 2)
                        project(0, 0, piece, piece)
                    prep(u0 + 4)
                    act.wait_ge(x_spilled, 16)
                    for r in range(2):
                        sigmoids(r, 0, r, 0)
                    for piece in (6, 7):
                        project(0, 0, piece, piece)
                    act.wait_ge(me_stored, 16 * MHEADS)
                    pair(0, 0, False, first=True)
                    with act.Fori(0, KB // 2 - 1) as d:
                        pair(d * 2 + 1, 1, False)
                        pair(d * 2 + 2, 0, False)
                    pair(KB - 1, 1, True)

                u0, f0, v0 = base["E", i]
                if i % 2 == 0:
                    source = mix_f
                    act.wait_ge(conv_step, 5 * (KB - 1) + 1)
                    act.wait_ge(w_used, u0)
                else:
                    source = mx
                    act.wait_ge(o_sum_ready, ITEMS * KB)
                    act.dma_start(me_f[:], d_me).then_inc(me_loaded, 16)
                    act.dma_start(x[:], d_x).then_inc(x_back, 16)
                    act.wait_ge(mx_loaded, 16)
                for m, h in mix_order:
                    if m == KB - 1:
                        if i % 2 == 0:
                            act.wait_ge(conv_step, 5 * KB + 1)
                        else:
                            act.wait_ge(o_sum_ready, ITEMS * KB)
                    act.activation(xg_hi[:, m, ln[h]], source[:, m, ln[h]], ACT.Copy).then_inc(mx_hi_ready, 1)
                prep(u0 + 2)
                if i % 2 == 1:
                    act.wait_ge(me_loaded, 16)
                for m in range(MHEADS):
                    act.activation(me_hi[:, m, :], me_f[:, m, :], ACT.Copy).then_inc(me_hi_ready, 1)
                prep(u0 + 3)
                prep(u0 + 4)
                with act.Fori(1, KB // 2) as pm:
                    for j in range(3):
                        prep(u0 + j + 2, pm * 3, pm)

                u0, f0, v0 = base["F", i]
                nu, a0 = 2 * i + 1, FBLK * i
                for m, h in split_order(nu):
                    split(nu, m, h)
                prep(u0 + 2)
                for m in range(KB):
                    square(nu, m)
                    if m == KB // 2:
                        prep(u0 + 3)
                norm_root(nu)
                norm_spread(nu)

                def silu(blk, blocks, visits):
                    act.wait_ge(evacuated, visits)
                    act.activation(gate[:, blk, :], gate[:, blk, :], ACT.Silu).then_inc(silu_done, 1)

                def products(blocks, dst=act_hi):
                    for blk in range(2):
                        act.wait_ge(prod_ready, blocks + (blk + 1))
                        act.activation(dst[:, blk, :], up[:, blk, :], ACT.Copy).then_inc(act_hi_ready, 1)

                silu(0, a0, v0 + 2)
                silu(1, a0, v0 + 4)
                prep(u0 + 4)
                prep(u0 + 5)
                products(a0)
                with act.Fori(0, FGROUPS - 2) as g:
                    n, v = u0 + 4, g * 24 + (v0 + 8)
                    prep(n + 2, g * 6, g * 2)
                    silu(0, None, v + 2)
                    prep(n + 3, g * 6, g * 2)
                    silu(1, None, v + 4)
                    for j in (4, 5, 6, 7):
                        prep(n + j, g * 6, g * 2)
                    products(g * 2 + (a0 + 2))
                n, v = u0 + 4 + 6 * (FGROUPS - 2), v0 + 8 + 24 * (FGROUPS - 2)
                prep(n + 2)
                silu(0, None, v + 2)
                prep(n + 3)
                silu(1, None, v + 4)
                prep(n + 4)
                prep(n + 5)
                products(a0 + FBLK - 2, act_hi2)
                prep(n + 6)
                prep(n + 7)
                prep(base["end", i][0])
                if i + 1 < LAYERS:
                    for m, h in split_order(nu + 1):
                        split(nu + 1, m, h)
                    prep(base["end", i][0] + 1)

        @block.vector
        def _(dve):
            def prep(u, more=0, rounds=0):
                s = u % WSLOTS
                if u >= UNITS:
                    return
                dve.wait_ge(w_hi_ready, more + (u + 1))
                dve.tensor_tensor(w_lo[:, s, :], raw[:, s, :], fp(w_hi[:, s, :]), ALU.subtract
                                  ).then_inc(w_lo_ready, 1)

            def split(nu, m, h):
                i, g = nu // 2, 2 * (nu % 2)
                dve.wait_ge(xg_hi_ready, split_count(nu, m, h))
                dve.scalar_tensor_tensor(xg_lo[:, m, ln[h]], x[:, m, ln[h]], gain[:, g, i, m:m + 1],
                                         fp(xg_hi[:, m, ln[h]]), ALU.mult, ALU.subtract).then_inc(xg_lo_ready, 1)

            def reciprocals(ready, done):
                dve.wait_ge(ready[0], ready[1])
                if done > 1:
                    dve.wait_ge(recip_ready, done - 1)
                dve.reciprocal(recip[:], root[:]).then_inc(recip_ready, 1)
                dve.wait_ge(recip_ready, done)

            def diagonal(dst, signal):
                dve.tensor_tensor(dst[:], ident[:].unsqueeze(1).to_broadcast([P, KB, P]),
                                  recip[:].unsqueeze(2).to_broadcast([P, KB, P]), ALU.mult).then_inc(signal, 1)

            def norm(nu):
                reciprocals((root_ready, nu + 1), LAYERS + nu + 1)
                diagonal(diag, diag_ready)

            def scaled(dst, b, h):
                dve.tensor_tensor(dst, ps[:, b, :], R[:, ln[h]], ALU.mult).then_inc(evacuated, 1)

            dve.memset(eps[:], EPS).then_inc(eps_made, 1)

            dve.wait_ge(consts_in, 48)

            def memory_lo(i):
                for m in range(KB):
                    dve.wait_ge(mg_hi_ready, KB * i + m + 1)
                    dve.scalar_tensor_tensor(mg_lo[i][:, m, :], mem[:, m, :], gain[:, 1, i, m:m + 1],
                                             fp(mg_hi[i][:, m, :]), ALU.mult, ALU.subtract).then_inc(mg_lo_ready, 1)

            prep(0)
            memory_lo(0)
            prep(1)
            dve.scalar_tensor_tensor(g_qk[:], g_heads[:, 0, :], float(P) ** 0.5, g_heads[:, 1, :],
                                     ALU.mult, ALU.mult).then_inc(gqk_ready, 1)
            prep(2)
            dve.wait_ge(mroot_ready, 2)
            dve.reciprocal(mr[:], mrt[:]).then_inc(mr_ready, 1)
            dve.reciprocal(mcol[:], mcol_t[:]).then_inc(mr_ready, 1)
            memory_lo(1)
            dve.wait_ge(mr_ready, 2)
            dve.wait_ge(gqk_ready, 1)

            def normed_keys(i):
                dve.wait_ge(kspread, i + 1)
                dve.wait_ge(evacuated, base["A", i][2] + MHEADS)
                dve.scalar_tensor_tensor(kf[:], kf[:], g_qk[:, i:i + 1], banks(6), ALU.mult, ALU.mult
                                         ).then_inc(kn_ready, 1)
                dve.wait_ge(ka_hi_ready, i + 1)
                if i > 0:
                    dve.wait_ge(kv_stored, 64 * i)
                dve.tensor_tensor(ka_lo[:], kf[:], fp(ka_hi[:]), ALU.subtract).then_inc(ka_lo_ready, 1)
                dve.wait_ge(ka_lo_ready, i + 1)

            for i in range(LAYERS):
                u0, f0, v0 = base["A", i]

                def keys_out(n):
                    dve.wait_ge(w_used, u0 + n + 1)
                    dve.tensor_tensor(kf[:, n * NMEM:(n + 1) * NMEM], ps[:, n, 0:NMEM], mr[:], ALU.mult
                                      ).then_inc(evacuated, 1)

                for n in range(MHEADS):
                    if i > 0 or n > 0:
                        prep(u0 + n + 2)
                    if i > 0:
                        for h in range(2):
                            split(0, MHEADS + n, h)
                    else:
                        keys_out(n)
                if i > 0:
                    normed_keys(i - 1)
                    for n in range(MHEADS):
                        keys_out(n)
                for g in range(2):
                    for n in (2 * g, 2 * g + 1):
                        prep(u0 + MHEADS + n + 2)
                        if i == 0:
                            for h in range(2):
                                split(0, n, h)
                    for mb in range(2):
                        dve.wait_ge(va_hi_ready, MHEADS * i + 2 * g + mb + 1)
                        cols = slice(g * 2 * P, (g + 1) * 2 * P)
                        dve.scalar_tensor_tensor(
                            va_lo[:, mb, cols], ps[:, 6 - 2 * g + mb, 0:2 * P], mcol[:, mb:mb + 1],
                            fp(va_hi[:, mb, cols]), ALU.mult, ALU.subtract).then_inc(evacuated, 1)
                reciprocals((kroot_ready, i + 1), i + 1)
                diagonal(kdiag, kdiag_ready)

            for i in range(LAYERS):
                u0, f0, v0 = base["B", i]
                if i == 0:
                    normed_keys(LAYERS - 1)
                prep(u0 + 2)
                prep(u0 + 3)

                def query_half(h, half):
                    hd = MHEADS * i + h
                    dve.wait_ge(qsq_ready, 2 * hd + half + 1)
                    dve.tensor_tensor(q_lo[:, h % 2, ln[half]], ps[:, (6 if h == 1 else 0) + half, :],
                                      fp(q_hi[:, h % 2, ln[half]]), ALU.subtract).then_inc(evacuated, 1)

                def query_root(h):
                    hd = MHEADS * i + h
                    dve.wait_ge(qstat_full, hd + 1)
                    if hd > 0:
                        dve.wait_ge(rq_ready, hd)
                    dve.tensor_tensor(rq_v[:], ps[:, 3, 0:KB], eps_r2[:], ALU.add).then_inc(rqv_ready, 1)
                    dve.wait_ge(rqs_ready, hd + 1)
                    y, s0 = rq[:, h % 2, :], 4 * hd
                    dve.reciprocal(y, rq_s[:]).then_inc(rq_step, 1)
                    dve.wait_ge(rq_step, s0 + 1)
                    dve.tensor_tensor(rq_t[:], rq_v[:], y, ALU.mult).then_inc(rq_step, 1)
                    dve.wait_ge(rq_step, s0 + 2)
                    dve.tensor_tensor(rq_t[:], rq_t[:], y, ALU.mult).then_inc(rq_step, 1)
                    dve.wait_ge(rq_step, s0 + 3)
                    dve.tensor_scalar(rq_t[:], rq_t[:], -0.5, 1.5, ALU.mult, ALU.add).then_inc(rq_step, 1)
                    dve.wait_ge(rq_step, s0 + 4)
                    dve.tensor_tensor(y, y, rq_t[:], ALU.mult).then_inc(rq_ready, 1)
                    dve.wait_ge(rq_ready, hd + 1)

                def maxima(n):
                    h, b, g = n // 4, n % 2, BATCHES * i + n
                    dve.wait_ge(scores_full, g + 1)
                    if g >= 2:
                        dve.wait_ge(nbias_ready, g - 1)
                    dve.tensor_reduce(smax[:, b, :], ps[:, 4 + b, :].rearrange("p (j c) -> p j c", j=2), AX_X, ALU.max
                                      ).then_inc(max_ready, 1)
                    dve.wait_ge(max_ready, g + 1)
                    if g >= 2:
                        dve.wait_ge(exp_done, 2 * (g - 1))
                    tb = 2 * (n % 4)
                    dve.scalar_tensor_tensor(nbias[:, b, :], smax[:, b, :], -1.0, rq[:, h % 2, tb:tb + 2],
                                             ALU.mult, ALU.mult).then_inc(nbias_ready, 1)

                def normalize(n):
                    b, g = n % 2, BATCHES * i + n
                    dve.wait_ge(exp_done, 2 * g + 2)
                    if g >= 2:
                        dve.wait_ge(prob_ready, g - 1)
                    dve.reciprocal(rsums[:, b, :], psums[:, b, :]).then_inc(rsum_ready, 1)
                    dve.wait_ge(rsum_ready, g + 1)
                    dve.tensor_tensor(prob[:, b], prob[:, b], rsums[:, b, :].unsqueeze(2).to_broadcast([P, 2, NMEM]),
                                      ALU.mult).then_inc(prob_ready, 1)

                for h in range(2):
                    for half in range(2):
                        query_half(h, half)
                dve.wait_ge(root_ready, 2 * i + 1)
                dve.tensor_scalar(eps_r2[:], ps[:, 5, 0:KB], EPS, EPS, ALU.add, ALU.mult).then_inc(eps_r2_ready, 1)
                dve.wait_ge(eps_r2_ready, i + 1)
                norm(2 * i)
                query_root(0)
                query_root(1)
                prep(u0 + 4)
                maxima(0)
                maxima(1)
                normalize(0)
                for n in range(BATCHES):
                    b, g = n % 2, BATCHES * i + n
                    if n in (2, 4, 6, 8):
                        query_half(2 + (n - 2) // 4, (n // 2 + 1) % 2)
                    if n == 5:
                        prep(u0 + 5)
                    if n in (6, 10):
                        query_root(n // 4 + 1)
                    if n + 2 < BATCHES:
                        maxima(n + 2)
                    if n + 1 < BATCHES:
                        normalize(n + 1)
                    dve.wait_ge(pT_hi_ready, g + 1)
                    dve.tensor_tensor(pT_lo[:, b].rearrange("p a c -> p (a c)"), ps[:, 6 + b, :],
                                      fp(pT_hi[:, b].rearrange("p a c -> p (a c)")), ALU.subtract
                                      ).then_inc(pT_lo_ready, 1)

                u0, f0, v0 = base["C", i]
                dve.wait_ge(r_ready, 2 * i + 1)
                if i % 2 == 0:
                    dve.memset(cy[:, 0:2], 0.0).then_inc(conv_step, 1)

                    def block_out(b):
                        dve.wait_ge(conv_step, b * 5 + 1)
                        for j, dst in enumerate((cb, cc, cu)):
                            prep(u0 + j + 2, b * 3)
                            for h in range(2):
                                if h == 0:
                                    dve.wait_ge(bank_full, b * 3 + (f0 + j + 1))
                                else:
                                    dve.wait_ge(w_used, b * 3 + (u0 + j + 1))
                                scaled(dst[:, ln[h]], 2 * j + h, h)

                    def convolve(b, at):
                        dve.wait_ge(evacuated, b * 6 + (base["C", i][2] + 6))
                        dve.tensor_tensor(cy[:, 2:], cu[:], cc[:], ALU.mult).then_inc(conv_step, 1)
                        dve.wait_ge(conv_step, b * 5 + 2)
                        mixed = mix_f[:, at, :].rearrange("p a c -> p (a c)")
                        dve.tensor_scalar(mixed, cy[:, 2:], taps[:, 2, at], None, ALU.mult).then_inc(conv_step, 1)
                        for j in (1, 0):
                            dve.wait_ge(conv_step, b * 5 + (4 - j))
                            dve.scalar_tensor_tensor(mixed, cy[:, j:j + SEQ], taps[:, j, at], mixed,
                                                     ALU.mult, ALU.add).then_inc(conv_step, 1)
                        dve.wait_ge(conv_step, b * 5 + 5)
                        dve.tensor_tensor(mixed, mixed, cb[:], ALU.mult).then_inc(conv_step, 1)

                    with dve.Fori(0, KB - 1) as b:
                        block_out(b)
                        convolve(b, bass.ds(b, 1))
                    block_out(KB - 1)
                else:
                    def scan(row, par, r, t):
                        n = 2 * P * (t + 1)
                        dve.wait_ge(keep_ready, row + 1)
                        k = keep[:, par, r, 0:n][:, ::-1]
                        dve.tensor_tensor_scan(k, k, k, 1.0, ALU.mult, ALU.bypass).then_inc(scanned, 1)

                    def project(hp, piece, b=7):
                        part, h = piece // 2, piece % 2
                        if h == 0:
                            dve.wait_ge(bank_full, hp * 3 + (f0 + part + 1))
                        else:
                            dve.wait_ge(w_used, hp * 3 + (u0 + part + 1))
                        if part > 0:
                            dve.wait_ge(sqk_lo_ready, hp * 8 + (4 * part - 2 + 2 * h))
                        if part == 2:
                            dve.wait_ge(sqk_hi_ready, hp * 12 + (8 + 4 * h))
                        if part == 0:
                            dve.scalar_tensor_tensor(tf[:, ln[h]], ps[:, b, :], float(SHEAD) ** -0.5,
                                                     R[:, ln[h]], ALU.mult, ALU.mult).then_inc(evacuated, 1)
                        else:
                            scaled(tf[:, ln[h]], b, h)

                    def lo_part(hp, to, piece):
                        part, half = piece // 2, ln[piece % 2]
                        for hh in range(2):
                            slot, rows, twin = head_place(hh, to)
                            hi, lo = ((sq[rows, slot, half], sq[twin, slot, half]),
                                      (sk[rows, slot, half], sk_lo[rows, to, half]))[part]
                            dve.wait_ge(sqk_hi_ready, hp * 12 + ((2, 4)[part] * piece - 4 * part + hh + 1))
                            dve.tensor_tensor(lo, tf[rows, half], fp(hi), ALU.subtract).then_inc(sqk_lo_ready, 1)

                    def values(hp, to, n, b=7):
                        blocks = slice(4 * n, 4 * n + 4)
                        dve.wait_ge(vT_hi_ready, hp * 2 + (n + 1))
                        dve.tensor_tensor(sv[:, to, blocks, :, SHEAD:], ps[:, b, :].rearrange(
                            "p (b h c) -> p b h c", b=4, h=2), fp(sv[:, to, blocks, :, 0:SHEAD]), ALU.subtract
                                          ).then_inc(vT_lo_ready, 1)

                    def chunk(hp, it, c):
                        n = CHUNKS_BEFORE[it] + c
                        dve.wait_ge(aT_hi_ready, hp * CHUNKS + (n + 1))
                        dve.tensor_tensor(aT_lo[:, n % 2].rearrange("p a c -> p (a c)"), ps[:, 4 + n % 2, :],
                                          fp(aT_hi[:, n % 2].rearrange("p a c -> p (a c)")), ALU.subtract
                                          ).then_inc(aT_lo_ready, 1)

                    def pair(hp, par, last, first=False):
                        for it in range(ITEMS):
                            t, hh = it % 4, it // 4

                            def finished(n):
                                if not last and (it, n) in ENDS:
                                    project(hp + 1, ENDS[it, n])

                            for c in range(min(t + 1, 2)):
                                chunk(hp, it, c)
                            if not (last and it == ITEMS - 1):
                                for r in range(2):
                                    row, n = hp * ROWS + (2 * (it + 1) + r), 2 * P * ((it + 1) % 4 + 1)
                                    scan(row, (it + 1) % 2, r, (it + 1) % 4)
                                    if last and r == 1:
                                        dve.wait_ge(scanned, row + 1)
                                        dve.wait_ge(sig_ready, row + 1)
                                        own = sig[:, (it + 1) % 2, r, 0:n - 1]
                                        dve.tensor_tensor(own, own, keep[:, (it + 1) % 2, r, 1:n], ALU.mult
                                                          ).then_inc(a_ready, 1)
                                    finished(r)
                            if not last and it in (0, 3, 7):
                                prep(u0 + 5 + (it + 1) // 4, hp * 3)
                            if not last and it in (4, 5):
                                lo_part(hp + 1, 1 - par, it - 2)
                            for c in range(2, t + 1):
                                finished(c)
                                chunk(hp, it, c)
                                if it == ITEMS - 1 and not last:
                                    values(hp + 1, 1 - par, c - 2)
                            if t >= 1:
                                finished(t + 1)
                            rows = slice(hh * SHEAD, (hh + 1) * SHEAD)
                            if last:
                                dst = mx[rows, KB - 1, t * 2 * P:(t + 1) * 2 * P]
                            else:
                                dst = o_sum[rows, it % 2, :]
                                if not (first and it < 2):
                                    dve.wait_ge(so_stored[it % 2], hp * (8 * ITEMS) + 16 * (it // 2))
                            dve.wait_ge(o_low_ready, hp * ITEMS + (it + 1))
                            dve.tensor_tensor(dst, ps[0:SHEAD, 6, 0:2 * P], o_low[rows, :], ALU.add
                                              ).then_inc(o_sum_ready, 1)
                            if not last and it in (1, 2):
                                lo_part(hp + 1, 1 - par, it - 1)

                    for piece in range(6):
                        if piece in (0, 2, 4):
                            prep(u0 + 2 + piece // 2)
                        project(0, piece, piece)
                        if piece < 4:
                            lo_part(0, 0, piece)
                        if piece == 4:
                            for r in range(2):
                                scan(r, 0, r, 0)
                    for n in range(2):
                        values(0, 0, n, 6 + n)
                    pair(0, 0, False, first=True)
                    with dve.Fori(0, KB // 2 - 1) as d:
                        pair(d * 2 + 1, 1, False)
                        pair(d * 2 + 2, 0, False)
                    pair(KB - 1, 1, True)

                u0, f0, v0 = base["E", i]
                source = mix_f if i % 2 == 0 else mx
                for n, (m, h) in enumerate(mix_order):
                    if i % 2 == 0 and n == 2 * (KB - 1):
                        convolve(KB - 1, slice(KB - 1, KB))
                    dve.wait_ge(mx_hi_ready, 2 * KB * i + n + 1)
                    dve.tensor_tensor(xg_lo[:, m, ln[h]], source[:, m, ln[h]], fp(xg_hi[:, m, ln[h]]), ALU.subtract
                                      ).then_inc(mx_lo_ready, 1)
                prep(u0 + 2)
                dve.wait_ge(mx_lo_ready, 2 * KB * (i + 1))
                for m in range(MHEADS):
                    dve.wait_ge(me_hi_ready, MHEADS * i + m + 1)
                    dve.tensor_tensor(me_lo[:, m, :], me_f[:, m, :], fp(me_hi[:, m, :]), ALU.subtract
                                      ).then_inc(me_lo_ready, 1)
                if i % 2 == 1:
                    dve.wait_ge(x_back, 16)
                prep(u0 + 3)
                prep(u0 + 4)

                def add_pair(pm, block):
                    for j in range(4):
                        if j < 3:
                            dve.wait_ge(bank_full, pm * 3 + (f0 + j + 1))
                        else:
                            dve.wait_ge(w_used, pm * 3 + (u0 + 3))
                        xs = block(j // 2)[:, ln[j % 2]]
                        dve.tensor_tensor(xs, xs, ps[:, j, :], ALU.add).then_inc(evacuated, 1)

                add_pair(0, lambda a: x[:, a, :])
                with dve.Fori(1, KB // 2 - 1) as pm:
                    for j in range(3):
                        prep(u0 + j + 2, pm * 3)
                    add_pair(pm, lambda a: x[:, bass.ds(pm * 2 + a, 1), :].rearrange("p a c -> p (a c)"))
                nu = 2 * i + 1
                for j in range(3):
                    prep(u0 + 3 * (KB // 2 - 1) + j + 2)
                for m, h in split_order(nu):
                    if m < KB - 2:
                        split(nu, m, h)
                add_pair(KB // 2 - 1, lambda a: x[:, KB - 2 + a, :])

                u0, f0, v0 = base["F", i]
                nu, a0 = 2 * i + 1, FBLK * i
                for m, h in split_order(nu):
                    if m >= KB - 2:
                        split(nu, m, h)
                prep(u0 + 2)
                prep(u0 + 3)
                for m in (KB - 2, KB - 1):
                    for h in range(2):
                        n = 2 * KB * nu + 2 * m + h
                        dve.wait_ge(sq_ready, n + 1)
                        dve.wait_ge(acc_added, max(n - 1, 2 * KB * nu + 2 * (KB - 2)))
                        dve.tensor_tensor(R[:, ln[h]], R[:, ln[h]], squares[1][:, h, :], ALU.add).then_inc(acc_added, 1)
                norm(nu)
                dve.wait_ge(r_ready, nu + 1)

                def fill(dst, blk, f, u, b0):
                    for h in range(2):
                        if h == 0:
                            dve.wait_ge(bank_full, f)
                        else:
                            dve.wait_ge(w_used, u)
                        scaled(dst[:, blk, ln[h]], (b0 + h) % 8, h)

                def product(blk, blocks, visits, hi=act_hi, lo=act_lo):
                    dve.wait_ge(evacuated, visits)
                    dve.wait_ge(silu_done, blocks + (blk + 1))
                    dve.tensor_tensor(up[:, blk, :], gate[:, blk, :], up[:, blk, :], ALU.mult
                                      ).then_inc(prod_ready, 1)
                    dve.wait_ge(act_hi_ready, blocks + (blk + 1))
                    dve.tensor_tensor(lo[:, blk, :], up[:, blk, :], fp(hi[:, blk, :]), ALU.subtract
                                      ).then_inc(act_lo_ready, 1)

                def down(f, u, v, j0, after=None):
                    dve.wait_ge(evacuated, v)
                    for n in range(2 * KB):
                        m, h = n // 2, n % 2
                        if n < 2 * KB - 1:
                            dve.wait_ge(bank_full, f + (n + 1))
                        else:
                            dve.wait_ge(w_used, u)
                        dve.tensor_tensor(x[:, m, ln[h]], x[:, m, ln[h]], ps[:, (j0 + n) % 8, :], ALU.add
                                          ).then_inc(evacuated, 1)
                        if after and h == 1 and m > 0:
                            after(m - 1)
                    if after:
                        after(KB - 1)

                fill(gate, 0, f0 + 1, u0 + 1, 0)
                fill(gate, 1, f0 + 2, u0 + 2, 2)
                prep(u0 + 4)
                fill(up, 0, f0 + 3, u0 + 3, 6)
                prep(u0 + 5)
                fill(up, 1, f0 + 4, u0 + 4, 0)
                product(0, a0, v0 + 6)
                product(1, a0, v0 + 8)
                with dve.Fori(0, FGROUPS - 2) as g:
                    n, f, v, b = u0 + 4, g * 19 + (f0 + 4), g * 24 + (v0 + 8), g * 2 + (a0 + 2)
                    more = g * 6
                    dve.wait_ge(act_lo_ready, b)
                    prep(n + 2, more)
                    fill(gate, 0, f + 1, more + (n + 1), 2)
                    prep(n + 3, more)
                    fill(gate, 1, f + 2, more + (n + 2), 4)
                    prep(n + 4, more)
                    down(f + 2, more + (n + 4), v + 4, 6)
                    prep(n + 5, more)
                    prep(n + 6, more)
                    fill(up, 0, f + 18, more + (n + 5), 22)
                    prep(n + 7, more)
                    fill(up, 1, f + 19, more + (n + 6), 24)
                    product(0, b, v + 22)
                    product(1, b, v + 24)
                n, f, v, b = (u0 + 4 + 6 * (FGROUPS - 2), f0 + 4 + 19 * (FGROUPS - 2), v0 + 8 + 24 * (FGROUPS - 2),
                              a0 + FBLK - 2)
                dve.wait_ge(act_lo_ready, b)
                prep(n + 2)
                fill(gate, 0, f + 1, n + 1, 2)
                prep(n + 3)
                fill(gate, 1, f + 2, n + 2, 4)
                prep(n + 4)
                fill(up, 0, f + 3, n + 3, 6)
                prep(n + 5)
                fill(up, 1, f + 4, n + 4, 8)
                product(0, b, v + 6, act_hi2, act_lo2)
                product(1, b, v + 8, act_hi2, act_lo2)
                prep(n + 6)
                down(f + 4, n + 6, v + 8, 2)
                prep(n + 7)
                ue, fe, ve = base["end", i]
                prep(ue)
                if i + 1 < LAYERS:
                    down(fe - 15, ue, ve - 16, 2, after=lambda m: [split(nu + 1, m, h) for h in range(2)])
                    prep(ue + 1)
                else:
                    down(fe - 15, ue, ve - 16, 2)

        @block.tensor
        def _(pe):
            def three(out, whi, wlo, mhi, mlo, start, stop):
                pe.matmul(out, whi, mhi, start=start, stop=False)
                pe.matmul(out, whi, mlo, start=False, stop=False)
                return pe.matmul(out, wlo, mhi, start=False, stop=stop)

            def unit(u, more, bank_of, waits, first=None, halves=(0, 1), ks=range(KB)):
                s = u % WSLOTS
                pe.wait_ge(w_lo_ready, more + (u + 1))
                for h in halves:
                    if waits[h] is not None:
                        pe.wait_ge(evacuated, waits[h])
                    for k in ks:
                        if first is not None:
                            pe.wait_ge(xg_lo_ready, split_count(first, k, h))
                        c = slice(k * P, (k + 1) * P)
                        last = three(ps[:, bank_of(h), :], w_hi[:, s, c], w_lo[:, s, c],
                                     xg_hi[:, k, ln[h]], xg_lo[:, k, ln[h]], k == 0, k == KB - 1)
                    if KB - 1 in ks:
                        last.then_inc(bank_full if h == 0 else w_used, 1)

            def norm(nu):
                pe.wait_ge(acc_added, 2 * KB * (nu + 1))
                for b in range(KB):
                    last = pe.matmul(ps[:, 5, b:b + 1], R[:, b * P:(b + 1) * P], mean_all[:, 0:1], start=True, stop=True)
                last.then_inc(stat_full, 1)

            def spread_factors(src, b, signal):
                for h in range(2):
                    last = pe.matmul(ps[:, b + h, :], mean_head[:], src[:, 4 * h:4 * h + 4, :].rearrange("p a c -> p (a c)"),
                                     start=True, stop=True)
                last.then_inc(signal, 1)

            def memory_keys(i, n):
                u = base["A", i][0] + n
                s = u % WSLOTS
                pe.wait_ge(w_lo_ready, u + 1)
                for k in range(KB):
                    if n == 0:
                        pe.wait_ge(mg_lo_ready, KB * i + k + 1)
                    c = slice(k * P, (k + 1) * P)
                    last = three(ps[:, n, 0:NMEM], w_hi[:, s, c], w_lo[:, s, c], mg_hi[i][:, k, :], mg_lo[i][:, k, :],
                                 k == 0, k == KB - 1)
                last.then_inc(w_used, 1)

            memory_keys(0, 0)
            pe.wait_ge(consts_made, 4)
            pe.wait_ge(msq_ready, 1)
            for k in range(KB):
                pe.matmul(ps[:, 4, 0:NMEM], mean_all[:], msq[:, k, :], start=(k == 0), stop=(k == KB - 1))
            for mb in range(2):
                for k in range(KB):
                    last = pe.matmul(ps[:, 5, mb:mb + 1], msq[:, k, mb * P:(mb + 1) * P], mean_all[:, 0:1],
                                     start=(k == 0), stop=(k == KB - 1))
            last.then_inc(mstat_full, 1)
            for i in range(LAYERS):
                u0, f0, v0 = base["A", i]
                if i > 0:
                    pe.wait_ge(evacuated, v0)
                for n in range(MHEADS):
                    if i > 0 or n > 0:
                        memory_keys(i, n)
                if i > 0:
                    pe.wait_ge(kdiag_ready, i)
                    spread_factors(kdiag, 6, kspread)
                    pe.wait_ge(kn_ready, i)
                if i == 0:
                    pe.wait_ge(mroot_ready, 2)
                for g in range(2):
                    for n in range(2):
                        u = u0 + MHEADS + 2 * g + n
                        s = u % WSLOTS
                        pe.wait_ge(w_lo_ready, u + 1)
                        for mb in range(2):
                            tok = slice(mb * P, (mb + 1) * P)
                            for k in range(4):
                                c = slice(k * 2 * P, (k + 1) * 2 * P)
                                last = three(ps[:, 6 - 2 * g + mb, 0:2 * P], mg_hi[i][:, 4 * n + k, tok],
                                             mg_lo[i][:, 4 * n + k, tok], w_hi[:, s, c], w_lo[:, s, c],
                                             n == 0 and k == 0, n == 1 and k == 3)
                        last.then_inc(w_used, 1)
                pe.wait_ge(ksq_ready, i + 1)
                pe.wait_ge(evacuated, v0 + MHEADS + 1)
                for b in range(KB):
                    last = pe.matmul(ps[:, 6, b:b + 1], ksq[:, b * P:(b + 1) * P], mean_head[:, 0:1],
                                     start=True, stop=True)
                last.then_inc(kstat_full, 1)

            for i in range(LAYERS):
                u0, f0, v0 = base["B", i]

                def qstat(h):
                    hd = MHEADS * i + h
                    pe.wait_ge(qsq_ready, 2 * hd + 2)
                    if hd > 0:
                        pe.wait_ge(rqv_ready, hd)
                    for b in range(KB):
                        last = pe.matmul(ps[:, 3, b:b + 1], qsq[:, h % 2, b * P:(b + 1) * P], mean_head[:, 0:1],
                                         start=True, stop=True)
                    last.then_inc(qstat_full, 1)

                def scores(n):
                    h, b, g = n // 4, n % 2, BATCHES * i + n
                    pe.wait_ge(evacuated, v0 + 2 * h + 2)
                    if n == 0:
                        pe.wait_ge(kv_loaded, 64 * (i + 1))
                        pe.wait_ge(r_ready, 2 * i + 1)
                    if n >= 2:
                        pe.wait_ge(exp_done, 2 * (g - 1))
                    ks = slice(h * NMEM, (h + 1) * NMEM)
                    for j in range(2):
                        tok = slice((2 * (n % 4) + j) * P, (2 * (n % 4) + j + 1) * P)
                        last = three(ps[:, 4 + b, j * NMEM:(j + 1) * NMEM], q_hi[:, h % 2, tok], q_lo[:, h % 2, tok],
                                     k_hi[:, ks], k_lo[:, ks], True, True)
                    last.then_inc(scores_full, 1)

                def turn_probs(n):
                    b, g = n % 2, BATCHES * i + n
                    pe.wait_ge(prob_ready, g + 1)
                    if n < 2:
                        pe.wait_ge(evacuated, v0 + 4)
                    else:
                        pe.wait_ge(pT_lo_ready, g - 1)
                    for mb in range(2):
                        for j in range(2):
                            last = pe.transpose(ps[:, 6 + b, (2 * mb + j) * P:(2 * mb + j + 1) * P],
                                                prob[:, b, j, mb * P:(mb + 1) * P], ident[:])
                    last.then_inc(pT_full, 1)

                def attended(n):
                    h, b, g = n // 4, n % 2, BATCHES * i + n
                    pe.wait_ge(pT_lo_ready, g + 1)
                    if g > 0:
                        pe.wait_ge(mo_ready, g)
                    hs = slice(h * P, (h + 1) * P)
                    for mb in range(2):
                        last = three(ps[:, 2, 0:2 * P], v_hi[:, mb, hs], v_lo[:, mb, hs],
                                     pT_hi[:, b, mb, :], pT_lo[:, b, mb, :], mb == 0, mb == 1)
                    last.then_inc(mo_full, 1)

                def quarter_unit(h, q):
                    u, half = u0 + h, q // 2
                    s = u % WSLOTS
                    if q == 0:
                        pe.wait_ge(w_lo_ready, u + 1)
                    if q % 2 == 0:
                        pe.wait_ge(evacuated, v0 + (1 if h == 2 else 5) + half)
                    for k in range(4 * (q % 2), 4 * (q % 2) + 4):
                        c = slice(k * P, (k + 1) * P)
                        last = three(ps[:, half, :], w_hi[:, s, c], w_lo[:, s, c],
                                     xg_hi[:, k, ln[half]], xg_lo[:, k, ln[half]], k == 0, k == KB - 1)
                    if q % 2 == 1:
                        last.then_inc(bank_full if half == 0 else w_used, 1)

                pe.wait_ge(evacuated, v0 - MHEADS if i == 0 else v0)
                unit(u0, 0, lambda h: h, (None, None), first=2 * i, halves=(0,))
                if i == 0:
                    pe.wait_ge(evacuated, v0)
                    pe.wait_ge(kdiag_ready, LAYERS)
                    spread_factors(kdiag, 6, kspread)
                unit(u0, 0, lambda h: h, (None, None), first=2 * i, halves=(1,))
                if i == 0:
                    pe.wait_ge(kn_ready, LAYERS)
                unit(u0 + 1, 0, lambda h: 6 + h, (None, None))
                norm(2 * i)
                qstat(0)
                quarter_unit(2, 0)
                pe.wait_ge(diag_ready, 2 * i + 1)
                spread_factors(diag, 4, spread)
                qstat(1)
                scores(0)
                scores(1)
                quarter_unit(2, 1)
                for n in range(BATCHES):
                    if n in (5, 9):
                        qstat(1 + n // 4)
                    if n + 2 < BATCHES:
                        scores(n + 2)
                    turn_probs(n)
                    if n > 0:
                        attended(n - 1)
                    if n < 6:
                        quarter_unit(2 + (n + 2) // 4, (n + 2) % 4)
                    elif n < 14:
                        h, q = (n - 6) // 4, (n - 6) % 4
                        if q == 0:
                            pe.wait_ge(w_lo_ready, base["C", i][0] + 1)
                            pe.wait_ge(evacuated, v0 + 7 + h)
                        s = base["C", i][0] % WSLOTS
                        for k in (2 * q, 2 * q + 1):
                            c = slice(k * P, (k + 1) * P)
                            last = three(ps[:, h, :], w_hi[:, s, c], w_lo[:, s, c],
                                         xg_hi[:, k, ln[h]], xg_lo[:, k, ln[h]], k == 0, k == KB - 1)
                        if q == 3:
                            last.then_inc(bank_full if h == 0 else w_used, 1)
                attended(BATCHES - 1)

                u0, f0, v0 = base["C", i]
                pe.wait_ge(evacuated, v0)
                pe.wait_ge(mo_ready, BATCHES * (i + 1))
                if i % 2 == 0:
                    for j in (1, 2):
                        unit(u0 + j, 0, lambda h: 2 * j + h, (None, None))
                    with pe.Fori(1, KB) as b:
                        for j in range(3):
                            v = b * 6 + (v0 + 2 * j - 5)
                            unit(u0 + j, b * 3, lambda h: 2 * j + h, (v, v + 1))
                else:
                    def z(row, par, hh, r, t, first):
                        if not first:
                            pe.wait_ge(sig_ready, row - 1)
                        slot, hd, _ = head_place(hh, par)
                        q = slice((2 * t + r) * P, (2 * t + r + 1) * P)
                        n = 2 * P * (t + 1)
                        for c in range(0, n, HALF):
                            w = min(HALF, n - c)
                            o = ps[:, 2 * r + c // HALF, :]
                            final = c + w == n
                            pe.matmul(o[:, 0:w], sq[:, slot, q], sk[:, slot, c:c + w], start=True, stop=False)
                            pe.matmul(o[:, 0:w], sq[hd, slot, q], sk_lo[hd, par, c:c + w], start=False, stop=not final)
                        m = (2 - r) * P
                        pe.matmul(o[:, w - m:w], ident_r[:], mask_r[:, 0:m], start=False, stop=True
                                  ).then_inc(z_full, 1)

                    def project(hp, piece, ks=range(KB), first=False):
                        part, h = piece // 2, piece % 2
                        s = (u0 + part) % WSLOTS
                        if 0 in ks:
                            if h == 0:
                                pe.wait_ge(w_lo_ready, hp * 3 + (u0 + part + 1))
                            if not first:
                                pe.wait_ge(evacuated, hp * 6 + (v0 + piece))
                                if piece == 0:
                                    pe.wait_ge(vT_lo_ready, hp * 2)
                        for k in ks:
                            c = slice(k * P, (k + 1) * P)
                            last = three(ps[:, piece if first else 7, :], w_hi[:, s, c], w_lo[:, s, c],
                                         xg_hi[:, k, ln[h]], xg_lo[:, k, ln[h]], k == 0, k == KB - 1)
                            if k == KB - 1:
                                last.then_inc(bank_full if h == 0 else w_used, 1)

                    def turn_values(hp, n, b0=7):
                        pe.wait_ge(evacuated, hp * 6 + (v0 + 6))
                        if n == 1 and b0 == 7:
                            pe.wait_ge(vT_lo_ready, hp * 2 + 1)
                        for b in range(4):
                            tok = slice((4 * n + b) * P, (4 * n + b + 1) * P)
                            last = pe.transpose(ps[:, b0, b * P:(b + 1) * P], tf[:, tok], ident[:])
                        last.then_inc(vT_full, 1)

                    def turn(hp, it, c, par, first):
                        n = CHUNKS_BEFORE[it] + c
                        if c == 0:
                            pe.wait_ge(a_ready, hp * ROWS + (2 * it + 2))
                        if not (first and n < 2):
                            pe.wait_ge(aT_lo_ready, hp * CHUNKS + (n - 1))
                        for kk in range(2):
                            for r in range(2):
                                k = 2 * c + kk
                                last = pe.transpose(ps[:, 4 + n % 2, (2 * kk + r) * P:(2 * kk + r + 1) * P],
                                                    sig[:, it % 2, r, k * P:(k + 1) * P], ident[:])
                        last.then_inc(aT_full, 1)

                    def weighted(hp, it, c, par, first):
                        n, t = CHUNKS_BEFORE[it] + c, it % 4
                        pe.wait_ge(aT_lo_ready, hp * CHUNKS + (n + 1))
                        if c == 0 and not (first and it == 0):
                            pe.wait_ge(o_sum_ready, hp * ITEMS + it)
                        for kk in range(2):
                            v = sv[:, par, 2 * c + kk, it // 4, :]
                            o = ps[:, 6, 0:2 * P]
                            pe.matmul(o, v, aT_hi[:, n % 2, kk, :], start=(c == 0 and kk == 0), stop=False)
                            last = pe.matmul(o, v, aT_lo[:, n % 2, kk, :], start=False, stop=(c == t and kk == 1))
                        last.then_inc(pv_done, 1)

                    def pair(hp, par, last, first=False):
                        steps = [0]

                        def fill(n):
                            while n > 0 and not last:
                                piece, k = divmod(steps[0], KB)
                                k1 = min(k + n, KB)
                                project(hp + 1, piece, range(k, k1))
                                steps[0] += k1 - k
                                n -= k1 - k

                        for it in range(ITEMS):
                            t = it % 4
                            for c in range(min(t + 1, 2)):
                                turn(hp, it, c, par, first)
                            if it == ITEMS - 1 and not last:
                                pe.wait_ge(sqk_lo_ready, hp * 8 + 16)
                                pe.wait_ge(sqk_hi_ready, hp * 12 + 24)
                            for r in range(2):
                                if it < ITEMS - 1:
                                    z(hp * ROWS + (2 * (it + 1) + r), par, (it + 1) // 4, r, (it + 1) % 4,
                                      False)
                                elif not last:
                                    z(hp * ROWS + (ROWS + r), 1 - par, 0, r, 0, False)
                                fill(FILL[it][r])
                            if it == 0:
                                pe.wait_ge(vT_lo_ready, hp * 2 + 2)
                            for c in range(t + 1):
                                if c > 0:
                                    fill(FILL[it][c + 1])
                                    if it == ITEMS - 1 and not last and c % 2 == 1:
                                        turn_values(hp + 1, c // 2)
                                weighted(hp, it, c, par, first)
                                if c + 2 <= t:
                                    turn(hp, it, c + 2, par, first)

                    for piece in range(2, 6):
                        if piece == 5:
                            pe.wait_ge(sqk_lo_ready, 8)
                            pe.wait_ge(sqk_hi_ready, 12)
                            for r in range(2):
                                z(r, 0, 0, r, 0, True)
                        project(0, piece, first=True)
                    for n in range(2):
                        turn_values(0, n, 6 + n)
                    pair(0, 0, False, first=True)
                    with pe.Fori(0, KB // 2 - 1) as d:
                        pair(d * 2 + 1, 1, False)
                        pair(d * 2 + 2, 0, False)
                    pair(KB - 1, 1, True)

                u0, f0, v0 = base["E", i]
                pe.wait_ge(evacuated, v0)

                def out_pair(pm, first):
                    for ks in (range(KB - 1), range(KB - 1, KB)) if first else (range(KB),):
                        for a in range(2):
                            s = (u0 + a) % WSLOTS
                            if 0 in ks:
                                pe.wait_ge(w_lo_ready, pm * 3 + (u0 + a + 1))
                            for h in range(2):
                                if not first:
                                    pe.wait_ge(evacuated, pm * 4 + (v0 + 2 * a + h - 3))
                                for k in ks:
                                    if first and a == 0:
                                        pe.wait_ge(mx_lo_ready, 2 * KB * i + mix_order.index((k, h)) + 1)
                                    c = slice(k * P, (k + 1) * P)
                                    last = three(ps[:, 2 * a + h, :], w_hi[:, s, c], w_lo[:, s, c],
                                                 xg_hi[:, k, ln[h]], xg_lo[:, k, ln[h]], k == 0, False)
                            if KB - 1 in ks:
                                last.then_inc(w_used, 1)
                    s = (u0 + 2) % WSLOTS
                    pe.wait_ge(w_lo_ready, pm * 3 + (u0 + 3))
                    if first:
                        pe.wait_ge(me_lo_ready, MHEADS * (i + 1))
                    for a in range(2):
                        for h in range(2):
                            for k in range(MHEADS):
                                c = slice((2 * k + a) * P, (2 * k + a + 1) * P)
                                last = three(ps[:, 2 * a + h, :], w_hi[:, s, c], w_lo[:, s, c],
                                             me_hi[:, k, ln[h]], me_lo[:, k, ln[h]], False, k == MHEADS - 1)
                            last.then_inc(w_used if a == 1 and h == 1 else bank_full, 1)

                out_pair(0, True)
                with pe.Fori(1, KB // 2) as pm:
                    out_pair(pm, False)

                u0, f0, v0 = base["F", i]

                def down(n, more, blocks, v, j0, hi=act_hi, lo=act_lo, ahead=0):
                    pe.wait_ge(act_lo_ready, blocks)
                    for j in range(2 if ahead == 0 else 1):
                        pe.wait_ge(w_lo_ready, more + (n + j + 1))
                    order = [(q, 0) for q in range(ahead)] + [(q, 1) for q in range(ahead)] + \
                            [(q, j) for q in range(ahead, 2 * KB) for j in range(2)]
                    for q, j in order:
                        m, h = q // 2, q % 2
                        if j == 0:
                            pe.wait_ge(evacuated, v + (q - 5))
                        elif ahead and q == 0:
                            pe.wait_ge(w_lo_ready, n + 2)
                        s, c = (n + j) % WSLOTS, slice(m * P, (m + 1) * P)
                        last = three(ps[:, (j0 + q) % 8, :], w_hi[:, s, c], w_lo[:, s, c],
                                     hi[:, j, ln[h]], lo[:, j, ln[h]], j == 0, j == 1)
                        if j == 1 and q < 2 * KB - 1:
                            last.then_inc(bank_full, 1)
                        elif j == 1:
                            last.then_inc(w_used, 2)

                unit(u0, 0, lambda h: h, (v0 - 3, v0 - 2), first=2 * i + 1)
                unit(u0 + 1, 0, lambda h: 2 + h, (v0 - 1, v0))
                unit(u0 + 2, 0, lambda h: 6 + h, (None, None), halves=(0,))
                norm(2 * i + 1)
                unit(u0 + 2, 0, lambda h: 6 + h, (None, None), halves=(1,), ks=range(KB // 2))
                pe.wait_ge(diag_ready, 2 * i + 2)
                spread_factors(diag, 4, spread)
                unit(u0 + 2, 0, lambda h: 6 + h, (None, None), halves=(1,), ks=range(KB // 2, KB))
                unit(u0 + 3, 0, lambda h: h, (v0 + 1, v0 + 2))
                with pe.Fori(0, FGROUPS - 2) as g:
                    n, more, v = u0 + 4, g * 6, g * 24 + (v0 + 8)
                    unit(n, more, lambda h: 2 + h, (v - 5, v - 4))
                    unit(n + 1, more, lambda h: 4 + h, (v - 3, v - 2))
                    down(n + 2, more, g * 2 + (FBLK * i + 2), v + 4, 6)
                    unit(n + 4, more, lambda h: (22 + h) % 8, (v + 15, v + 16))
                    unit(n + 5, more, lambda h: (24 + h) % 8, (v + 17, v + 18))
                n, v = u0 + 4 + 6 * (FGROUPS - 2), v0 + 8 + 24 * (FGROUPS - 2)
                for j in range(4):
                    unit(n + j, 0, lambda h: (2 + 2 * j + h) % 8, (v + 2 * j - 5, v + 2 * j - 4))
                down(n + 4, 0, FBLK * (i + 1) - 2, v + 8, 2)
                down(n + 6, 0, FBLK * (i + 1), v + 24, 2, act_hi2, act_lo2, ahead=4)


def kernel(x, mem, w_in, w_out, w_mem_kv, w_conv, w_ffn_in, w_ffn_out, g_mix, g_mem, g_ffn, g_q, g_k):
    import concourse.bacc as bacc
    from concourse.bass_utils import run_bass_kernel_spmd

    def blocks(v):
        v = np.asarray(v)
        return np.ascontiguousarray(np.moveaxis(v.reshape(*v.shape[:-1], KB, P), -1, 0))

    weights = [np.asarray(w) for w in (w_in, w_out, w_mem_kv, w_ffn_in, w_ffn_out)]
    arrays = {
        "xT": np.ascontiguousarray(np.asarray(x)[0].reshape(SEQ, KB, P).transpose(2, 1, 0)),
        "memT": np.ascontiguousarray(np.asarray(mem)[0].reshape(NMEM, KB, P).transpose(2, 1, 0)),
        "wpack": pack_weights(*weights),
        "gain": blocks(np.stack([np.asarray(g) for g in (g_mix, g_mem, g_ffn)])),
        "taps": blocks(np.asarray(w_conv)[0]),
        "g_heads": np.ascontiguousarray(np.stack([np.asarray(g_q), np.asarray(g_k)]).transpose(2, 0, 1)),
    }
    nc = bacc.Bacc("TRN2", target_bir_lowering=False, num_devices=1)
    ap = {n: nc.dram_tensor(n, a.shape, F32, kind="ExternalInput").ap() for n, a in arrays.items()}
    out = nc.dram_tensor("out", (P, KB, SEQ), F32, kind="ExternalOutput").ap()
    trunk(nc, ap["xT"], ap["memT"], ap["wpack"], [(n, ap[n]) for n in ("gain", "taps", "g_heads")], out)
    r = run_bass_kernel_spmd(nc, [arrays], core_ids=[0])
    got = np.asarray(r.results[0]["out"])
    return np.ascontiguousarray(got.transpose(2, 1, 0).reshape(1, SEQ, DM))
```
